# Optimizing a Trainium2 kernel written in Bass

```python
import jax
import jax.numpy as jnp
from jax import lax
import numpy as np

D_MODEL = 2048
BATCH = 1
SEQ = 128
DEPTH = 1
DEC_BATCH = 1
DEC_SEQ = 128
PAST_LEN = 128

GRID_W = 64
GLA_W = D_MODEL // 2
CONV_W = D_MODEL - GLA_W
GLA_HEADS = 4
DV_HEAD = GLA_W // GLA_HEADS
DK_HEAD = DV_HEAD // 2
GLA_DK = GLA_HEADS * DK_HEAD
GATE_RANK = 16
GATE_TAU = 16.0
CHUNK = 64
CONV_K = 31
N_EXPERTS = 16
N_GROUPS = 4
EXPERTS_PER_GROUP = N_EXPERTS // N_GROUPS
TOP_K = 2
MOE_FF = D_MODEL // 2
EXPERT_BLOCK = 128
DEEPNORM_ALPHA = (2 * DEPTH) ** 0.25
DEEPNORM_BETA = (8 * DEPTH) ** -0.25
EPS = 1e-5
V_START = 2 * GLA_DK
V_END = V_START + GLA_W
SPLIT_POINTS = (GLA_DK, 2 * GLA_DK, V_END, V_END + GLA_W, V_END + GLA_W + GATE_RANK, V_END + GLA_W + 2 * GATE_RANK)
IN_COLS = SPLIT_POINTS[-1] + 2 * CONV_W

kernel_name = 'hybrid_gla_conformer_moe_diffusion_step'

def _layernorm(x, g, b):
    xf = x.astype(jnp.float32)
    mu = jnp.mean(xf, axis=-1, keepdims=True)
    xc = xf - mu
    var = jnp.mean(xc * xc, axis=-1, keepdims=True)
    return (xc * lax.rsqrt(var + EPS) * g + b).astype(x.dtype)

def _pos_embed_2d(rows):
    n_freq = D_MODEL // 4
    omega = 1.0 / (10000.0 ** (jnp.arange(n_freq, dtype=jnp.float32) / n_freq))
    t = jnp.arange(rows * GRID_W)
    pr = (t // GRID_W).astype(jnp.float32)[:, None] * omega
    pc = (t % GRID_W).astype(jnp.float32)[:, None] * omega
    return jnp.concatenate([jnp.sin(pr), jnp.cos(pr), jnp.sin(pc), jnp.cos(pc)], axis=-1)

def _gla_chunk_scan(q, k, v, g, s0):
    bsz, nh, t, _ = q.shape
    n = t // CHUNK
    blk = lambda a: a.reshape(bsz, nh, n, CHUNK, a.shape[-1])
    q, k, v, g = blk(q), blk(k), blk(v), blk(g)
    b = jnp.cumsum(g, axis=3)
    b_last = b[:, :, :, -1:, :]
    q_t = q * jnp.exp(b)
    k_t = k * jnp.exp(-b)
    causal = jnp.tril(jnp.ones((CHUNK, CHUNK), dtype=bool))
    attn = jnp.where(causal, jnp.einsum('bhnid,bhnjd->bhnij', q_t, k_t), 0.0)
    o_intra = jnp.einsum('bhnij,bhnje->bhnie', attn, v)
    kv = jnp.einsum('bhnjd,bhnje->bhnde', k * jnp.exp(b_last - b), v)
    decay = jnp.exp(b_last[:, :, :, 0, :])

    def step(s, inp):
        d, u = inp
        return d[..., None] * s + u, s

    s_fin, s_start = lax.scan(step, s0, (jnp.moveaxis(decay, 2, 0), jnp.moveaxis(kv, 2, 0)))
    o_inter = jnp.einsum('bhnid,nbhde->bhnie', q_t, s_start)
    return (o_intra + o_inter).reshape(bsz, nh, t, -1), s_fin

def _gla_bidir(q, k, v, g_f, g_b, s0_f, s0_b):
    o_f, s_f = _gla_chunk_scan(q, k, v, g_f, s0_f)
    flip = lambda a: jnp.flip(a, axis=2)
    o_b, s_b = _gla_chunk_scan(flip(q), flip(k), flip(v), flip(g_b), s0_b)
    return o_f + flip(o_b), s_f, s_b

def _mixer(h, s0_f, s0_b, w_in, w_gate_up, b_gate, gla_norm_g, w_dw, b_dw, conv_ln_g, conv_ln_b, w_out):
    bsz, t, _ = h.shape
    proj = h @ w_in
    q, k, v, r, zf, zb, pw = jnp.split(proj, SPLIT_POINTS, axis=-1)
    heads = lambda a: a.reshape(bsz, t, GLA_HEADS, -1).transpose(0, 2, 1, 3).astype(jnp.float32)
    q = heads(q) * (DK_HEAD ** -0.5)
    k = heads(k)
    v = heads(v)
    g_f = heads(jax.nn.log_sigmoid((zf @ w_gate_up[0] + b_gate[0]).astype(jnp.float32)) / GATE_TAU)
    g_b = heads(jax.nn.log_sigmoid((zb @ w_gate_up[1] + b_gate[1]).astype(jnp.float32)) / GATE_TAU)
    o, s_f, s_b = _gla_bidir(q, k, v, g_f, g_b, s0_f.astype(jnp.float32), s0_b.astype(jnp.float32))
    o = o * lax.rsqrt(jnp.mean(o * o, axis=-1, keepdims=True) + EPS)
    o = o.transpose(0, 2, 1, 3).reshape(bsz, t, GLA_W) * gla_norm_g
    y_gla = (o * jax.nn.silu(r.astype(jnp.float32))).astype(h.dtype)
    u = pw[..., :CONV_W] * jax.nn.sigmoid(pw[..., CONV_W:])
    u = lax.conv_general_dilated(u, w_dw[:, None, :], window_strides=(1,),
                                 padding=((CONV_K // 2, CONV_K // 2),),
                                 dimension_numbers=('NWC', 'WIO', 'NWC'),
                                 feature_group_count=CONV_W) + b_dw
    y_conv = jax.nn.silu(_layernorm(u, conv_ln_g, conv_ln_b))
    out = jnp.concatenate([y_gla, y_conv], axis=-1) @ w_out
    return out, s_f, s_b

def _routed_experts(hf, expert_idx, gate, w_g, w_u, w_d):
    n_tok, d = hf.shape
    m = n_tok * TOP_K
    flat_e = expert_idx.reshape(-1)
    order = jnp.argsort(flat_e)
    sorted_e = flat_e[order]
    tok = (order // TOP_K).astype(jnp.int32)
    w_sorted = gate.reshape(-1)[order]
    counts = jnp.bincount(flat_e, length=N_EXPERTS)
    padded = (counts + EXPERT_BLOCK - 1) // EXPERT_BLOCK * EXPERT_BLOCK
    pad_end = jnp.cumsum(padded)
    pad_start = pad_end - padded
    start = jnp.cumsum(counts) - counts
    dest = pad_start[sorted_e] + jnp.arange(m) - start[sorted_e]
    n_blk = (m + N_EXPERTS * (EXPERT_BLOCK - 1) + EXPERT_BLOCK - 1) // EXPERT_BLOCK
    p = n_blk * EXPERT_BLOCK
    buf_tok = jnp.zeros((p,), jnp.int32).at[dest].set(tok)
    buf_w = jnp.zeros((p,), hf.dtype).at[dest].set(w_sorted.astype(hf.dtype))
    blk_e = jnp.minimum(jnp.searchsorted(pad_end, jnp.arange(n_blk) * EXPERT_BLOCK, side='right'), N_EXPERTS - 1)

    def run_block(args):
        e, idx, wt = args
        xb = hf[idx]
        hb = jax.nn.silu(xb @ w_g[e]) * (xb @ w_u[e])
        return ((hb @ w_d[e]) * wt[:, None]).astype(hf.dtype)

    out = lax.map(run_block, (blk_e, buf_tok.reshape(n_blk, EXPERT_BLOCK), buf_w.reshape(n_blk, EXPERT_BLOCK)))
    return jnp.zeros_like(hf).at[buf_tok].add(out.reshape(p, d))

def _moe(h, w_router, b_router, w_g, w_u, w_d):
    bsz, t, d = h.shape
    hf = h.reshape(-1, d)
    n_tok = hf.shape[0]
    logits = (hf @ w_router).astype(jnp.float32) + b_router
    probs = jax.nn.softmax(logits, axis=-1)
    pg = probs.reshape(n_tok, N_GROUPS, EXPERTS_PER_GROUP)
    group_score = lax.top_k(pg, TOP_K)[0].sum(axis=-1)
    g_sel = jnp.argmax(group_score, axis=-1)
    in_group = pg[jnp.arange(n_tok), g_sel]
    top_p, top_local = lax.top_k(in_group, TOP_K)
    expert_idx = (g_sel[:, None] * EXPERTS_PER_GROUP + top_local).astype(jnp.int32)
    gate = top_p / jnp.sum(top_p, axis=-1, keepdims=True)
    return _routed_experts(hf, expert_idx, gate, w_g, w_u, w_d).reshape(bsz, t, d)

def _layer(x, cond, s0_f, s0_b, w_mod, b_mod, mixer_w, ln1_g, ln1_b, ln2_g, ln2_b, moe_w):
    mod = (cond @ w_mod + b_mod)[:, None, :]
    sh1, sc1, g1, sh2, sc2, g2 = jnp.split(mod, 6, axis=-1)
    m, s_f, s_b = _mixer(x * (1 + sc1) + sh1, s0_f, s0_b, *mixer_w)
    x = _layernorm(DEEPNORM_ALPHA * x + g1 * m, ln1_g, ln1_b)
    f = _moe(x * (1 + sc2) + sh2, *moe_w)
    x = _layernorm(DEEPNORM_ALPHA * x + g2 * f, ln2_g, ln2_b)
    return x, s_f, s_b

def setup_inputs(seed: int = 0) -> dict:
    key = jax.random.key(seed)
    ks = jax.random.split(key, 32)
    nrm = lambda kk, shape, s: jax.random.normal(kk, shape, jnp.float32) * s
    x_prompt = nrm(ks[0], (BATCH, SEQ, D_MODEL), 1.0)
    x_sample = nrm(ks[1], (DEC_BATCH, DEC_SEQ, D_MODEL), 1.0)
    state_gla = nrm(ks[2], (DEC_BATCH, DEPTH, 2, GLA_HEADS, DK_HEAD, DV_HEAD), 0.5)
    c = nrm(ks[3], (DEC_BATCH, D_MODEL), 1.0)
    c_ctx = nrm(ks[4], (D_MODEL,), 1.0)
    w_mod = nrm(ks[5], (DEPTH, D_MODEL, 6 * D_MODEL), 0.5 * D_MODEL ** -0.5)
    b_mod = nrm(ks[6], (DEPTH, 6 * D_MODEL), 0.02)
    w_in = nrm(ks[7], (DEPTH, D_MODEL, IN_COLS), D_MODEL ** -0.5)
    w_in = w_in.at[:, :, V_START:V_END].multiply(DEEPNORM_BETA)
    w_gate_up = nrm(ks[8], (DEPTH, 2, GATE_RANK, GLA_DK), GATE_RANK ** -0.5)
    b_gate = nrm(ks[9], (DEPTH, 2, GLA_DK), 0.5)
    gla_norm_g = 1.0 + nrm(ks[10], (DEPTH, GLA_W), 0.05)
    w_dw = nrm(ks[11], (DEPTH, CONV_K, CONV_W), CONV_K ** -0.5)
    b_dw = nrm(ks[12], (DEPTH, CONV_W), 0.02)
    conv_ln_g = 1.0 + nrm(ks[13], (DEPTH, CONV_W), 0.05)
    conv_ln_b = nrm(ks[14], (DEPTH, CONV_W), 0.02)
    w_out = nrm(ks[15], (DEPTH, GLA_W + CONV_W, D_MODEL), DEEPNORM_BETA * (GLA_W + CONV_W) ** -0.5)
    ln1_g = 1.0 + nrm(ks[16], (DEPTH, D_MODEL), 0.05)
    ln1_b = nrm(ks[17], (DEPTH, D_MODEL), 0.02)
    ln2_g = 1.0 + nrm(ks[18], (DEPTH, D_MODEL), 0.05)
    ln2_b = nrm(ks[19], (DEPTH, D_MODEL), 0.02)
    w_router = nrm(ks[20], (D_MODEL, N_EXPERTS), D_MODEL ** -0.5)
    b_router = nrm(ks[21], (N_EXPERTS,), 0.01)
    w_e_gate = nrm(ks[22], (DEPTH, N_EXPERTS, D_MODEL, MOE_FF), D_MODEL ** -0.5)
    w_e_up = nrm(ks[23], (DEPTH, N_EXPERTS, D_MODEL, MOE_FF), D_MODEL ** -0.5)
    w_e_down = nrm(ks[24], (DEPTH, N_EXPERTS, MOE_FF, D_MODEL), DEEPNORM_BETA * MOE_FF ** -0.5)
    return {'x_prompt': x_prompt, 'x_sample': x_sample, 'state_gla': state_gla, 'c': c, 'c_ctx': c_ctx,
            'w_mod': w_mod, 'b_mod': b_mod, 'w_in': w_in, 'w_gate_up': w_gate_up, 'b_gate': b_gate,
            'gla_norm_g': gla_norm_g, 'w_dw': w_dw, 'b_dw': b_dw, 'conv_ln_g': conv_ln_g, 'conv_ln_b': conv_ln_b,
            'w_out': w_out, 'ln1_g': ln1_g, 'ln1_b': ln1_b, 'ln2_g': ln2_g, 'ln2_b': ln2_b,
            'w_router': w_router, 'b_router': b_router, 'w_e_gate': w_e_gate, 'w_e_up': w_e_up, 'w_e_down': w_e_down}

def reference(x_prompt, x_sample, state_gla, c, c_ctx, w_mod, b_mod, w_in, w_gate_up, b_gate, gla_norm_g,
              w_dw, b_dw, conv_ln_g, conv_ln_b, w_out, ln1_g, ln1_b, ln2_g, ln2_b,
              w_router, b_router, w_e_gate, w_e_up, w_e_down):
    def layer_weights(l):
        mixer_w = (w_in[l], w_gate_up[l], b_gate[l], gla_norm_g[l], w_dw[l], b_dw[l], conv_ln_g[l], conv_ln_b[l], w_out[l])
        moe_w = (w_router, b_router, w_e_gate[l], w_e_up[l], w_e_down[l])
        return mixer_w, moe_w

    cond_ctx = jax.nn.silu(c_ctx)[None, :]
    zero_state = jnp.zeros((x_prompt.shape[0], GLA_HEADS, DK_HEAD, DV_HEAD), jnp.float32)
    xp = x_prompt
    states = []
    for l in range(DEPTH):
        mixer_w, moe_w = layer_weights(l)
        xp, s_f, s_b = _layer(xp, cond_ctx, zero_state, zero_state, w_mod[l], b_mod[l], mixer_w,
                              ln1_g[l], ln1_b[l], ln2_g[l], ln2_b[l], moe_w)
        states.append(jnp.stack([s_f, s_b], axis=1))
    new_state_gla = jnp.stack(states, axis=1).astype(x_prompt.dtype)

    rows = x_sample.shape[1] // GRID_W
    cond_lat = jax.nn.silu(c)
    xs = x_sample + _pos_embed_2d(rows).astype(x_sample.dtype)
    for l in range(DEPTH):
        mixer_w, moe_w = layer_weights(l)
        xs, _, _ = _layer(xs, cond_lat, state_gla[:, l, 0], state_gla[:, l, 1], w_mod[l], b_mod[l], mixer_w,
                          ln1_g[l], ln1_b[l], ln2_g[l], ln2_b[l], moe_w)
    return (xp, xs, new_state_gla)


_drawn_inputs = setup_inputs


def setup_inputs(seed=0):
    import zlib

    import numpy as np

    out = dict(_drawn_inputs(seed))
    spreads = {}
    factors = {'state_gla': 5.958,
     'gla_norm_g': 14.95,
     'b_dw': 5.073,
     'conv_ln_g': 19.645,
     'conv_ln_b': 28.518,
     'ln2_b': 2.918,
     'b_router': 20.668}
    for name, (base, spread) in spreads.items():
        noise = np.random.default_rng([zlib.crc32(name.encode()), seed]).standard_normal(out[name].shape)
        drawn = base * np.exp(spread * noise) if base else spread * noise
        out[name] = jnp.asarray(drawn.astype(out[name].dtype))
    for name, factor in factors.items():
        out[name] = (out[name] * factor).astype(out[name].dtype)
    return out
```

```python
from contextlib import ExitStack

import concourse.bass as bass
from concourse import mybir

ALU = mybir.AluOpType
ACT = mybir.ActivationFunctionType
F32 = mybir.dt.float32
I32 = mybir.dt.int32
U32 = mybir.dt.uint32
AX = mybir.AxisListType

P = 128
G = 2
D = 2048
KT = D // P
BANK = 512
NQ = D // BANK
HEADS, DK, DV = 4, 128, 256
HALF = 64
GLA_W = CONV_W = 1024
CC = CONV_W // P
TAPS, PAD = 31, 15
RANK = 16
NE, NGRP, PER = 16, 4, 4
FF = 1024
FT = FF // P
EPS = 1e-5
ALPHA = 2.0 ** 0.25
TAU = 16.0
QSCALE = DK ** -0.5

SLOTS = 8
UNIT = 2048
SEG_UNITS = KT
PASS_UNITS = 8
PASSES_IN = 5
PASS_COL = (4128, 3104, 0, 1024, 2048)
Z_COL = 3072
STEP_UNITS = 24
PRE_UNITS = 6 * SEG_UNITS + (PASSES_IN + 2) * PASS_UNITS
MAX_EXTRA = G * P * 2 // (HALF + 1)
NSTEP = NE + MAX_EXTRA

C_ID, C_INCF, C_RESTF, C_INCB, C_RESTB, C_BEFORE, C_ONES, C_IOTA, C_SEL = [P * i for i in range(9)]
C_KEY = C_SEL + 2 * P
C_J = C_KEY + 32
C_JV = C_J + 16 * MAX_EXTRA
C_EXP = C_JV + MAX_EXTRA
C_END = C_EXP + NSTEP + 1


def hybrid_step(nc, x_prompt, x_sample, state_gla, c, c_ctx, w_mod, b_mod, w_in, w_gate_up, b_gate,
                gla_norm_g, w_dw, b_dw, conv_ln_g, conv_ln_b, w_out, ln1_g, ln1_b, ln2_g, ln2_b,
                w_router, b_router, w_e_gate, w_e_up, w_e_down, table, pos,
                y_prompt, y_sample, new_state):
    with ExitStack() as ctx:
        def sb(name, shape, dt=F32):
            return ctx.enter_context(nc.sbuf_tensor(name, shape, dt))

        def sem(name):
            return ctx.enter_context(nc.semaphore(name))

        ps = [ctx.enter_context(nc.psum_tensor(f"bank{i}", [P, BANK], F32)) for i in range(8)]

        ring = sb("ring", [P, SLOTS, UNIT])
        xres = sb("xres", [P, G, D])
        hT = sb("hT", [P, KT, G * P])
        arena = sb("arena", [P, 5 * 2048])
        work = sb("work", [P, 10720])
        const = sb("const", [P, C_END])
        modrow = sb("modrow", [P, 4, BANK])
        lnrow = sb("lnrow", [P, 2, BANK])
        rows = sb("rows", [56, P])
        condT = sb("condT", [P, KT, 32])
        gcol = sb("gcol", [P, 3, CC])
        tapT = sb("tapT", [P, CC, 32])
        wr = sb("wr", [P, KT, NE])
        br = sb("br", [P, NE])
        modcol = sb("modcol", [P, 2, NQ, NQ, 2])
        decay = sb("decay", [P, 2, 2, HEADS])
        small = sb("small", [P, 64])
        stats = sb("stats", [P, G, NQ, 6])
        rt = sb("rt", [P, 14, 32])
        extra = sb("extra", [P, 8, NE * MAX_EXTRA])
        etab = sb("etab", [P, NSTEP + 1], I32)
        vtab = sb("vtab", [P, MAX_EXTRA], I32)
        b64 = sb("b64", [P, NSTEP + 1])

        def part(t, at, *dims):
            n = 1
            for d in dims:
                n *= d
            v = t[:, at:at + n]
            if len(dims) == 2:
                return v.rearrange("p (a b) -> p a b", a=dims[0])
            if len(dims) == 3:
                return v.rearrange("p (a b c) -> p a b c", a=dims[0], b=dims[1])
            return v

        qk = part(arena, 0, G, 1024)
        vv = part(arena, 2048, G, 1024)
        rs = part(arena, 4096, G, 1024)
        uu = part(arena, 6144, G, 1024)
        convacc = part(arena, 6144, CC, G, P)
        gg = part(arena, 8192, G, 2, BANK)
        wz = part(arena, 0, KT, 32)
        wgu = part(arena, 512, 2, BANK)
        bg = part(arena, 2048, 2, BANK)
        zT = part(arena, 3072, 256)
        taprow = part(arena, 4096, 1024)
        posb = part(arena, 6144, D)
        h2 = part(arena, 0, G, D)
        acc = part(arena, 4096, G, D)
        g1b = part(arena, 4096, G, D)
        XT = part(arena, 8192, KT, HALF)
        kTt = part(work, 0, 2, HEADS, P)
        kdec = part(work, 1024, 2, BANK)
        attnT = part(work, 2048, 2, HEADS, P)
        qTt = part(work, 3072, 2, HEADS, P)
        smid = part(work, 4096, 2, HEADS, DV)
        sig = part(work, 4096, G, 1024)
        s0 = part(work, 6144, 2, HEADS, DV)
        UW = P + 2 * PAD
        uT = part(work, 8192, CC, G, UW)
        G2b = part(work, 0, G, D)
        B2b = part(work, 4096, G, D)
        ye = part(work, 0, 1024)
        hs = part(work, 1024, BANK)
        hh = part(work, 1536, BANK)
        hTm = part(work, 2048, 4, P)
        sel = part(work, 2560, G, P)
        wsel = part(work, 2816, G, P)
        wselT = part(work, 3072, G, P)
        lng = part(work, 4096, D)
        lnb = part(work, 6144, D)
        junk = part(work, 8192, BANK)

        ident = const[:, C_ID:C_ID + P]
        incl = [const[:, C_INCF:C_INCF + P], const[:, C_INCB:C_INCB + P]]
        rest = [const[:, C_RESTF:C_RESTF + P], const[:, C_RESTB:C_RESTB + P]]
        before = const[:, C_BEFORE:C_BEFORE + P]
        ones = const[:, C_ONES:C_ONES + P]
        iota = const[:, C_IOTA:C_IOTA + P]
        pick = [const[:, C_SEL + i * P:C_SEL + (i + 1) * P] for i in range(2)]
        key4 = const[:, C_KEY:C_KEY + 32]

        slot = [sem(f"slot{i}") for i in range(SLOTS)]
        used = sem("weights_used")
        s_zero = sem("zeroed")
        s_const, s_rows, s_tap, s_wz, s_wgu, s_s0, s_wr, s_bmod, s_bmod2, s_ln, s_lnb, s_ln2 = [
            sem(n) for n in ("const_in", "rows_in", "taps_in", "wz_in", "wgu_in", "s0_in", "router_in",
                             "bmod_in", "bmod2_in", "ln1_in", "ln1_bcast_in", "ln2_bcast_in")]
        s_x = [sem("x_prompt_in"), sem("x_sample_in")]
        silu_c = sem("cond_silu")
        rows_ps, tap_ps, cond_rdy, tap_rdy, xpos = [sem(n) for n in (
            "rows_ps", "tap_ps", "cond_ready", "tap_ready", "pos_added")]
        xT_ps, xT_ev, mod_ev, modT_ps, col_rdy, h_dve, h_act = [sem(n) for n in (
            "xT_ps", "xT_evacuated", "mod_evacuated", "modT_ps", "modcol_ready", "h1_prompt", "h1_sample")]
        z_ps, z_ev, gate_ps, gate_l, gate_rdy = [sem(n) for n in (
            "z_ps", "z_evacuated", "gate_ps", "gate_log", "gate_ready")]
        ev = [sem(f"pass{i}_evacuated") for i in range(PASSES_IN)]
        uT_ps, uT_ev, conv_c, back_ps, back_var, back_ev = [sem(n) for n in (
            "uT_ps", "uT_evacuated", "conv_chain", "conv_back_ps", "conv_var", "conv_normed")]
        a_ps, a_exp, a_rdy, at_ps, at_ev, kv_ps, kv_ev, kv2_ps, o_ps, o_sq, o_rdy = [sem(n) for n in (
            "decays_ps", "decays_exp", "qk_decayed", "attn_ps", "attn_masked", "kv_ps", "state_mid", "kv2_ps",
            "o_ps", "o_rms", "o_ready")]
        fin_rdy, state_out = sem("final_state_ready"), sem("state_out")
        yT_ps, yT_ev, cT_ps, cT_ev = [sem(n) for n in ("yT_ps", "yT_evacuated", "cT_ps", "cT_evacuated")]
        bc_ps, bc_ev, row2 = [sem(n) for n in ("bcast_ps", "bcast_evacuated", "ln1_mod_rows")]
        m_ev, ln_v, ln_s, h2_rdy, h2T_ps, h2T_v, h2T_s, lg_ps = [sem(n) for n in (
            "m_evacuated", "ln1_var", "ln1_sd", "h2_ready", "h2T_ps", "h2T_dve", "h2T_act", "logits_ps")]
        lmax, lexp, sel_rdy, rk_ps, ov_rdy, cx_ps, tab_rdy = [sem(n) for n in (
            "logit_max", "logit_exp", "selected", "rank_ps", "overflow_ready", "prefix_ps", "tables_ready")]
        dch, ach = sem("dve_chain"), sem("act_chain")
        st_sel, st_gath, st_xv, st_xa, st_wT, st_hs, st_h, st_hTp, st_hTv, st_yv, st_ya, st_cmb, st_add = [
            sem(n) for n in ("step_sel", "step_gather_ps", "step_x_dve", "step_x_act", "step_wT", "step_silu",
                             "step_h", "step_hT_ps", "step_hT", "step_y_dve", "step_y_act",
                             "step_combine_ps", "step_added")]
        dn_ps, gu_ps = sem("step_down_ps"), sem("step_gate_up_ps")
        x1_rdy, t_bc, t_mul, t_var, t_sd, t_nrm, t_gain, t_out, out_s = [sem(n) for n in (
            "x1_ready", "tail_g2_ps", "tail_g2_used", "tail_var", "tail_sd", "tail_normed", "tail_gained",
            "tail_ready", "out_done")]
        st_onehot = sem("step_onehot")
        pch = sem("pool_chain")

        wmod2, win2, wout2 = w_mod[0], w_in[0], w_out[0]

        def seg_slice(q):
            return slice(32 * q, 32 * q + 32)

        block = ctx.enter_context(nc.Block())

        @block.sync
        def _(sp):
            n = 0

            def unit(dst, src):
                nonlocal n
                if n >= SLOTS:
                    sp.wait_ge(used, n - SLOTS + 1)
                sp.dma_start(dst, src).then_inc(slot[n % SLOTS], 16)
                n += 1

            def segment(s):
                for kt in range(KT):
                    unit(ring[:, n % SLOTS, :], wmod2[kt * P:(kt + 1) * P, s * D:(s + 1) * D])

            def wide_pass(w, col):
                for u in range(PASS_UNITS):
                    unit(ring[:, n % SLOTS, :].rearrange("p (i n) -> p i n", i=2),
                         w[u * 256:(u + 1) * 256, col:col + 1024].rearrange("(i p) n -> p i n", i=2))

            segment(0)
            segment(1)
            for col in PASS_COL:
                wide_pass(win2, col)
            for s in range(2, 6):
                segment(s)
            wide_pass(wout2, 0)
            wide_pass(wout2, 1024)

            def expert(t, e):
                for i in range(STEP_UNITS):
                    sl = i % SLOTS
                    r = i // 2
                    if i < 16:
                        w = w_e_gate if i % 2 == 0 else w_e_up
                        src = w[0, e, r * 256:(r + 1) * 256, :].rearrange("(i p) n -> p i n", i=2)
                        dst = ring[:, sl, :].rearrange("p (i n) -> p i n", i=2)
                    else:
                        src = w_e_down[0, e, (i - 16) * P:(i - 15) * P, :]
                        dst = ring[:, sl, :]
                    sp.wait_ge(used, t * STEP_UNITS + (PRE_UNITS + i - SLOTS + 1))
                    sp.dma_start(dst, src).then_inc(slot[sl], 16)

            with sp.Fori(0, NE) as e:
                expert(e, e)
            sp.wait_ge(tab_rdy, 1)
            with sp.Fori(0, MAX_EXTRA) as j:
                go = sp.value_load(vtab[0:1, bass.ds(j, 1)], min_val=0, max_val=1)
                eo = sp.value_load(etab[0:1, bass.ds(j + NE, 1)], min_val=0, max_val=NE - 1)
                with sp.If(go > 0):
                    expert(j + NE, eo)

        @block.gpsimd
        def _(pool):
            for t in (modrow[:, :, :], lnrow[:, :, :], wgu, condT[:, :, :], attnT, uT, b64[:, :]):
                nc.gpsimd.memset(t, 0.0).then_inc(s_zero, 1)
            pool.wait_ge(h2_rdy, 2)
            pool.wait_ge(s_lnb, 32)
            for g in range(G):
                nc.gpsimd.tensor_tensor(xres[:, g, :], xres[:, g, :], lng, ALU.mult).then_inc(pch, 1)
            for g in range(G):
                pool.wait_ge(pch, g + 1)
                nc.gpsimd.tensor_tensor(xres[:, g, :], xres[:, g, :], lnb, ALU.add).then_inc(x1_rdy, 1)
            pool.wait_ge(s_ln2, 32)
            for g in range(G):
                pool.wait_ge(t_nrm, g + 1)
                nc.gpsimd.tensor_tensor(acc[:, g, :], acc[:, g, :], lng, ALU.mult).then_inc(t_gain, 1)

        @block.scalar
        def _(act):
            n = 0

            def link(ins):
                nonlocal n
                n += 1
                ins.then_inc(ach, 1)
                act.wait_ge(ach, n)

            act.dma_start(const[:, :], table).then_inc(s_const, 16)
            r128 = lambda a: a.rearrange("(k p) -> k p", p=P)
            act.dma_start(rows[0:16, :], r128(c_ctx)).then_inc(s_rows, 16)
            act.dma_start(rows[16:32, :], r128(c[0])).then_inc(s_rows, 16)
            act.dma_start(rows[32:40, :], r128(gla_norm_g[0])).then_inc(s_rows, 16)
            act.dma_start(rows[40:48, :], r128(conv_ln_g[0])).then_inc(s_rows, 16)
            act.dma_start(rows[48:56, :], r128(conv_ln_b[0])).then_inc(s_rows, 16)
            act.dma_start(taprow[0:TAPS, :], w_dw[0]).then_inc(s_tap, 16)
            act.dma_start(taprow[TAPS:TAPS + 1, :], b_dw).then_inc(s_tap, 16)
            act.dma_start(xres[:, 0, :], x_prompt[0]).then_inc(s_x[0], 16)
            act.dma_start(xres[:, 1, :], x_sample[0]).then_inc(s_x[1], 16)
            act.dma_start(posb, pos).then_inc(s_x[1], 16)
            act.wait_ge(s_zero, 7)
            mod_rows = b_mod[0].rearrange("(s q j) -> q s j", q=NQ, j=BANK)
            for g in range(G):
                act.dma_start(modrow[g:97 + g:32, :, :], mod_rows[:, 0:4, :]).then_inc(s_bmod, 16)
            for i, w in enumerate((ln1_g, ln1_b)):
                for g in range(G):
                    act.dma_start(lnrow[g:97 + g:32, i, :], w[0].rearrange("(q j) -> q j", q=NQ)).then_inc(s_ln, 16)
            act.dma_start(wz, win2[:, Z_COL:Z_COL + 32].rearrange("(k p) n -> p k n", p=P)).then_inc(s_wz, 16)
            for d in range(2):
                act.dma_start(wgu[RANK * d:RANK * d + RANK, d, :], w_gate_up[0, d]).then_inc(s_wgu, 16)
            act.dma_start(bg[0:1, :, :], b_gate).then_inc(s_wgu, 16)
            act.dma_start(s0, state_gla[0, 0].rearrange("d h k v -> k d h v")).then_inc(s_s0, 16)
            act.dma_start(wr[:, :, :], w_router.rearrange("(k p) e -> p k e", p=P)).then_inc(s_wr, 16)
            act.dma_start(br[:, :], b_router.partition_broadcast(P)).then_inc(s_wr, 16)

            act.wait_ge(s_rows, 80)
            nc.scalar.activation(rows[0:32, :], rows[0:32, :], ACT.Silu).then_inc(silu_c, 1)

            act.wait_ge(modT_ps, 2)
            for g in range(G):
                act.dma_start(modrow[g:97 + g:32, 0:2, :], mod_rows[:, 4:6, :]).then_inc(s_bmod2, 16)

            act.wait_ge(col_rdy, 2)
            for kt in range(KT):
                q, j = divmod(kt, NQ)
                nc.scalar.activation(hT[:, kt, P:2 * P], hT[:, kt, P:2 * P], ACT.Identity,
                                     bias=modcol[:, 0, q, j, 1:2], scale=modcol[:, 1, q, j, 1:2]).then_inc(h_act, 1)
            act.wait_ge(z_ps, 1)
            nc.scalar.copy(zT[0:32, :], ps[0][0:32, 0:256]).then_inc(z_ev, 1)

            for i in range(4):
                dst = gg[:, i // 2, i % 2, :]
                act.wait_ge(gate_ps, i + 1)
                link(nc.scalar.activation(dst, ps[4 + i][:, :], ACT.Abs))
                link(nc.scalar.activation(dst, dst, ACT.Exp, scale=-1.0))
                nc.scalar.activation(dst, dst, ACT.Ln, bias=ones[:, 0:1]).then_inc(gate_l, 1)

            def passed(p):
                act.wait_ge(used, 2 * SEG_UNITS + (p + 1) * PASS_UNITS)

            def evac(p, dst, func):
                passed(p)
                for g in range(G):
                    for hf in range(2):
                        nc.scalar.activation(dst[:, g, hf * BANK:(hf + 1) * BANK],
                                             ps[(p % 2) * 4 + 2 * g + hf][:, :], func).then_inc(ev[p], 1)

            evac(0, sig, ACT.Sigmoid)
            evac(2, qk, ACT.Copy)
            evac(3, vv, ACT.Copy)
            evac(4, rs, ACT.Silu)

            for gi, g in enumerate((1, 0)):
                if gi:
                    act.wait_ge(o_ps, 2)
                for d in range(2):
                    act.wait_ge(a_ps, 6 * gi + 1 + d)
                    nc.scalar.activation(qTt[:, d], ps[2 + d][:, :].rearrange("p (h t) -> p h t", h=HEADS),
                                         ACT.Exp).then_inc(a_exp, 1)
                    nc.scalar.activation(kTt[:, d], ps[2 + d][:, :].rearrange("p (h t) -> p h t", h=HEADS),
                                         ACT.Exp, scale=-1.0).then_inc(a_exp, 1)
                    act.wait_ge(a_ps, 6 * gi + 3 + d)
                    nc.scalar.activation(kdec[:, d, :], ps[4 + d][:, :], ACT.Exp).then_inc(a_exp, 1)
                if g == 0:
                    for i in range(4):
                        act.wait_ge(kv_ps, 4 + i + 1)
                        nc.scalar.copy(smid[:, i // 2, 2 * (i % 2):2 * (i % 2) + 2, :],
                                       ps[4 + i][:, :].rearrange("p (h v) -> p h v", h=2)).then_inc(kv_ev, 1)
                for h in range(HEADS):
                    act.wait_ge(o_ps, 2 * gi + h // 2 + 1)
                    link(nc.scalar.activation(junk[:, 0:DV], ps[2 + h // 2][:, (h % 2) * DV:(h % 2 + 1) * DV],
                                              ACT.Square, accum_out=small[:, 4 * g + h:4 * g + h + 1]))
                nc.scalar.activation(small[:, 16 + 4 * g:20 + 4 * g], small[:, 4 * g:4 * g + 4], ACT.Sqrt,
                                     bias=small[:, 63:64], scale=1.0 / DV).then_inc(o_sq, 1)

            act.wait_ge(fin_rdy, 8)
            act.dma_start(new_state[0, 0].rearrange("d h k v -> k d h v"), s0).then_inc(state_out, 16)
            act.wait_ge(back_var, 1)
            nc.scalar.activation(small[:, 32:34], small[:, 28:30], ACT.Sqrt, bias=small[:, 63:64]).then_inc(o_sq, 1)
            for i in range(G * CC):
                g, cc = divmod(i, CC)
                act.wait_ge(cT_ps, i // 4 + 1)
                nc.scalar.activation(hT[:, CC + cc, g * P:(g + 1) * P], ps[(6, 7, 0, 1)[i // 4]][:, (i % 4) * P:(i % 4 + 1) * P],
                                     ACT.Silu, bias=gcol[:, 2, cc:cc + 1], scale=gcol[:, 1, cc:cc + 1]).then_inc(cT_ev, 1)
            for i in range(24):
                dst = (g1b, G2b, B2b)[i // 8]
                g, q = divmod(i % 8, NQ)
                act.wait_ge(bc_ps, i + 1)
                if i == 8:
                    act.wait_ge(cT_ps, 4)
                    act.wait_ge(state_out, 16)
                nc.scalar.copy(dst[:, g, q * BANK:(q + 1) * BANK], ps[4 + i % 4][:, :]).then_inc(bc_ev, 1)
            for g in range(G):
                act.wait_ge(ln_v, g + 1)
                nc.scalar.activation(small[:, 40 + g:41 + g], small[:, 37 + 2 * g:38 + 2 * g], ACT.Sqrt,
                                     bias=small[:, 63:64]).then_inc(ln_s, 1)
                for b in range(2):
                    act.wait_ge(h2T_ps, 4 * g + 2 * b + 2)
                    nc.scalar.copy(hT[:, 4 * (2 * b + 1):4 * (2 * b + 2), g * P:(g + 1) * P],
                                   ps[2 * b + 1][:, :].rearrange("p (k t) -> p k t", k=4)).then_inc(h2T_s, 1)
            act.wait_ge(h2_rdy, 2)
            act.dma_start(lng, ln1_g[0].partition_broadcast(P)).then_inc(s_lnb, 16)
            act.dma_start(lnb, ln1_b[0].partition_broadcast(P)).then_inc(s_lnb, 16)
            act.wait_ge(lmax, 1)
            for g in range(G):
                nc.scalar.activation(rt[:, 1, g * NE:(g + 1) * NE], rt[:, 0, g * NE:(g + 1) * NE], ACT.Exp,
                                     bias=small[:, 44 + g:45 + g], accum_out=small[:, 48 + g:49 + g]).then_inc(lexp, 1)

            def expert(t):
                act.wait_ge(st_gath, t * 3 + 2)
                nc.scalar.copy(XT[:, 8:16, :], ps[3][:, :].rearrange("p (k s) -> p k s", k=8)).then_inc(st_xa, 1)
                act.wait_ge(st_gath, t * 3 + 3)
                nc.scalar.copy(wselT, ps[4][:, 0:G * P].rearrange("p (g t) -> p g t", g=G)).then_inc(st_wT, 1)
                act.wait_ge(used, t * STEP_UNITS + (PRE_UNITS + 16))
                nc.scalar.activation(hs, ps[0][:, :], ACT.Silu).then_inc(st_hs, 1)
                act.wait_ge(used, t * STEP_UNITS + (PRE_UNITS + 24))
                nc.scalar.copy(ye[:, BANK:2 * BANK], ps[6][:, :]).then_inc(st_ya, 1)

            with act.Fori(0, NE) as t:
                expert(t)
            act.wait_ge(tab_rdy, 1)
            with act.Fori(0, MAX_EXTRA) as j:
                go = act.value_load(vtab[0:1, bass.ds(j, 1)], min_val=0, max_val=1)
                with act.If(go > 0):
                    expert(j + NE)

            act.wait_ge(x1_rdy, 2)
            act.dma_start(lng, ln2_g[0].partition_broadcast(P)).then_inc(s_ln2, 16)
            act.dma_start(lnb, ln2_b[0].partition_broadcast(P)).then_inc(s_ln2, 16)
            for g in range(G):
                act.wait_ge(t_var, g + 1)
                nc.scalar.activation(small[:, 40 + g:41 + g], small[:, 37 + 2 * g:38 + 2 * g], ACT.Sqrt,
                                     bias=small[:, 63:64]).then_inc(t_sd, 1)
            for g, y in enumerate((y_prompt, y_sample)):
                act.wait_ge(t_out, g + 1)
                act.dma_start(y[0], acc[:, g, :]).then_inc(out_s, 16)
            act.wait_ge(out_s, 32)

        @block.tensor
        def _(pe):
            n = 0
            mm = nc.tensor.matmul
            tr = nc.tensor.transpose

            def arrive():
                pe.wait_ge(slot[n % SLOTS], 16 * (n // SLOTS + 1))

            pe.wait_ge(s_const, 16)
            pe.wait_ge(s_rows, 80)
            pe.wait_ge(silu_c, 1)
            tr(ps[6][:, 0:56], rows[:, :], ident[0:56, 0:56]).then_inc(rows_ps, 1)
            pe.wait_ge(s_tap, 32)
            for cc in range(CC):
                last = tr(ps[7][:, cc * 32:cc * 32 + 32], taprow[0:32, cc * P:(cc + 1) * P], ident[0:32, 0:32])
            last.then_inc(tap_ps, 1)

            def seg_units(bank, kts):
                nonlocal n
                for kt in kts:
                    arrive()
                    for q in range(NQ):
                        last = mm(ps[bank][seg_slice(q), :], condT[:, kt, :],
                                  ring[:, n % SLOTS, q * BANK:(q + 1) * BANK], start=(kt == 0), stop=(kt == KT - 1))
                    last.then_inc(used, 1)
                    n += 1

            pe.wait_ge(cond_rdy, 1)
            seg_units(0, range(KT))
            pe.wait_ge(s_x[0], 16)
            for b in range(8):
                g = b // 4
                if b == 4:
                    pe.wait_ge(xpos, 1)
                if b >= 4:
                    pe.wait_ge(xT_ev, b - 3)
                for i in range(4):
                    kt = 4 * (b % 4) + i
                    last = tr(ps[1 + b % 4][:, i * P:(i + 1) * P], xres[:, g, kt * P:(kt + 1) * P], ident)
                last.then_inc(xT_ps, 1)
            seg_units(5, range(KT))
            pe.wait_ge(tap_rdy, 2)
            for s in range(2):
                pe.wait_ge(mod_ev, s + 1)
                for j in range(4):
                    last = tr(ps[6 + s][:, j * P:(j + 1) * P], modrow[:, s, j * P:(j + 1) * P], ident)
                last.then_inc(modT_ps, 1)
            pe.wait_ge(s_wz, 16)
            for kt in range(KT):
                pe.wait_ge(h_dve, kt + 1)
                pe.wait_ge(h_act, kt + 1)
                last = mm(ps[0][0:32, 0:256], wz[:, kt, :], hT[:, kt, :], start=(kt == 0), stop=(kt == KT - 1))
            last.then_inc(z_ps, 1)
            pe.wait_ge(z_ev, 1)
            pe.wait_ge(s_wgu, 48)
            for i in range(4):
                g, d = divmod(i, 2)
                mm(ps[4 + i][:, :], zT[0:32, g * P:(g + 1) * P], wgu[0:32, d, :], start=True, stop=False)
                mm(ps[4 + i][:, :], ones[0:1, :], bg[0:1, d, :], start=False, stop=True).then_inc(gate_ps, 1)

            def wide_pass(st):
                nonlocal n
                for u in range(PASS_UNITS):
                    arrive()
                    for i in range(2):
                        kt = 2 * u + i
                        for g in range(G):
                            for hf in range(2):
                                last = mm(ps[st * 4 + 2 * g + hf][:, :], hT[:, kt, g * P:(g + 1) * P],
                                          ring[:, n % SLOTS, i * 1024 + hf * BANK:i * 1024 + (hf + 1) * BANK],
                                          start=(kt == 0), stop=(kt == KT - 1))
                    last.then_inc(used, 1)
                    n += 1

            wide_pass(0)
            pe.wait_ge(gate_rdy, 4)
            wide_pass(1)
            pe.wait_ge(ev[0], 4)
            wide_pass(0)
            pe.wait_ge(ev[1], 4)
            for i in range(G * CC):
                g, cc = divmod(i, CC)
                last = tr(ps[4 + i // 4][:, (i % 4) * P:(i % 4 + 1) * P], uu[:, g, cc * P:(cc + 1) * P], ident)
                if i % 4 == 3:
                    last.then_inc(uT_ps, 1)
            pe.wait_ge(uT_ev, 4)
            wide_pass(1)
            pe.wait_ge(ev[2], 4)
            wide_pass(0)

            def half_segment(k):
                s = 2 + k // 2
                if k == 0:
                    pe.wait_ge(ev[4], 4)
                if k in (4, 6):
                    pe.wait_ge(mod_ev, s - 1)
                seg_units(s % 2, range(8 * (k % 2), 8 * (k % 2) + 8))

            def decays(gi, g):
                if gi == 0:
                    pe.wait_ge(gate_rdy, 4)
                    pe.wait_ge(ev[3], 4)
                else:
                    pe.wait_ge(o_rdy, 4)
                    pe.wait_ge(kv_ev, 8)
                for d in range(2):
                    for h in range(HEADS):
                        last = mm(ps[2 + d][:, h * P:(h + 1) * P], gg[:, g, d, h * P:(h + 1) * P], incl[d],
                                  start=True, stop=True)
                    last.then_inc(a_ps, 1)
                for d in range(2):
                    mm(ps[4 + d][:, :], rest[d], gg[:, g, d, :], start=True, stop=True).then_inc(a_ps, 1)
                for i in range(2):
                    for h in range(HEADS):
                        last = tr(ps[6 + i][:, h * P:(h + 1) * P], qk[:, g, i * 512 + h * P:i * 512 + (h + 1) * P], ident)
                    last.then_inc(a_ps, 1)

            def kv(g, chunk, signal):
                for d in range(2):
                    r = slice(HALF * chunk[d], HALF * chunk[d] + HALF)
                    for h in range(HEADS):
                        last = mm(ps[4 + 2 * d + h // 2][:, (h % 2) * DV:(h % 2 + 1) * DV],
                                  kdec[r, d, h * P:(h + 1) * P], vv[r, g, h * DV:(h + 1) * DV], start=True, stop=True)
                        if h % 2:
                            last.then_inc(signal, 1)

            def scores(gi, g):
                pe.wait_ge(a_rdy, 8 * (gi + 1))
                for d in range(2):
                    for h in range(HEADS):
                        last = mm(ps[2 + d][:, h * P:(h + 1) * P], kTt[:, d, h, :], qTt[:, d, h, :],
                                  start=True, stop=True)
                    last.then_inc(at_ps, 1)
                kv(g, (0, 1), kv_ps)

            def outputs(gi, g):
                pe.wait_ge(at_ev, 2 * (gi + 1))
                pe.wait_ge(kv_ev, 8 if gi == 0 else 12)
                if g == 1:
                    pe.wait_ge(s_s0, 16)
                for h in range(HEADS):
                    o = ps[2 + h // 2][:, (h % 2) * DV:(h % 2 + 1) * DV]
                    v = vv[:, g, h * DV:(h + 1) * DV]
                    mm(o, attnT[:, 0, h, :], v, start=True, stop=False)
                    parts = [(0, 1, smid), (1, 0, smid)]
                    if g == 1:
                        parts += [(0, 0, s0), (1, 1, s0)]
                    mm(o, attnT[:, 1, h, :], v, start=False, stop=False)
                    for i, (d, ch, st) in enumerate(parts):
                        r = slice(HALF * ch, HALF * ch + HALF)
                        last = mm(o[r, :], qTt[:, d, h, r], st[:, d, h, :], start=False,
                                  stop=(i >= len(parts) - 2))
                    if h % 2:
                        last.then_inc(o_ps, 1)

            half_segment(0)
            decays(0, 1)
            half_segment(1)
            scores(0, 1)
            half_segment(2)
            outputs(0, 1)
            half_segment(3)
            decays(1, 0)
            half_segment(4)
            scores(1, 0)
            half_segment(5)
            pe.wait_ge(kv_ev, 12)
            kv(0, (1, 0), kv2_ps)
            outputs(1, 0)
            half_segment(6)
            pe.wait_ge(fin_rdy, 8)
            pe.wait_ge(conv_c, TAPS * CC)
            for i in range(G * CC):
                g, cc = divmod(i, CC)
                last = tr(ps[4 + i // 4][:, (i % 4) * P:(i % 4 + 1) * P], convacc[:, cc, g, :], ident)
                if i % 4 == 3:
                    last.then_inc(back_ps, 1)
            half_segment(7)
            pe.wait_ge(o_rdy, 8)
            pe.wait_ge(back_ev, 2)
            for i in range(G * 8):
                g, kt = divmod(i, 8)
                last = tr(ps[2 + i // 4][:, (i % 4) * P:(i % 4 + 1) * P], vv[:, g, kt * P:(kt + 1) * P], ident)
                if i % 4 == 3:
                    last.then_inc(yT_ps, 1)
            pe.wait_ge(mod_ev, 6)
            for i in range(G * CC):
                g, cc = divmod(i, CC)
                last = tr(ps[(6, 7, 0, 1)[i // 4]][:, (i % 4) * P:(i % 4 + 1) * P], uu[:, g, cc * P:(cc + 1) * P], ident)
                if i % 4 == 3:
                    last.then_inc(cT_ps, 1)

            def broadcast(i, row, g, q):
                pe.wait_ge(bc_ev, i - 3) if i >= 4 else None
                mm(ps[4 + i % 4][:, :], pick[g][seg_slice(q), :], row[seg_slice(q), :],
                   start=True, stop=True).then_inc(bc_ps, 1)

            pe.wait_ge(yT_ev, 4)
            pe.wait_ge(cT_ev, G * CC)
            for i in range(8):
                broadcast(i, modrow[:, 2, :], i // 4, i % 4)
            wide_pass(0)
            pe.wait_ge(row2, 1)
            for i in range(16):
                row = (modrow[:, 0, :], modrow[:, 3, :])[i // 8]
                broadcast(8 + i, row, i % 8 // 4, i % 4)
            pe.wait_ge(bc_ev, 24)
            wide_pass(1)

            pe.wait_ge(m_ev, 4)
            for g in range(G):
                pe.wait_ge(h2_rdy, g + 1)
                for b in range(4):
                    if g:
                        pe.wait_ge((h2T_v, h2T_s)[b % 2], b // 2 + 1)
                    for i in range(4):
                        kt = 4 * b + i
                        last = tr(ps[b][:, i * P:(i + 1) * P], h2[:, g, kt * P:(kt + 1) * P], ident)
                    last.then_inc(h2T_ps, 1)
            pe.wait_ge(s_wr, 32)
            for g in range(G):
                pe.wait_ge(h2T_v, 2 * (g + 1))
                pe.wait_ge(h2T_s, 2 * (g + 1))
                for kt in range(KT):
                    last = mm(ps[4][:, g * NE:(g + 1) * NE], hT[:, kt, g * P:(g + 1) * P], wr[:, kt, :],
                              start=(kt == 0), stop=(kt == KT - 1))
                last.then_inc(lg_ps, 1)
            pe.wait_ge(sel_rdy, 1)
            s_g = [rt[:, 8, 0:NE], rt[:, 8, NE:2 * NE]]
            mm(ps[5][:, 0:NE], before, s_g[0], start=True, stop=True)
            mm(ps[5][:, NE:2 * NE], before, s_g[1], start=True, stop=False)
            mm(ps[5][:, NE:2 * NE], ones, s_g[0], start=False, stop=True)
            mm(ps[5][:, 32:48], ones, s_g[0], start=True, stop=False)
            mm(ps[5][:, 32:48], ones, s_g[1], start=False, stop=True)
            mm(ps[5][0:NE, 48:49], s_g[0], ones[:, 0:1], start=True, stop=False)
            mm(ps[5][0:NE, 48:49], s_g[1], ones[:, 0:1], start=False, stop=True).then_inc(rk_ps, 1)
            pe.wait_ge(ov_rdy, 1)
            mm(ps[6][:, 0:NE], rt[0:NE, 9:13, :], before[0:NE, 0:NE], start=True, stop=True).then_inc(cx_ps, 1)

            def expert(t):
                def unit_in(i):
                    pe.wait_ge(slot[i % SLOTS], t * 48 + 16 * (PRE_UNITS // SLOTS + i // SLOTS + 1))

                pe.wait_ge(st_onehot, t * 2 + 2)
                pe.wait_ge(st_add, t * 8 + 8)
                for kt in range(KT):
                    for g in range(G):
                        last = mm(ps[2 + kt // 8][:, (kt % 8) * HALF:(kt % 8 + 1) * HALF],
                                  h2[:, g, kt * P:(kt + 1) * P], sel[:, g, 0:HALF], start=(g == 0), stop=(g == 1))
                    if kt % 8 == 7:
                        last.then_inc(st_gath, 1)
                pe.wait_ge(st_sel, t + 1)
                for g in range(G):
                    last = tr(ps[4][:, g * P:(g + 1) * P], wsel[:, g, :], ident)
                last.then_inc(st_gath, 1)
                pe.wait_ge(st_xv, t + 1)
                pe.wait_ge(st_xa, t + 1)
                for i in range(16):
                    unit_in(i)
                    for k in range(2):
                        kt = 2 * (i // 2) + k
                        for hf in range(2):
                            last = mm(ps[i % 2][HALF * hf:HALF * hf + HALF, :], XT[:, kt, :],
                                      ring[:, i % SLOTS, k * 1024 + hf * BANK:k * 1024 + (hf + 1) * BANK],
                                      start=(kt == 0), stop=(kt == KT - 1))
                    last.then_inc(used, 1)
                pe.wait_ge(st_h, t + 1)
                for j in range(4):
                    last = tr(ps[7][:, j * P:(j + 1) * P], hh[:, j * P:(j + 1) * P], ident)
                last.then_inc(st_hTp, 1)
                pe.wait_ge(st_hTv, t + 1)
                for i in range(FT):
                    unit_in(16 + i)
                    lhsT = hTm[:, i % 4, HALF * (i // 4):HALF * (i // 4) + HALF]
                    for b in range(2):
                        for hf in range(2):
                            last = mm(ps[5 + b][HALF * hf:HALF * hf + HALF, :], lhsT,
                                      ring[:, i, hf * 1024 + b * BANK:hf * 1024 + (b + 1) * BANK],
                                      start=(i == 0), stop=(i == FT - 1))
                    last.then_inc(used, 1)
                pe.wait_ge(st_wT, t + 1)
                for j in range(8):
                    g, b, hf = j // 4, j // 2 % 2, j % 2
                    if j == 0:
                        pe.wait_ge(st_yv, t + 1)
                    if j == 2:
                        pe.wait_ge(st_ya, t + 1)
                    if j >= 4:
                        pe.wait_ge(st_add, t * 8 + (8 + j - 3))
                    r = slice(HALF * hf, HALF * hf + HALF)
                    mm(ps[(2, 3, 0, 1)[j % 4]][:, :], wselT[r, g, :], ye[r, b * BANK:(b + 1) * BANK],
                       start=True, stop=True).then_inc(st_cmb, 1)

            with pe.Fori(0, NE) as t:
                expert(t)
            pe.wait_ge(tab_rdy, 1)
            with pe.Fori(0, MAX_EXTRA) as j:
                go = pe.value_load(vtab[0:1, bass.ds(j, 1)], min_val=0, max_val=1)
                with pe.If(go > 0):
                    expert(j + NE)

            for g in range(G):
                for q in range(NQ):
                    if g:
                        pe.wait_ge(t_mul, q + 1)
                    mm(ps[4 + q][:, :], pick[g][seg_slice(q), :], modrow[seg_slice(q), 1, :],
                       start=True, stop=True).then_inc(t_bc, 1)

        @block.vector
        def _(dve):
            n = 0
            v = nc.vector

            def link(ins):
                nonlocal n
                n += 1
                ins.then_inc(dch, 1)
                dve.wait_ge(dch, n)

            link(v.memset(small[:, 63:64], EPS))
            dve.wait_ge(s_zero, 7)
            dve.wait_ge(rows_ps, 1)
            v.tensor_copy(gcol[:, :, :], ps[6][:, 32:56].rearrange("p (a c) -> p a c", a=3)).then_inc(tap_rdy, 1)
            v.tensor_copy(condT[:, :, 0:2].rearrange("p k c -> p c k"),
                          ps[6][:, 0:32].rearrange("p (c k) -> p c k", c=2)).then_inc(cond_rdy, 1)
            dve.wait_ge(tap_ps, 1)
            v.tensor_copy(tapT[:, :, :], ps[7][:, 0:256].rearrange("p (c k) -> p c k", c=CC)).then_inc(tap_rdy, 1)
            dve.wait_ge(s_x[1], 32)
            v.tensor_tensor(xres[:, 1, :], xres[:, 1, :], posb, ALU.add).then_inc(xpos, 1)

            def evac_seg(bank, s, units):
                dve.wait_ge(used, units)
                v.tensor_tensor(modrow[:, s % 4, :], ps[bank][:, :], modrow[:, s % 4, :], ALU.add).then_inc(mod_ev, 1)

            dve.wait_ge(s_bmod, 32)
            evac_seg(0, 0, SEG_UNITS)
            for b in range(8):
                g = b // 4
                dve.wait_ge(xT_ps, b + 1)
                v.tensor_copy(hT[:, 4 * (b % 4):4 * (b % 4) + 4, g * P:(g + 1) * P],
                              ps[1 + b % 4][:, :].rearrange("p (k t) -> p k t", k=4)).then_inc(xT_ev, 1)
            evac_seg(5, 1, 2 * SEG_UNITS)
            for s in range(2):
                dve.wait_ge(modT_ps, s + 1)
                src = ps[6 + s][:, :].rearrange("p (j q r) -> p q j r", j=NQ, q=NQ)[:, :, :, 0:2]
                if s == 0:
                    v.tensor_copy(modcol[:, 0], src).then_inc(col_rdy, 1)
                else:
                    v.tensor_scalar(modcol[:, 1], src, 1.0, None, ALU.add).then_inc(col_rdy, 1)
            dve.wait_ge(col_rdy, 2)
            dve.wait_ge(xT_ev, 8)
            for kt in range(KT):
                q, j = divmod(kt, NQ)
                v.tensor_scalar(hT[:, kt, 0:P], hT[:, kt, 0:P], modcol[:, 1, q, j, 0:1], modcol[:, 0, q, j, 0:1],
                                ALU.mult, ALU.add).then_inc(h_dve, 1)
            for i in range(4):
                dst = gg[:, i // 2, i % 2, :]
                dve.wait_ge(gate_l, i + 1)
                v.scalar_tensor_tensor(dst, ps[4 + i][:, :], 0.0, dst, ALU.min, ALU.subtract).then_inc(gate_rdy, 1)
            dve.wait_ge(used, 2 * SEG_UNITS + 2 * PASS_UNITS)
            dve.wait_ge(xpos, 1)
            for i in range(4):
                g, hf = divmod(i, 2)
                dve.wait_ge(ev[0], i + 1)
                cs = slice(hf * BANK, (hf + 1) * BANK)
                v.tensor_tensor(uu[:, g, cs], ps[4 + i][:, :], sig[:, g, cs], ALU.mult).then_inc(ev[1], 1)
            for i in range(4):
                g = i // 2
                dve.wait_ge(uT_ps, i + 1)
                v.tensor_copy(uT[:, 4 * (i % 2):4 * (i % 2) + 4, g, PAD:PAD + P],
                              ps[4 + i][:, :].rearrange("p (c t) -> p c t", c=4)).then_inc(uT_ev, 1)
            dve.wait_ge(uT_ev, 4)
            done = 0
            for c0 in range(0, CC, 2):
                for k in range(TAPS):
                    for cc in (c0, c0 + 1):
                        src = uT[:, cc, :, k:k + P]
                        if k == 0:
                            last = v.tensor_scalar(convacc[:, cc], src, tapT[:, cc, 0:1], tapT[:, cc, TAPS:TAPS + 1],
                                                   ALU.mult, ALU.add)
                        else:
                            dve.wait_ge(conv_c, done - 1)
                            last = v.scalar_tensor_tensor(convacc[:, cc], src, tapT[:, cc, k:k + 1], convacc[:, cc],
                                                          ALU.mult, ALU.add)
                        last.then_inc(conv_c, 1)
                        done += 1

            def gla(gi, g):
                for d in range(2):
                    dve.wait_ge(a_exp, 6 * gi + 3 * d + 1)
                    cols = (63, 127) if d == 0 else (0, 64)
                    for ch in range(2):
                        link(v.tensor_copy(decay[:, d, ch, :], qTt[:, d, :, cols[ch]]))
                    dve.wait_ge(a_ps, 6 * gi + 5)
                    v.scalar_tensor_tensor(qTt[:, d], ps[6][:, :].rearrange("p (h t) -> p h t", h=HEADS), QSCALE,
                                           qTt[:, d], ALU.mult, ALU.mult).then_inc(a_rdy, 1)
                    dve.wait_ge(a_exp, 6 * gi + 3 * d + 2)
                    dve.wait_ge(a_ps, 6 * gi + 6)
                    v.tensor_tensor(kTt[:, d], ps[7][:, :].rearrange("p (h t) -> p h t", h=HEADS), kTt[:, d],
                                    ALU.mult).then_inc(a_rdy, 1)
                    dve.wait_ge(a_exp, 6 * gi + 3 * d + 3)
                    v.tensor_tensor(kdec[:, d, :], qk[:, g, 512:1024], kdec[:, d, :], ALU.mult).then_inc(a_rdy, 2)
                for d in range(2):
                    dve.wait_ge(at_ps, 2 * gi + d + 1)
                    v.copy_predicated(attnT[:, d], incl[d].bitcast(U32).unsqueeze(1).broadcast_to([P, HEADS, P]),
                                      ps[2 + d][:, :].rearrange("p (h t) -> p h t", h=HEADS)).then_inc(at_ev, 1)
                if g == 1:
                    dve.wait_ge(s_s0, 16)
                    for i in range(8):
                        d, h = divmod(i, HEADS)
                        dve.wait_ge(kv_ps, i // 2 + 1)
                        v.scalar_tensor_tensor(smid[:, d, h, :], s0[:, d, h, :], decay[:, d, d, h:h + 1],
                                               ps[4 + i // 2][:, (i % 2) * DV:(i % 2 + 1) * DV],
                                               ALU.mult, ALU.add).then_inc(kv_ev, 1)
                else:
                    dve.wait_ge(kv_ev, 12)
                    for i in range(8):
                        d, h = divmod(i, HEADS)
                        dve.wait_ge(kv2_ps, i // 2 + 1)
                        v.scalar_tensor_tensor(s0[:, d, h, :], smid[:, d, h, :], decay[:, d, 1 - d, h:h + 1],
                                               ps[4 + i // 2][:, (i % 2) * DV:(i % 2 + 1) * DV],
                                               ALU.mult, ALU.add).then_inc(fin_rdy, 1)
                dve.wait_ge(o_sq, gi + 1)
                link(v.reciprocal(small[:, 20 + 4 * g:24 + 4 * g], small[:, 16 + 4 * g:20 + 4 * g]))
                for h in range(HEADS):
                    v.scalar_tensor_tensor(vv[:, g, h * DV:(h + 1) * DV], ps[2 + h // 2][:, (h % 2) * DV:(h % 2 + 1) * DV],
                                           small[:, 20 + 4 * g + h:21 + 4 * g + h], rs[:, g, h * DV:(h + 1) * DV],
                                           ALU.mult, ALU.mult).then_inc(o_rdy, 1)

            dve.wait_ge(ev[4], 4)
            gla(0, 1)
            dve.wait_ge(s_bmod, 32)
            evac_seg(0, 2, 2 * SEG_UNITS + 5 * PASS_UNITS + SEG_UNITS)
            gla(1, 0)
            evac_seg(1, 3, 2 * SEG_UNITS + 5 * PASS_UNITS + 2 * SEG_UNITS)
            dve.wait_ge(s_bmod2, 32)
            evac_seg(0, 4, 2 * SEG_UNITS + 5 * PASS_UNITS + 3 * SEG_UNITS)
            for i in range(4):
                g, b = divmod(i, 2)
                dve.wait_ge(back_ps, i + 1)
                link(v.bn_stats(stats[:, g, b, :], ps[4 + i][:, :]))
            for g in range(G):
                link(v.bn_aggr(small[:, 50 + 2 * g:52 + 2 * g], stats[:, g, 0:2, :]))
            v.tensor_copy(small[:, 28:30], small[:, 51:54:2]).then_inc(back_var, 1)
            dve.wait_ge(o_sq, 3)
            link(v.reciprocal(small[:, 34:36], small[:, 32:34]))
            for g in range(G):
                for b in range(2):
                    last = v.tensor_scalar(uu[:, g, b * BANK:(b + 1) * BANK], ps[4 + 2 * g + b][:, :],
                                           small[:, 50 + 2 * g:51 + 2 * g], small[:, 34 + g:35 + g],
                                           ALU.subtract, ALU.mult)
                last.then_inc(back_ev, 1)
            evac_seg(1, 5, 2 * SEG_UNITS + 5 * PASS_UNITS + 4 * SEG_UNITS)
            for i in range(4):
                g, b = divmod(i, 2)
                dve.wait_ge(yT_ps, i + 1)
                v.tensor_tensor(hT[:, 4 * b:4 * b + 4, g * P:(g + 1) * P],
                                ps[2 + i][:, :].rearrange("p (k t) -> p k t", k=4),
                                gcol[:, 0, 4 * b:4 * b + 4].unsqueeze(2).broadcast_to([P, 4, P]), ALU.mult).then_inc(yT_ev, 1)
            dve.wait_ge(s_ln, 64)
            dve.wait_ge(mod_ev, 5)
            link(v.scalar_tensor_tensor(lnrow[:, 1, :], modrow[:, 0, :], 1.0, lnrow[:, 1, :], ALU.add, ALU.mult))
            link(v.scalar_tensor_tensor(modrow[:, 0, :], modrow[:, 0, :], 1.0, lnrow[:, 0, :], ALU.add, ALU.mult))
            v.tensor_tensor(modrow[:, 3, :], modrow[:, 3, :], lnrow[:, 1, :], ALU.add).then_inc(row2, 1)

            dve.wait_ge(bc_ev, 8)
            for p in range(2):
                dve.wait_ge(used, 6 * SEG_UNITS + 5 * PASS_UNITS + (p + 1) * PASS_UNITS)
                for g in range(G):
                    for hf in range(2):
                        q = 2 * p + hf
                        cs = slice(q * BANK, (q + 1) * BANK)
                        ins = v.tensor_tensor(g1b[:, g, cs], ps[4 * p + 2 * g + hf][:, :], g1b[:, g, cs], ALU.mult)
                        ins.then_inc(m_ev, 1)
                        dve.wait_ge(m_ev, 4 * p + 2 * g + hf + 1)
                        link(v.scalar_tensor_tensor(xres[:, g, cs], xres[:, g, cs], ALPHA, g1b[:, g, cs], ALU.mult, ALU.add))
                        v.bn_stats(stats[:, g, q, :], xres[:, g, cs]).then_inc(dch, 1)
                        n += 1
            dve.wait_ge(dch, n)
            for g in range(G):
                v.bn_aggr(small[:, 36 + 2 * g:38 + 2 * g], stats[:, g, :, :]).then_inc(ln_v, 1)
            for g in range(G):
                dve.wait_ge(ln_s, g + 1)
                link(v.reciprocal(small[:, 42 + g:43 + g], small[:, 40 + g:41 + g]))
                link(v.tensor_scalar(xres[:, g, :], xres[:, g, :], small[:, 36 + 2 * g:37 + 2 * g],
                                     small[:, 42 + g:43 + g], ALU.subtract, ALU.mult))
                if g == 0:
                    dve.wait_ge(bc_ev, 24)
                link(v.tensor_tensor(h2[:, g, :], xres[:, g, :], G2b[:, g, :], ALU.mult))
                v.tensor_tensor(h2[:, g, :], h2[:, g, :], B2b[:, g, :], ALU.add).then_inc(h2_rdy, 1)
                for b in range(2):
                    dve.wait_ge(h2T_ps, 4 * g + 2 * b + 1)
                    v.tensor_copy(hT[:, 8 * b:8 * b + 4, g * P:(g + 1) * P],
                                  ps[2 * b][:, :].rearrange("p (k t) -> p k t", k=4)).then_inc(h2T_v, 1)
            v.memset(acc, 0.0).then_inc(st_add, 8)
            dve.wait_ge(st_add, 8)

            N8 = G * NGRP
            f = lambda i: rt[:, i, 0:32]
            f3 = lambda i: rt[:, i, 0:32].rearrange("p (a b) -> p a b", b=PER)
            f8 = lambda i: rt[:, 13, 8 * i:8 * i + 8]
            b4 = lambda a: a.unsqueeze(2).broadcast_to([P, a.shape[1], PER])
            bN = lambda a: a.unsqueeze(2).broadcast_to([P, G, NE])
            g16 = lambda i: rt[:, i, 0:32].rearrange("p (g e) -> p g e", g=G)
            dve.wait_ge(s_wr, 32)
            dve.wait_ge(lg_ps, 2)
            link(v.tensor_tensor(g16(0), ps[4][:, 0:32].rearrange("p (g e) -> p g e", g=G),
                                 br[:, :].unsqueeze(1).broadcast_to([P, G, NE]), ALU.add))
            link(v.tensor_reduce(small[:, 24:26], g16(0), AX.X, ALU.max))
            v.tensor_scalar(small[:, 44:46], small[:, 24:26], -1.0, None, ALU.mult).then_inc(lmax, 1)
            dve.wait_ge(lexp, 2)
            link(v.reciprocal(small[:, 54:56], small[:, 48:50]))
            link(v.tensor_tensor(g16(2), g16(1), bN(small[:, 54:56]), ALU.mult))

            def best(src, mx, key, hot):
                link(v.tensor_reduce(mx, src, AX.X, ALU.max))
                link(v.tensor_tensor(key, src, b4(mx), ALU.is_equal))
                link(v.tensor_tensor(key, key, key4[:, 0:4 * mx.shape[1]].rearrange("p (a b) -> p a b", b=PER), ALU.mult))
                link(v.tensor_reduce(f8(3)[:, 0:mx.shape[1]], key, AX.X, ALU.max))
                link(v.tensor_tensor(hot, key, b4(f8(3)[:, 0:mx.shape[1]]), ALU.is_equal))

            best(f3(2), f8(0), f3(3), f3(4))
            link(v.scalar_tensor_tensor(f(5), f(4), -4.0, f(2), ALU.mult, ALU.add))
            best(f3(5), f8(1), f3(3), f3(6))
            link(v.tensor_tensor(f8(0), f8(0), f8(1), ALU.add))
            grp = rt[:, 7, 0:8]
            best(f8(0).rearrange("p (a b) -> p a b", b=NGRP), small[:, 24:26],
                 rt[:, 3, 0:8].rearrange("p (a b) -> p a b", b=NGRP), grp.rearrange("p (a b) -> p a b", b=NGRP))
            link(v.tensor_tensor(f(4), f(4), f(6), ALU.add))
            v.tensor_tensor(f3(8), f3(4), b4(grp), ALU.mult).then_inc(sel_rdy, 1)
            dve.wait_ge(sel_rdy, 1)
            link(v.tensor_tensor(f(5), f(8), f(2), ALU.mult))
            link(v.tensor_reduce(small[:, 24:26], g16(5), AX.X, ALU.add))
            link(v.reciprocal(small[:, 26:28], small[:, 24:26]))
            link(v.tensor_tensor(g16(5), g16(5), bN(small[:, 26:28]), ALU.mult))
            dve.wait_ge(rk_ps, 1)
            link(v.scalar_tensor_tensor(f(7), ps[5][:, 0:32], 1.0, f(8), ALU.add, ALU.mult))
            link(v.tensor_scalar(f(7), f(7), -1.0, None, ALU.add))
            ov, ovp = rt[:, 6, 0:NE], rt[0:NE, 6, NE:NE + 1]
            for i in range(1, 4):
                for dst, src in ((ov, ps[5][:, 32:48]), (ovp, ps[5][0:NE, 48:49])):
                    if i == 1:
                        link(v.tensor_scalar(dst, src, HALF + 0.5, None, ALU.is_gt))
                    else:
                        link(v.scalar_tensor_tensor(dst, src, i * HALF + 0.5, dst, ALU.is_gt, ALU.add))
            v.tensor_copy(rt[0:NE, 9:13, :], ovp.unsqueeze(2).broadcast_to([NE, 4, 32])).then_inc(ov_rdy, 1)
            dve.wait_ge(cx_ps, 1)
            link(v.tensor_tensor(rt[:, 3, 0:NE], ps[6][:, 0:NE], ov, ALU.add))
            ex = lambda i: extra[:, i, :].rearrange("p (j e) -> p j e", j=MAX_EXTRA)
            jn = lambda a: a.unsqueeze(1).broadcast_to([P, MAX_EXTRA, NE])
            jrow = const[:, C_J:C_J + NE * MAX_EXTRA].rearrange("p (j e) -> p j e", j=MAX_EXTRA)
            link(v.tensor_tensor(ex(0), jn(rt[:, 3, 0:NE]), jrow, ALU.is_le))
            link(v.tensor_tensor(ex(1), ex(0), jn(ov), ALU.mult))
            link(v.tensor_reduce(extra[:, 2, 0:MAX_EXTRA], ex(0), AX.X, ALU.add))
            link(v.tensor_reduce(extra[:, 3, 0:MAX_EXTRA], ex(1), AX.X, ALU.add))
            link(v.tensor_tensor(extra[:, 4, 0:MAX_EXTRA], const[:, C_JV:C_JV + MAX_EXTRA],
                                 extra[:, 3, 0:MAX_EXTRA], ALU.subtract))
            link(v.tensor_scalar(b64[:, NE:NSTEP], extra[:, 4, 0:MAX_EXTRA], float(HALF), None, ALU.mult))
            link(v.tensor_scalar(vtab[:, :], extra[:, 2, 0:MAX_EXTRA], NE - 0.5, None, ALU.is_lt))
            link(v.tensor_copy(etab[:, :], const[:, C_EXP:C_EXP + NSTEP + 1]))
            v.tensor_scalar(etab[:, NE:NSTEP], extra[:, 2, 0:MAX_EXTRA], NE - 1.0, None, ALU.min).then_inc(tab_rdy, 1)
            dve.wait_ge(tab_rdy, 1)

            def select(t, e):
                for g in range(G):
                    v.tensor_scalar(sel[:, g, :], iota, b64[:, bass.ds(t, 1)], rt[:, 7, bass.ds(e + g * NE, 1)],
                                    ALU.add, ALU.is_equal).then_inc(st_onehot, 1)
                dve.wait_ge(st_onehot, t * 2 + 2)
                for g in range(G):
                    last = v.tensor_scalar(wsel[:, g, :], sel[:, g, :], rt[:, 5, bass.ds(e + g * NE, 1)], None, ALU.mult)
                last.then_inc(st_sel, 1)

            def expert(t):
                dve.wait_ge(st_gath, t * 3 + 1)
                v.tensor_copy(XT[:, 0:8, :], ps[2][:, :].rearrange("p (k s) -> p k s", k=8)).then_inc(st_xv, 1)
                dve.wait_ge(st_hs, t + 1)
                v.tensor_tensor(hh, hs, ps[1][:, :], ALU.mult).then_inc(st_h, 1)
                dve.wait_ge(st_hTp, t + 1)
                v.tensor_copy(hTm, ps[7][:, :].rearrange("p (j t) -> p j t", j=4)).then_inc(st_hTv, 1)
                nxt = dve.value_load(etab[0:1, bass.ds(t + 1, 1)], min_val=0, max_val=NE - 1)
                select(t + 1, nxt)
                dve.wait_ge(used, t * STEP_UNITS + (PRE_UNITS + 24))
                v.tensor_copy(ye[:, 0:BANK], ps[5][:, :]).then_inc(st_yv, 1)
                for j in range(8):
                    g, b, hf = j // 4, j // 2 % 2, j % 2
                    c0 = hf * 1024 + b * BANK
                    dve.wait_ge(st_cmb, t * 8 + (j + 1))
                    v.tensor_tensor(acc[:, g, c0:c0 + BANK], ps[(2, 3, 0, 1)[j % 4]][:, :], acc[:, g, c0:c0 + BANK],
                                    ALU.add).then_inc(st_add, 1)

            select(0, 0)
            with dve.Fori(0, NE) as t:
                expert(t)
            with dve.Fori(0, MAX_EXTRA) as j:
                go = dve.value_load(vtab[0:1, bass.ds(j, 1)], min_val=0, max_val=1)
                with dve.If(go > 0):
                    expert(j + NE)

            dve.wait_ge(x1_rdy, 2)
            for g in range(G):
                for q in range(NQ):
                    cs = slice(q * BANK, (q + 1) * BANK)
                    dve.wait_ge(t_bc, 4 * g + q + 1)
                    v.tensor_tensor(acc[:, g, cs], ps[4 + q][:, :], acc[:, g, cs], ALU.mult).then_inc(t_mul, 1)
                    dve.wait_ge(t_mul, 4 * g + q + 1)
                    link(v.scalar_tensor_tensor(acc[:, g, cs], xres[:, g, cs], ALPHA, acc[:, g, cs], ALU.mult, ALU.add))
                    link(v.bn_stats(stats[:, g, q, :], acc[:, g, cs]))
                v.bn_aggr(small[:, 36 + 2 * g:38 + 2 * g], stats[:, g, :, :]).then_inc(t_var, 1)
                dve.wait_ge(t_sd, g + 1)
                link(v.reciprocal(small[:, 42 + g:43 + g], small[:, 40 + g:41 + g]))
                v.tensor_scalar(acc[:, g, :], acc[:, g, :], small[:, 36 + 2 * g:37 + 2 * g],
                                small[:, 42 + g:43 + g], ALU.subtract, ALU.mult).then_inc(t_nrm, 1)
            for g in range(G):
                dve.wait_ge(t_gain, g + 1)
                v.tensor_tensor(acc[:, g, :], acc[:, g, :], lnb, ALU.add).then_inc(t_out, 1)


_INS = ['x_prompt', 'x_sample', 'state_gla', 'c', 'c_ctx', 'w_mod', 'b_mod', 'w_in', 'w_gate_up', 'b_gate',
        'gla_norm_g', 'w_dw', 'b_dw', 'conv_ln_g', 'conv_ln_b', 'w_out', 'ln1_g', 'ln1_b', 'ln2_g', 'ln2_b',
        'w_router', 'b_router', 'w_e_gate', 'w_e_up', 'w_e_down']
_OUTS = [((1, 128, 2048), 'float32'), ((1, 128, 2048), 'float32'), ((1, 1, 2, 4, 128, 256), 'float32')]


def _constants():
    import numpy as np
    t = np.zeros((P, C_END), np.float32)
    s, m = np.arange(P)[:, None], np.arange(P)[None, :]
    same = s // HALF == m // HALF
    t[:, C_ID:C_ID + P] = s == m
    t[:, C_INCF:C_INCF + P] = (same & (s <= m)) / TAU
    t[:, C_RESTF:C_RESTF + P] = (same & (s > m)) / TAU
    t[:, C_INCB:C_INCB + P] = (same & (s >= m)) / TAU
    t[:, C_RESTB:C_RESTB + P] = (same & (s < m)) / TAU
    t[:, C_BEFORE:C_BEFORE + P] = s < m
    t[:, C_ONES:C_ONES + P] = 1.0
    t[:, C_IOTA:C_IOTA + P] = m % HALF
    for g in range(G):
        t[g::32, C_SEL + g * P:C_SEL + (g + 1) * P] = 1.0
    t[:, C_KEY:C_KEY + 32] = np.tile([4, 3, 2, 1], 8)
    t[:, C_J:C_J + NE * MAX_EXTRA] = np.repeat(np.arange(MAX_EXTRA), NE)
    t[:, C_JV:C_JV + MAX_EXTRA] = np.arange(MAX_EXTRA) + 1
    t[:, C_EXP:C_END] = np.minimum(np.arange(NSTEP + 1), NE - 1)
    nf = D // 4
    omega = np.float32(1.0) / np.power(np.float32(10000.0), np.arange(nf, dtype=np.float32) / np.float32(nf))
    tok = np.arange(P)
    pr = (tok // 64).astype(np.float32)[:, None] * omega
    pc = (tok % 64).astype(np.float32)[:, None] * omega
    pos = np.concatenate([np.sin(pr), np.cos(pr), np.sin(pc), np.cos(pc)], axis=-1).astype(np.float32)
    return t, pos


def kernel(**inputs):
    import numpy as _np
    import concourse.bacc as _bacc
    from concourse import mybir as _mybir
    from concourse.bass_utils import run_bass_kernel_spmd as _run

    nc = _bacc.Bacc("TRN2", target_bir_lowering=False, num_devices=1)
    arrays, args = {}, []
    table, pos = _constants()
    for name, a in [(n, inputs[n]) for n in _INS] + [("table", table), ("pos", pos)]:
        a = _np.ascontiguousarray(a)
        arrays[f"in_{name}_dram"] = a
        args.append(nc.dram_tensor(f"in_{name}_dram", a.shape, _mybir.dt.from_np(a.dtype), kind="ExternalInput").ap())
    for i, (shape, dtype) in enumerate(_OUTS):
        dt = _mybir.dt.from_np(_np.dtype(dtype))
        args.append(nc.dram_tensor(f"out_{i}_dram", shape, dt, kind="ExternalOutput").ap())
    hybrid_step(nc, *args)
    r = _run(nc, [arrays], core_ids=[0])
    return tuple(r.results[0][f"out_{i}_dram"] for i in range(len(_OUTS)))
```

```python
from contextlib import ExitStack

import concourse.bass as bass
from concourse import mybir

ALU = mybir.AluOpType
ACT = mybir.ActivationFunctionType
F32 = mybir.dt.float32
I32 = mybir.dt.int32
U32 = mybir.dt.uint32
AX = mybir.AxisListType

P = 128
G = 2
D = 2048
KT = D // P
BANK = 512
NQ = D // BANK
HEADS, DK, DV = 4, 128, 256
HALF = 64
CAP = 128
BLK = 32
NBLK = CAP // BLK
GLA_W = CONV_W = 1024
CC = CONV_W // P
TAPS, PAD = 31, 15
RANK = 16
NE, NGRP, PER = 16, 4, 4
FF = 1024
FT = FF // P
EPS = 1e-5
ALPHA = 2.0 ** 0.25
TAU = 16.0
QSCALE = DK ** -0.5

SLOTS = 8
UNIT = 2048
SEG_UNITS = KT
PASS_UNITS = 8
PASSES_IN = 5
PASS_COL = (4128, 3104, 0, 1024, 2048)
Z_COL = 3072
GATE_BANKS = {1: (1, 2), 0: (2, 3)}
U_BANKS = (5, 6, 0, 5)
H2T_BANKS = (0, 1, 2, 7)
STEP_UNITS = 24
PRE_UNITS = 6 * SEG_UNITS + (PASSES_IN + 2) * PASS_UNITS
MAX_EXTRA = G * P * 2 // (CAP + 1)
NSTEP = NE + MAX_EXTRA

C_ID, C_INCF, C_RESTF, C_INCB, C_RESTB, C_BEFORE, C_ONES, C_IOTA, C_SEL = [P * i for i in range(9)]
C_SUM = C_SEL + 8 * P
C_KEY = C_SUM + 2
C_J = C_KEY + 32
C_EXP = C_J + 16 * MAX_EXTRA
C_OFF = C_EXP + NSTEP + 1
C_END = C_OFF + NSTEP + 1


def hybrid_step(nc, x_prompt, x_sample, state_gla, c, c_ctx, w_mod, b_mod, w_in, w_gate_up, b_gate,
                gla_norm_g, w_dw, b_dw, conv_ln_g, conv_ln_b, w_out, ln1_g, ln1_b, ln2_g, ln2_b,
                w_router, b_router, w_e_gate, w_e_up, w_e_down, table, pos,
                y_prompt, y_sample, new_state):
    with ExitStack() as ctx:
        def sb(name, shape, dt=F32):
            return ctx.enter_context(nc.sbuf_tensor(name, shape, dt))

        def sem(name):
            return ctx.enter_context(nc.semaphore(name))

        ps = [ctx.enter_context(nc.psum_tensor(f"bank{i}", [P, BANK], F32)) for i in range(8)]

        ring = sb("ring", [P, SLOTS, UNIT])
        xres = sb("xres", [P, G, D])
        hT = sb("hT", [P, KT, G * P])
        arena = sb("arena", [P, 5 * 2048])
        work = sb("work", [P, 10720])
        const = sb("const", [P, C_END])
        modrow = sb("modrow", [P, 4, BANK])
        lnrow = sb("lnrow", [P, 2, BANK])
        condT = sb("condT", [P, KT, 32])
        gcol = sb("gcol", [P, 3, CC])
        tapT = sb("tapT", [P, CC, 32])
        wr = sb("wr", [P, KT, NE])
        br = sb("br", [P, NE])
        bcol = sb("bcol", [P, 2, NQ, NQ])
        modcol = sb("modcol", [P, 2, NQ, NQ, 2])
        decay = sb("decay", [P, 2, 2, HEADS])
        small = sb("small", [P, 64])
        stats = sb("stats", [P, G, NQ, 6])
        rt = sb("rt", [P, 14, 32])
        extra = sb("extra", [P, 10, NE * MAX_EXTRA])
        steps = sb("steps", [P, 5, NSTEP + 1], I32)

        def part(t, at, *dims):
            n = 1
            for d in dims:
                n *= d
            v = t[:, at:at + n]
            if len(dims) == 2:
                return v.rearrange("p (a b) -> p a b", a=dims[0])
            if len(dims) == 3:
                return v.rearrange("p (a b c) -> p a b c", a=dims[0], b=dims[1])
            return v

        qk = part(arena, 0, G, 1024)
        vv = part(arena, 2048, G, 1024)
        rs = part(arena, 4096, G, 1024)
        uu = part(arena, 6144, G, 1024)
        convacc = part(arena, 6144, CC, G, P)
        gg = part(arena, 8192, G, 2, BANK)
        wz = part(arena, 0, KT, 32)
        zT = part(arena, 2048, 256)
        wgu = part(arena, 5120, 2, BANK)
        taprow = part(arena, 4096, 1024)
        posb = part(arena, 6144, D)
        rows = arena[0:88, 8192:8192 + P]
        h2 = part(arena, 0, G, D)
        acc = part(arena, 4096, G, D)
        g1b = part(arena, 4096, G, D)
        wsel = part(arena, 8192, G, CAP)
        wselT = part(arena, 8448, G, P)
        hTm = part(arena, 8704, NBLK, 2, P)
        wselN = part(arena, 9728, G, P)
        kTt = part(work, 0, 2, HEADS, P)
        kdec = part(work, 1024, 2, BANK)
        attnT = part(work, 2048, 2, HEADS, P)
        qTt = part(work, 3072, 2, HEADS, P)
        smid = part(work, 4096, 2, HEADS, DV)
        sig = part(work, 4096, G, 1024)
        s0 = part(work, 6144, 2, HEADS, DV)
        UW = P + 2 * PAD
        uT = part(work, 8192, CC, G, UW)
        modpart = part(work, 0, 2, BANK)
        grelu = part(work, 0, 2, BANK)
        segrow = part(work, 3072, BANK)
        G2b = part(work, 0, G, D)
        B2b = part(work, 4096, G, D)
        XT = part(work, 0, KT, CAP)
        ye = part(work, 2048, NBLK, BANK)
        hs = part(work, 8704, 2, 256)
        hh = part(work, 9216, 2, 256)
        sel = part(work, 9728, G, CAP)
        yf = part(hT[:, :, :].rearrange("p k t -> p (k t)"), 0, D)
        lng = part(work, 4096, D)
        lnb = part(work, 6144, D)
        junk = part(work, 8192, BANK)

        ident = const[:, C_ID:C_ID + P]
        incl = [const[:, C_INCF:C_INCF + P], const[:, C_INCB:C_INCB + P]]
        rest = [const[:, C_RESTF:C_RESTF + P], const[:, C_RESTB:C_RESTB + P]]
        before = const[:, C_BEFORE:C_BEFORE + P]
        ones = const[:, C_ONES:C_ONES + P]
        iota = const[:, C_IOTA:C_IOTA + P]
        pick = lambda g, q: const[:, C_SEL + (2 * q + g) * P:C_SEL + (2 * q + g + 1) * P]
        key4 = const[:, C_KEY:C_KEY + 32]

        slot = [sem(f"slot{i}") for i in range(SLOTS)]
        used = sem("weights_used")
        s_zero = sem("zeroed")
        s_const, s_rows, s_tap, s_wz, s_wgu, s_s0, s_wr, s_bmod, s_ln, s_lnb, s_ln2 = [
            sem(n) for n in ("const_in", "rows_in", "taps_in", "wz_in", "wgu_in", "s0_in", "router_in",
                             "bmod_in", "ln1_in", "ln1_bcast_in", "ln2_bcast_in")]
        s_x = [sem("x_prompt_in"), sem("x_sample_in")]
        silu_c = sem("cond_silu")
        rows_ps, tap_ps, cond_rdy, tap_rdy, xpos = [sem(n) for n in (
            "rows_ps", "tap_ps", "cond_ready", "tap_ready", "pos_added")]
        xT_ps, xT_ev, part_ev, col_ps, bcol_rdy, col_rdy, h_dve, h_act = [sem(n) for n in (
            "xT_ps", "xT_evacuated", "modpart_evacuated", "modcol_ps", "bcol_ready", "modcol_ready",
            "h1_prompt", "h1_sample")]
        seg_out, seg_add, seg_dve = [sem(n) for n in ("seg_out", "seg_added", "seg_evacuated")]
        z_ps, z_ev, gate_ps, gate_out, gate_rdy = [sem(n) for n in (
            "z_ps", "z_evacuated", "gate_ps", "gate_out", "gate_ready")]
        ev = [sem(f"pass{i}_evacuated") for i in range(PASSES_IN)]
        uT_ps, uT_ev, conv_c, back_ps, back_var, back_ev = [sem(n) for n in (
            "uT_ps", "uT_evacuated", "conv_chain", "conv_back_ps", "conv_var", "conv_normed")]
        a_ps, a_exp, a_rdy, at_ps, at_ev, kv_ps, kv_ev, kv2_ps, o_ps, o_sq, o_rdy = [sem(n) for n in (
            "decays_ps", "decays_exp", "qk_decayed", "attn_ps", "attn_masked", "kv_ps", "state_mid", "kv2_ps",
            "o_ps", "o_rms", "o_ready")]
        fin_rdy, state_out = sem("final_state_ready"), sem("state_out")
        yT_ps, yT_ev, cT_ps, cT_ev = [sem(n) for n in ("yT_ps", "yT_evacuated", "cT_ps", "cT_evacuated")]
        bc_ps, bc_ev, row2 = [sem(n) for n in ("bcast_ps", "bcast_evacuated", "ln1_mod_rows")]
        m_ev, ln_v, ln_s, xn_rdy, h2_rdy, h2T_ps, h2T_v, h2T_s, lg_ps = [sem(n) for n in (
            "m_evacuated", "ln1_var", "ln1_sd", "x_normed", "h2_ready", "h2T_ps", "h2T_dve", "h2T_act", "logits_ps")]
        lmax, lexp, sel_rdy, rk_ps, tab_rdy = [sem(n) for n in (
            "logit_max", "logit_exp", "selected", "rank_ps", "steps_ready")]
        dch, ach = sem("dve_chain"), sem("act_chain")
        st_onehot, st_sel, st_gath, st_wTp, st_wN, st_wT, st_xv, st_xa = [sem(n) for n in (
            "step_onehot", "step_weights", "step_gather_ps", "step_wT_ps", "step_wN", "step_wT", "step_x_dve", "step_x_act")]
        st_cmb, st_add = sem("step_combine_ps"), sem("step_added")
        bk_hs, bk_h, bk_hTp, bk_hT, bk_y, bk_yf = [sem(n) for n in (
            "block_silu", "block_h", "block_hT_ps", "block_hT", "block_y", "block_y_by_slot")]
        x1_rdy, t_bc, t_mul, t_var, t_sd, t_nrm, t_gain, t_out, out_s = [sem(n) for n in (
            "x1_ready", "tail_g2_ps", "tail_g2_used", "tail_var", "tail_sd", "tail_normed", "tail_gained",
            "tail_ready", "out_done")]
        pch = sem("pool_chain")

        wmod2, win2, wout2 = w_mod[0], w_in[0], w_out[0]

        def pass_bank(p, i):
            return (4 * p + i) % 7

        def pass_end(p):
            return 2 * SEG_UNITS + PASS_UNITS + 2 * PASS_UNITS * p - (1 if p else 0)

        def seg_slice(q):
            return slice(32 * q, 32 * q + 32)

        def for_steps(eng, expert, blocks):
            eng.wait_ge(tab_rdy, 1)
            with eng.Fori(0, NSTEP) as t:
                go = eng.value_load(steps[0:1, 3, bass.ds(t, 1)], min_val=0, max_val=1)
                with eng.If(go > 0):
                    nb = eng.value_load(steps[0:1, 1, bass.ds(t, 1)], min_val=1, max_val=NBLK)
                    b0 = eng.value_load(steps[0:1, 2, bass.ds(t, 1)], min_val=0, max_val=NBLK * NSTEP)
                    expert(t, b0)
                    for v in range(1, NBLK + 1):
                        with eng.If(nb == v):
                            blocks(t, b0, v)

        block = ctx.enter_context(nc.Block())

        @block.sync
        def _(sp):
            n = 0

            def unit(dst, src):
                nonlocal n
                if n >= SLOTS:
                    sp.wait_ge(used, n - SLOTS + 1)
                sp.dma_start(dst, src).then_inc(slot[n % SLOTS], 16)
                n += 1

            def segment(s, kts=range(KT)):
                for kt in kts:
                    unit(ring[:, n % SLOTS, :], wmod2[kt * P:(kt + 1) * P, s * D:(s + 1) * D])

            def first_mod(qb):
                for s in range(2):
                    for u in range(4):
                        unit(ring[:, n % SLOTS, :].rearrange("p (i n) -> p i n", i=4),
                             wmod2[u * 512:(u + 1) * 512, s * D + qb * BANK:s * D + (qb + 1) * BANK]
                             .rearrange("(i p) n -> p i n", i=4))

            def wide_pass(w, col, us=range(PASS_UNITS), seg=None, kt0=0):
                for i, u in enumerate(us):
                    unit(ring[:, n % SLOTS, :].rearrange("p (i n) -> p i n", i=2),
                         w[u * 256:(u + 1) * 256, col:col + 1024].rearrange("(i p) n -> p i n", i=2))
                    if seg is not None:
                        segment(seg, [kt0 + i])

            first_mod(0)
            for qb in range(1, NQ):
                first_mod(qb)
                wide_pass(win2, PASS_COL[0], (2 * qb - 2, 2 * qb - 1))
            wide_pass(win2, PASS_COL[0], (6, 7))
            for p in range(1, PASSES_IN):
                wide_pass(win2, PASS_COL[p], seg=2 + (p - 1) // 2, kt0=8 * ((p - 1) % 2))
            segment(4)
            wide_pass(wout2, 0)
            wide_pass(wout2, 1024)
            segment(5)

            def expert(t, e):
                for i in range(STEP_UNITS):
                    sl = i % SLOTS
                    r = i // 2
                    if i < 16:
                        w = w_e_gate if i % 2 == 0 else w_e_up
                        src = w[0, e, r * 256:(r + 1) * 256, :].rearrange("(i p) n -> p i n", i=2)
                        dst = ring[:, sl, :].rearrange("p (i n) -> p i n", i=2)
                    else:
                        src = w_e_down[0, e, (i - 16) * P:(i - 15) * P, :]
                        dst = ring[:, sl, :]
                    sp.wait_ge(used, t * STEP_UNITS + (PRE_UNITS + i - SLOTS + 1))
                    sp.dma_start(dst, src).then_inc(slot[sl], 16)

            with sp.Fori(0, NE) as e:
                expert(e, e)
            sp.wait_ge(tab_rdy, 1)
            with sp.Fori(0, MAX_EXTRA) as j:
                go = sp.value_load(steps[0:1, 3, bass.ds(j + NE, 1)], min_val=0, max_val=1)
                eo = sp.value_load(steps[0:1, 0, bass.ds(j + NE, 1)], min_val=0, max_val=NE - 1)
                with sp.If(go > 0):
                    expert(j + NE, eo)

        @block.gpsimd
        def _(pool):
            for t in (condT[:, :, :], modrow[:, :, :], lnrow[:, :, :], wgu, attnT, uT):
                nc.gpsimd.memset(t, 0.0).then_inc(s_zero, 1)
            nc.gpsimd.memset(zT, 1.0).then_inc(s_zero, 1)
            def gates(g):
                for d in range(2):
                    pool.wait_ge(gate_out, 4 * (1 - g) + 2 * d + 2)
                    nc.gpsimd.tensor_tensor(gg[:, g, d, :], gg[:, g, d, :], grelu[:, d, :], ALU.add).then_inc(gate_rdy, 1)

            def add_segment(s):
                pool.wait_ge(seg_out, s - 1)
                nc.gpsimd.tensor_tensor(modrow[:, s - 2, :], modrow[:, s - 2, :], segrow, ALU.add).then_inc(seg_add, 1)

            gates(1)
            pool.wait_ge(s_bmod, 32)
            add_segment(2)
            gates(0)
            add_segment(3)
            pool.wait_ge(xn_rdy, 2)
            pool.wait_ge(s_lnb, 32)
            for g in range(G):
                nc.gpsimd.tensor_tensor(xres[:, g, :], xres[:, g, :], lng, ALU.mult).then_inc(pch, 1)
            for g in range(G):
                pool.wait_ge(pch, g + 1)
                nc.gpsimd.tensor_tensor(xres[:, g, :], xres[:, g, :], lnb, ALU.add).then_inc(x1_rdy, 1)
            pool.wait_ge(s_ln2, 32)
            for g in range(G):
                pool.wait_ge(t_nrm, g + 1)
                nc.gpsimd.tensor_tensor(acc[:, g, :], acc[:, g, :], lng, ALU.mult).then_inc(t_gain, 1)

        @block.scalar
        def _(act):
            n = 0

            def link(ins):
                nonlocal n
                n += 1
                ins.then_inc(ach, 1)
                act.wait_ge(ach, n)

            act.dma_start(const[:, :], table).then_inc(s_const, 16)
            r128 = lambda a: a.rearrange("(k p) -> k p", p=P)
            act.dma_start(rows[0:16, :], r128(c_ctx)).then_inc(s_rows, 16)
            act.dma_start(rows[16:32, :], r128(c[0])).then_inc(s_rows, 16)
            act.dma_start(rows[32:40, :], r128(gla_norm_g[0])).then_inc(s_rows, 16)
            act.dma_start(rows[40:48, :], r128(conv_ln_g[0])).then_inc(s_rows, 16)
            act.dma_start(rows[48:56, :], r128(conv_ln_b[0])).then_inc(s_rows, 16)
            act.dma_start(rows[56:88, :], r128(b_mod[0, 0:2 * D])).then_inc(s_rows, 16)
            act.dma_start(taprow[0:TAPS, :], w_dw[0]).then_inc(s_tap, 16)
            act.dma_start(taprow[TAPS:TAPS + 1, :], b_dw).then_inc(s_tap, 16)
            act.dma_start(xres[:, 0, :], x_prompt[0]).then_inc(s_x[0], 16)
            act.dma_start(xres[:, 1, :], x_sample[0]).then_inc(s_x[1], 16)
            act.dma_start(posb, pos).then_inc(s_x[1], 16)
            act.wait_ge(s_zero, 7)
            mod_rows = b_mod[0].rearrange("(s q j) -> q s j", q=NQ, j=BANK)
            for g in range(G):
                act.dma_start(modrow[g:97 + g:32, :, :], mod_rows[:, 2:6, :]).then_inc(s_bmod, 16)
            for i, w in enumerate((ln1_g, ln1_b)):
                for g in range(G):
                    act.dma_start(lnrow[g:97 + g:32, i, :], w[0].rearrange("(q j) -> q j", q=NQ)).then_inc(s_ln, 16)
            act.dma_start(wz, win2[:, Z_COL:Z_COL + 32].rearrange("(k p) n -> p k n", p=P)).then_inc(s_wz, 16)
            for d in range(2):
                act.dma_start(wgu[RANK * d:RANK * d + RANK, d, :], w_gate_up[0, d]).then_inc(s_wgu, 16)
            act.dma_start(wgu[2 * RANK:2 * RANK + 1, :, :], b_gate).then_inc(s_wgu, 16)
            act.dma_start(s0, state_gla[0, 0].rearrange("d h k v -> k d h v")).then_inc(s_s0, 16)
            act.dma_start(wr[:, :, :], w_router.rearrange("(k p) e -> p k e", p=P)).then_inc(s_wr, 16)
            act.dma_start(br[:, :], b_router.partition_broadcast(P)).then_inc(s_wr, 16)

            act.wait_ge(s_rows, 96)
            nc.scalar.activation(rows[0:32, :], rows[0:32, :], ACT.Silu).then_inc(silu_c, 1)

            act.wait_ge(xT_ev, 8)
            for kt in range(KT):
                q, j = divmod(kt, NQ)
                act.wait_ge(col_rdy, q + 1)
                nc.scalar.activation(hT[:, kt, P:2 * P], hT[:, kt, P:2 * P], ACT.Identity,
                                     bias=modcol[:, 0, q, j, 1:2], scale=modcol[:, 1, q, j, 1:2]).then_inc(h_act, 1)

            def evac(p, dst, func):
                act.wait_ge(used, pass_end(p))
                for g in range(G):
                    for hf in range(2):
                        nc.scalar.activation(dst[:, g, hf * BANK:(hf + 1) * BANK],
                                             ps[pass_bank(p, 2 * g + hf)][:, :], func).then_inc(ev[p], 1)

            evac(0, sig, ACT.Sigmoid)
            act.wait_ge(z_ps, 1)
            nc.scalar.copy(zT[0:32, :], ps[6][0:32, 0:256]).then_inc(z_ev, 1)

            def gates(g, banks):
                if g == 0:
                    act.wait_ge(gate_rdy, 2)
                for d in range(2):
                    dst = gg[:, g, d, :]
                    act.wait_ge(gate_ps, 2 * (1 - g) + d + 1)
                    nc.scalar.activation(grelu[:, d, :], ps[banks[d]][:, :], ACT.Relu, scale=-1.0).then_inc(gate_out, 1)
                    link(nc.scalar.activation(dst, ps[banks[d]][:, :], ACT.Abs))
                    link(nc.scalar.activation(dst, dst, ACT.Exp, scale=-1.0))
                    nc.scalar.activation(dst, dst, ACT.Ln, bias=ones[:, 0:1]).then_inc(gate_out, 1)

            def segment_out(s):
                act.wait_ge(used, pass_end(2 * s - 2) + 1)
                if s == 3:
                    act.wait_ge(seg_add, 1)
                nc.scalar.copy(segrow, ps[7][:, :]).then_inc(seg_out, 1)

            gates(1, GATE_BANKS[1])
            evac(2, qk, ACT.Copy)
            segment_out(2)
            gates(0, GATE_BANKS[0])
            evac(3, vv, ACT.Copy)
            evac(4, rs, ACT.Silu)
            segment_out(3)

            for gi, g in enumerate((1, 0)):
                if gi:
                    act.wait_ge(o_ps, 2)
                else:
                    act.wait_ge(gate_rdy, 4)
                    act.wait_ge(seg_add, 2)
                for d in range(2):
                    act.wait_ge(a_ps, 6 * gi + 1 + d)
                    nc.scalar.activation(qTt[:, d], ps[2 + d][:, :].rearrange("p (h t) -> p h t", h=HEADS),
                                         ACT.Exp).then_inc(a_exp, 1)
                    nc.scalar.activation(kTt[:, d], ps[2 + d][:, :].rearrange("p (h t) -> p h t", h=HEADS),
                                         ACT.Exp, scale=-1.0).then_inc(a_exp, 1)
                    act.wait_ge(a_ps, 6 * gi + 3 + d)
                    nc.scalar.activation(kdec[:, d, :], ps[4 + d][:, :], ACT.Exp).then_inc(a_exp, 1)
                if g == 0:
                    for i in range(4):
                        act.wait_ge(kv_ps, 4 + i + 1)
                        nc.scalar.copy(smid[:, i // 2, 2 * (i % 2):2 * (i % 2) + 2, :],
                                       ps[4 + i][:, :].rearrange("p (h v) -> p h v", h=2)).then_inc(kv_ev, 1)
                for h in range(HEADS):
                    act.wait_ge(o_ps, 2 * gi + h // 2 + 1)
                    link(nc.scalar.activation(junk[:, 0:DV], ps[2 + h // 2][:, (h % 2) * DV:(h % 2 + 1) * DV],
                                              ACT.Square, accum_out=small[:, 4 * g + h:4 * g + h + 1]))
                nc.scalar.activation(small[:, 16 + 4 * g:20 + 4 * g], small[:, 4 * g:4 * g + 4], ACT.Sqrt,
                                     bias=small[:, 63:64], scale=1.0 / DV).then_inc(o_sq, 1)

            act.wait_ge(fin_rdy, 8)
            act.dma_start(new_state[0, 0].rearrange("d h k v -> k d h v"), s0).then_inc(state_out, 16)
            act.wait_ge(back_var, 1)
            nc.scalar.activation(small[:, 32:34], small[:, 28:30], ACT.Sqrt, bias=small[:, 63:64]).then_inc(o_sq, 1)
            for i in range(G * CC):
                g, cc = divmod(i, CC)
                act.wait_ge(cT_ps, i // 4 + 1)
                nc.scalar.activation(hT[:, CC + cc, g * P:(g + 1) * P], ps[(6, 7, 0, 1)[i // 4]][:, (i % 4) * P:(i % 4 + 1) * P],
                                     ACT.Silu, bias=gcol[:, 2, cc:cc + 1], scale=gcol[:, 1, cc:cc + 1]).then_inc(cT_ev, 1)
            for i in range(24):
                dst = (g1b, G2b, B2b)[i // 8]
                g, q = divmod(i % 8, NQ)
                act.wait_ge(bc_ps, i + 1)
                if i == 8:
                    act.wait_ge(cT_ps, 4)
                    act.wait_ge(state_out, 16)
                nc.scalar.copy(dst[:, g, q * BANK:(q + 1) * BANK], ps[4 + i % 4][:, :]).then_inc(bc_ev, 1)
            for g in range(G):
                act.wait_ge(ln_v, g + 1)
                nc.scalar.activation(small[:, 40 + g:41 + g], small[:, 37 + 2 * g:38 + 2 * g], ACT.Sqrt,
                                     bias=small[:, 63:64]).then_inc(ln_s, 1)
                for b in range(2):
                    act.wait_ge(h2T_ps, 4 * g + 2 * b + 2)
                    nc.scalar.copy(hT[:, 4 * (2 * b + 1):4 * (2 * b + 2), g * P:(g + 1) * P],
                                   ps[H2T_BANKS[2 * b + 1]][:, :].rearrange("p (k t) -> p k t", k=4)).then_inc(h2T_s, 1)
            act.wait_ge(h2_rdy, 2)
            act.dma_start(lng, ln1_g[0].partition_broadcast(P)).then_inc(s_lnb, 16)
            act.dma_start(lnb, ln1_b[0].partition_broadcast(P)).then_inc(s_lnb, 16)
            act.wait_ge(lmax, 1)
            for g in range(G):
                nc.scalar.activation(rt[:, 1, g * NE:(g + 1) * NE], rt[:, 0, g * NE:(g + 1) * NE], ACT.Exp,
                                     bias=small[:, 44 + g:45 + g], accum_out=small[:, 48 + g:49 + g]).then_inc(lexp, 1)

            def expert(t, b0):
                for i in (1, 3):
                    act.wait_ge(st_gath, t * 4 + (i + 1))
                    nc.scalar.copy(XT[:, 4 * i:4 * i + 4, :],
                                   ps[i][:, :].rearrange("p (k s) -> p k s", k=4)).then_inc(st_xa, 1)
                act.wait_ge(st_wTp, t + 1)
                nc.scalar.copy(wselN, ps[4][:, 0:256].rearrange("p (g t) -> p g t", g=G)).then_inc(st_wN, 1)

            def blocks(t, b0, v):
                act.wait_ge(used, t * STEP_UNITS + (PRE_UNITS + 16))
                for b in range(v):
                    if b >= 2:
                        act.wait_ge(bk_h, b0 + (b - 1))
                    nc.scalar.activation(hs[:, b % 2, :], ps[b][:, 0:256], ACT.Silu).then_inc(bk_hs, 1)
                act.wait_ge(st_cmb, t * 8 + 8)
                act.wait_ge(st_wN, t + 1)
                nc.scalar.copy(wselT, wselN).then_inc(st_wT, 1)
                act.wait_ge(used, t * STEP_UNITS + (PRE_UNITS + 24))
                act.wait_ge(bk_yf, b0 * 64 + 64)
                for b in range(v):
                    nc.scalar.copy(ye[:, b, :], ps[4 + b][:, :]).then_inc(bk_y, 1)
                    act.wait_ge(bk_y, b0 + (b + 2))
                    for q in range(4):
                        act.dma_start(yf[seg_slice(b), q * BANK:(q + 1) * BANK],
                                      ye[seg_slice(q), b, :]).then_inc(bk_yf, 16)

            for_steps(act, expert, blocks)

            act.wait_ge(x1_rdy, 2)
            act.dma_start(lng, ln2_g[0].partition_broadcast(P)).then_inc(s_ln2, 16)
            act.dma_start(lnb, ln2_b[0].partition_broadcast(P)).then_inc(s_ln2, 16)
            for g in range(G):
                act.wait_ge(t_var, g + 1)
                nc.scalar.activation(small[:, 40 + g:41 + g], small[:, 37 + 2 * g:38 + 2 * g], ACT.Sqrt,
                                     bias=small[:, 63:64]).then_inc(t_sd, 1)
            for g, y in enumerate((y_prompt, y_sample)):
                act.wait_ge(t_out, g + 1)
                act.dma_start(y[0], acc[:, g, :]).then_inc(out_s, 16)
            act.wait_ge(out_s, 32)

        @block.tensor
        def _(pe):
            n = 0
            mm = nc.tensor.matmul
            tr = nc.tensor.transpose

            def arrive():
                pe.wait_ge(slot[n % SLOTS], 16 * (n // SLOTS + 1))

            pe.wait_ge(s_const, 16)
            pe.wait_ge(s_rows, 96)
            pe.wait_ge(silu_c, 1)
            tr(ps[6][:, 0:88], rows[:, :], ident[0:88, 0:88]).then_inc(rows_ps, 1)
            pe.wait_ge(s_tap, 32)
            for cc in range(CC):
                last = tr(ps[7][:, cc * 32:cc * 32 + 32], taprow[0:32, cc * P:(cc + 1) * P], ident[0:32, 0:32])
            last.then_inc(tap_ps, 1)

            def seg_units(bank, kts):
                nonlocal n
                for kt in kts:
                    arrive()
                    for q in range(NQ):
                        last = mm(ps[bank][seg_slice(q), :], condT[:, kt, :],
                                  ring[:, n % SLOTS, q * BANK:(q + 1) * BANK], start=(kt == 0), stop=(kt == KT - 1))
                    last.then_inc(used, 1)
                    n += 1

            def first_mod(qb):
                nonlocal n
                for s in range(2):
                    if qb:
                        pe.wait_ge(part_ev, 2 * qb - 1 + s)
                    for u in range(4):
                        arrive()
                        for i in range(4):
                            last = mm(ps[4 + s][seg_slice(i), :], condT[:, 4 * u + i, :],
                                      ring[:, n % SLOTS, i * BANK:(i + 1) * BANK], start=(u == 0), stop=(u == 3))
                        last.then_inc(used, 1)
                        n += 1

            def mod_columns(qb):
                if qb:
                    pe.wait_ge(col_rdy, qb)
                for s in range(2):
                    pe.wait_ge(part_ev, 2 * qb + s + 1)
                    for j in range(NQ):
                        c0 = 8 * s + 2 * j
                        last = mm(ps[6][:, c0:c0 + 2], modpart[:, s, j * P:(j + 1) * P], const[:, C_SUM:C_SUM + 2],
                                  start=True, stop=True)
                last.then_inc(col_ps, 1)

            def wide_pass(bank, us=range(PASS_UNITS), before=None, after=None):
                nonlocal n
                for u in us:
                    arrive()
                    for i in range(2):
                        kt = 2 * u + i
                        for k in range(4):
                            if before and kt == 0:
                                before(k)
                            g, hf = divmod(k, 2)
                            last = mm(ps[bank[k]][:, :], hT[:, kt, g * P:(g + 1) * P],
                                      ring[:, n % SLOTS, i * 1024 + hf * BANK:i * 1024 + (hf + 1) * BANK],
                                      start=(kt == 0), stop=(kt == KT - 1))
                    last.then_inc(used, 1)
                    n += 1
                    if after:
                        after(u)

            pe.wait_ge(cond_rdy, 1)
            first_mod(0)
            pe.wait_ge(s_x[0], 16)
            for b in range(8):
                g = b // 4
                if b == 4:
                    pe.wait_ge(xpos, 1)
                if b >= 4:
                    pe.wait_ge(xT_ev, b - 3)
                for i in range(4):
                    kt = 4 * (b % 4) + i
                    last = tr(ps[b % 4][:, i * P:(i + 1) * P], xres[:, g, kt * P:(kt + 1) * P], ident)
                last.then_inc(xT_ps, 1)
            pe.wait_ge(bcol_rdy, 1)
            mod_columns(0)
            bank0 = [pass_bank(0, i) for i in range(4)]
            pe.wait_ge(xT_ev, 8)
            for qb in range(NQ):
                if qb < NQ - 1:
                    first_mod(qb + 1)
                pe.wait_ge(h_dve, 4 * qb + 4)
                pe.wait_ge(h_act, 4 * qb + 4)
                wide_pass(bank0, (2 * qb, 2 * qb + 1))
                if qb < NQ - 1:
                    mod_columns(qb + 1)
            pe.wait_ge(s_wz, 16)
            pe.wait_ge(col_rdy, NQ)
            for kt in range(KT):
                last = mm(ps[6][0:32, 0:256], wz[:, kt, :], hT[:, kt, :], start=(kt == 0), stop=(kt == KT - 1))
            last.then_inc(z_ps, 1)

            def gates(g, banks):
                for d in range(2):
                    mm(ps[banks[d]][:, :], zT[:, g * P:(g + 1) * P], wgu[:, d, :], start=True, stop=True).then_inc(gate_ps, 1)

            def u_transposed():
                pe.wait_ge(ev[1], 4)
                for i in range(G * CC):
                    g, cc = divmod(i, CC)
                    b = i // 4
                    if i == 12:
                        pe.wait_ge(uT_ev, 1)
                    last = tr(ps[U_BANKS[b]][:, (i % 4) * P:(i % 4 + 1) * P], uu[:, g, cc * P:(cc + 1) * P], ident)
                    if i % 4 == 3:
                        last.then_inc(uT_ps, 1)

            for p in range(1, PASSES_IN):
                def free_bank(k):
                    if p == 1 and k == 0:
                        pe.wait_ge(part_ev, 8)
                    if p == 1 and k == 2:
                        pe.wait_ge(z_ev, 1)
                    if p >= 2 and k == 0:
                        pe.wait_ge(ev[p - 2], 4)
                    if p == 2 and k == 0:
                        pe.wait_ge(gate_out, 4)
                    if p == 3 and k == 0:
                        pe.wait_ge(uT_ev, 4)
                    if p == 4 and k == 0:
                        pe.wait_ge(gate_out, 8)
                    if k == 3:
                        pe.wait_ge(ev[p - 1], 1)

                def after(u):
                    s = 2 + (p - 1) // 2
                    if u == 0 and p == 1:
                        pe.wait_ge(tap_rdy, 2)
                    if u == 0 and p == 3:
                        pe.wait_ge(seg_out, 1)
                    seg_units(7, [8 * ((p - 1) % 2) + u])
                    if p == 1 and u == 2:
                        pe.wait_ge(ev[0], 4)
                        pe.wait_ge(z_ev, 1)
                        pe.wait_ge(s_wgu, 48)
                        gates(1, GATE_BANKS[1])
                    if p == 2 and u == 1:
                        u_transposed()
                    if p == 3 and u == 1:
                        pe.wait_ge(ev[2], 4)
                        gates(0, GATE_BANKS[0])

                wide_pass([pass_bank(p, i) for i in range(4)], before=free_bank, after=after)

            def half_segment(k):
                seg_units(0, range(4 * k, 4 * k + 4))

            def decays(gi, g):
                if gi == 0:
                    pe.wait_ge(gate_rdy, 4)
                    pe.wait_ge(ev[4], 4)
                    pe.wait_ge(seg_out, 2)
                else:
                    pe.wait_ge(o_rdy, 4)
                    pe.wait_ge(kv_ev, 8)
                for d in range(2):
                    for h in range(HEADS):
                        last = mm(ps[2 + d][:, h * P:(h + 1) * P], gg[:, g, d, h * P:(h + 1) * P], incl[d],
                                  start=True, stop=True)
                    last.then_inc(a_ps, 1)
                for d in range(2):
                    mm(ps[4 + d][:, :], rest[d], gg[:, g, d, :], start=True, stop=True).then_inc(a_ps, 1)
                for i in range(2):
                    for h in range(HEADS):
                        last = tr(ps[6 + i][:, h * P:(h + 1) * P], qk[:, g, i * 512 + h * P:i * 512 + (h + 1) * P], ident)
                    last.then_inc(a_ps, 1)

            def kv(g, chunk, signal):
                for d in range(2):
                    r = slice(HALF * chunk[d], HALF * chunk[d] + HALF)
                    for h in range(HEADS):
                        last = mm(ps[4 + 2 * d + h // 2][:, (h % 2) * DV:(h % 2 + 1) * DV],
                                  kdec[r, d, h * P:(h + 1) * P], vv[r, g, h * DV:(h + 1) * DV], start=True, stop=True)
                        if h % 2:
                            last.then_inc(signal, 1)

            def scores(gi, g):
                pe.wait_ge(a_rdy, 8 * (gi + 1))
                for d in range(2):
                    for h in range(HEADS):
                        last = mm(ps[2 + d][:, h * P:(h + 1) * P], kTt[:, d, h, :], qTt[:, d, h, :],
                                  start=True, stop=True)
                    last.then_inc(at_ps, 1)
                kv(g, (0, 1), kv_ps)

            def outputs(gi, g):
                pe.wait_ge(at_ev, 2 * (gi + 1))
                pe.wait_ge(kv_ev, 8 if gi == 0 else 12)
                if g == 1:
                    pe.wait_ge(s_s0, 16)
                for h in range(HEADS):
                    o = ps[2 + h // 2][:, (h % 2) * DV:(h % 2 + 1) * DV]
                    v = vv[:, g, h * DV:(h + 1) * DV]
                    mm(o, attnT[:, 0, h, :], v, start=True, stop=False)
                    parts = [(0, 1, smid), (1, 0, smid)]
                    if g == 1:
                        parts += [(0, 0, s0), (1, 1, s0)]
                    mm(o, attnT[:, 1, h, :], v, start=False, stop=False)
                    for i, (d, ch, st) in enumerate(parts):
                        r = slice(HALF * ch, HALF * ch + HALF)
                        last = mm(o[r, :], qTt[:, d, h, r], st[:, d, h, :], start=False,
                                  stop=(i >= len(parts) - 2))
                    if h % 2:
                        last.then_inc(o_ps, 1)

            pe.wait_ge(ev[3], 4)
            half_segment(0)
            decays(0, 1)
            half_segment(1)
            scores(0, 1)
            half_segment(2)
            outputs(0, 1)
            half_segment(3)
            decays(1, 0)
            scores(1, 0)
            pe.wait_ge(kv_ev, 12)
            kv(0, (1, 0), kv2_ps)
            outputs(1, 0)
            pe.wait_ge(fin_rdy, 8)
            pe.wait_ge(conv_c, TAPS * CC)
            for i in range(G * CC):
                g, cc = divmod(i, CC)
                last = tr(ps[4 + i // 4][:, (i % 4) * P:(i % 4 + 1) * P], convacc[:, cc, g, :], ident)
                if i % 4 == 3:
                    last.then_inc(back_ps, 1)
            pe.wait_ge(o_rdy, 8)
            pe.wait_ge(back_ev, 2)
            for i in range(G * 8):
                g, kt = divmod(i, 8)
                last = tr(ps[2 + i // 4][:, (i % 4) * P:(i % 4 + 1) * P], vv[:, g, kt * P:(kt + 1) * P], ident)
                if i % 4 == 3:
                    last.then_inc(yT_ps, 1)
            pe.wait_ge(seg_dve, 1)
            for i in range(G * CC):
                g, cc = divmod(i, CC)
                last = tr(ps[(6, 7, 0, 1)[i // 4]][:, (i % 4) * P:(i % 4 + 1) * P], uu[:, g, cc * P:(cc + 1) * P], ident)
                if i % 4 == 3:
                    last.then_inc(cT_ps, 1)

            def broadcast(i, row, g, q):
                if i >= 4:
                    pe.wait_ge(bc_ev, i - 3)
                mm(ps[4 + i % 4][:, :], pick(g, q), row, start=True, stop=True).then_inc(bc_ps, 1)

            pe.wait_ge(yT_ev, 4)
            pe.wait_ge(cT_ev, G * CC)
            pe.wait_ge(seg_add, 1)
            for i in range(8):
                broadcast(i, modrow[:, 0, :], i // 4, i % 4)
            wide_pass([0, 1, 2, 3])
            pe.wait_ge(row2, 1)
            for i in range(16):
                row = (modrow[:, 2, :], modrow[:, 1, :])[i // 8]
                broadcast(8 + i, row, i % 8 // 4, i % 4)
            pe.wait_ge(bc_ev, 24)
            wide_pass([4, 5, 6, 7])

            pe.wait_ge(m_ev, 4)
            seg_units(3, range(0, 8))
            for g in range(G):
                pe.wait_ge(h2_rdy, g + 1)
                for b in range(4):
                    if g:
                        pe.wait_ge((h2T_v, h2T_s)[b % 2], b // 2 + 1)
                    for i in range(4):
                        kt = 4 * b + i
                        last = tr(ps[H2T_BANKS[b]][:, i * P:(i + 1) * P], h2[:, g, kt * P:(kt + 1) * P], ident)
                    last.then_inc(h2T_ps, 1)
                seg_units(3, (range(8, 12), range(14, 16))[g])
                if g == 0:
                    pe.wait_ge(s_wr, 32)
                pe.wait_ge(h2T_v, 2 * (g + 1))
                pe.wait_ge(h2T_s, 2 * (g + 1))
                for kt in range(KT):
                    last = mm(ps[4][:, g * NE:(g + 1) * NE], hT[:, kt, g * P:(g + 1) * P], wr[:, kt, :],
                              start=(kt == 0), stop=(kt == KT - 1))
                last.then_inc(lg_ps, 1)
                if g == 0:
                    seg_units(3, range(12, 14))
            pe.wait_ge(sel_rdy, 1)
            s_g = [rt[:, 8, 0:NE], rt[:, 8, NE:2 * NE]]
            mm(ps[5][:, 0:NE], before, s_g[0], start=True, stop=True)
            mm(ps[5][:, NE:2 * NE], before, s_g[1], start=True, stop=False)
            mm(ps[5][:, NE:2 * NE], ones, s_g[0], start=False, stop=True)
            mm(ps[5][:, 32:48], ones, s_g[0], start=True, stop=False)
            last = mm(ps[5][:, 32:48], ones, s_g[1], start=False, stop=True)
            last.then_inc(rk_ps, 1)

            def unit_in(t, i):
                pe.wait_ge(slot[i % SLOTS], t * 48 + 16 * (PRE_UNITS // SLOTS + i // SLOTS + 1))

            def expert(t, b0):
                pe.wait_ge(st_onehot, t * 2 + 2)
                pe.wait_ge(st_add, t * 8 + 8)
                for kt in range(KT):
                    for g in range(G):
                        last = mm(ps[kt // 4][:, (kt % 4) * P:(kt % 4 + 1) * P],
                                  h2[:, g, kt * P:(kt + 1) * P], sel[:, g, :], start=(g == 0), stop=(g == 1))
                    if kt % 4 == 3:
                        last.then_inc(st_gath, 1)
                pe.wait_ge(st_sel, t + 1)
                pe.wait_ge(bk_y, b0 + 1)
                for g in range(G):
                    last = tr(ps[4][:, g * P:(g + 1) * P], wsel[:, g, :], ident)
                last.then_inc(st_wTp, 1)
                pe.wait_ge(st_xv, t * 2 + 2)
                pe.wait_ge(st_xa, t * 2 + 2)
                pe.wait_ge(st_wN, t + 1)

            def combine(t, b0):
                pe.wait_ge(bk_yf, b0 * 64 + 64)
                pe.wait_ge(st_wT, t + 1)
                for j in range(8):
                    g, q = divmod(j, 4)
                    if g:
                        pe.wait_ge(st_add, t * 8 + (q + 9))
                    mm(ps[q][:, :], wselT[:, g, :], yf[:, q * BANK:(q + 1) * BANK], start=True, stop=True).then_inc(st_cmb, 1)

            def blocks(t, b0, v):
                for i in range(16):
                    unit_in(t, i)
                    for k in range(2):
                        kt = 2 * (i // 2) + k
                        for b in range(v):
                            for q in range(4):
                                last = mm(ps[b][seg_slice(q), (i % 2) * 256:(i % 2 + 1) * 256], XT[:, kt, b * BLK:(b + 1) * BLK],
                                          ring[:, i % SLOTS, k * 1024 + q * 256:k * 1024 + (q + 1) * 256],
                                          start=(i == 0 and k == 0), stop=(kt == KT - 1), skip_group_check=True)
                    last.then_inc(used, 1)
                for b in range(v):
                    pe.wait_ge(bk_h, b0 + (b + 1))
                    for j in range(2):
                        last = tr(ps[4 + b][:, j * P:(j + 1) * P], hh[:, b % 2, j * P:(j + 1) * P], ident)
                    last.then_inc(bk_hTp, 1)
                combine(t, b0)
                pe.wait_ge(bk_hT, b0 + v)
                for i in range(FT):
                    unit_in(t, 16 + i)
                    for b in range(v):
                        lhsT = hTm[:, b, i % 2, BLK * (i // 2):BLK * (i // 2 + 1)]
                        for q in range(4):
                            last = mm(ps[4 + b][seg_slice(q), :], lhsT, ring[:, i, q * BANK:(q + 1) * BANK],
                                      start=(i == 0), stop=(i == FT - 1))
                    last.then_inc(used, 1)
            pe.wait_ge(seg_dve, 2)
            for_steps(pe, expert, blocks)
            tl = pe.value_load(steps[0:1, 4, 0:1], min_val=NE, max_val=NSTEP)
            bl = pe.value_load(steps[0:1, 4, 1:2], min_val=NE, max_val=NBLK * NSTEP)
            pe.wait_ge(st_add, tl * 8 + 8)
            combine(tl, bl)

            for g in range(G):
                for q in range(NQ):
                    if g:
                        pe.wait_ge(t_mul, q + 1)
                    mm(ps[4 + q][:, :], pick(g, q), modrow[:, 3, :], start=True, stop=True).then_inc(t_bc, 1)

        @block.vector
        def _(dve):
            n = 0
            v = nc.vector

            def link(ins):
                nonlocal n
                n += 1
                ins.then_inc(dch, 1)
                dve.wait_ge(dch, n)

            link(v.memset(small[:, 63:64], EPS))
            dve.wait_ge(s_zero, 1)
            dve.wait_ge(rows_ps, 1)
            v.tensor_copy(condT[:, :, 0:2].rearrange("p k c -> p c k"),
                          ps[6][:, 0:32].rearrange("p (c k) -> p c k", c=2)).then_inc(cond_rdy, 1)
            v.tensor_copy(gcol[:, :, :], ps[6][:, 32:56].rearrange("p (a c) -> p a c", a=3)).then_inc(tap_rdy, 1)
            v.tensor_copy(bcol[:, 0], ps[6][:, 56:72].rearrange("p (a c) -> p a c", a=NQ))
            v.tensor_scalar(bcol[:, 1], ps[6][:, 72:88].rearrange("p (a c) -> p a c", a=NQ),
                            1.0, None, ALU.add).then_inc(bcol_rdy, 1)
            dve.wait_ge(bcol_rdy, 1)
            dve.wait_ge(tap_ps, 1)
            v.tensor_copy(tapT[:, :, :], ps[7][:, 0:256].rearrange("p (c k) -> p c k", c=CC)).then_inc(tap_rdy, 1)

            def parts_out(qb):
                if qb:
                    dve.wait_ge(col_ps, qb)
                for s in range(2):
                    dve.wait_ge(used, (10 * qb - 2 if qb else 0) + 4 * (s + 1))
                    v.tensor_copy(modpart[:, s, :], ps[4 + s][:, :]).then_inc(part_ev, 1)

            parts_out(0)
            for b in range(8):
                g = b // 4
                if b == 4:
                    dve.wait_ge(s_x[1], 32)
                    v.tensor_tensor(xres[:, 1, :], xres[:, 1, :], posb, ALU.add).then_inc(xpos, 1)
                dve.wait_ge(xT_ps, b + 1)
                v.tensor_copy(hT[:, 4 * (b % 4):4 * (b % 4) + 4, g * P:(g + 1) * P],
                              ps[b % 4][:, :].rearrange("p (k t) -> p k t", k=4)).then_inc(xT_ev, 1)
            dve.wait_ge(xT_ev, 8)
            for qb in range(NQ):
                if qb:
                    parts_out(qb)
                dve.wait_ge(col_ps, qb + 1)
                v.tensor_tensor(modcol[:, :, qb], ps[6][:, 0:16].rearrange("p (s j c) -> p s j c", s=2, j=NQ),
                                bcol[:, :, qb].unsqueeze(3).broadcast_to([P, 2, NQ, G]), ALU.add).then_inc(col_rdy, 1)
                dve.wait_ge(col_rdy, qb + 1)
                for j in range(NQ):
                    kt = NQ * qb + j
                    v.tensor_scalar(hT[:, kt, 0:P], hT[:, kt, 0:P], modcol[:, 1, qb, j, 0:1], modcol[:, 0, qb, j, 0:1],
                                    ALU.mult, ALU.add).then_inc(h_dve, 1)
            dve.wait_ge(used, pass_end(1))
            dve.wait_ge(xpos, 1)
            for i in range(4):
                g, hf = divmod(i, 2)
                dve.wait_ge(ev[0], i + 1)
                cs = slice(hf * BANK, (hf + 1) * BANK)
                v.tensor_tensor(uu[:, g, cs], ps[pass_bank(1, i)][:, :], sig[:, g, cs], ALU.mult).then_inc(ev[1], 1)
            for i in range(4):
                g = i // 2
                dve.wait_ge(uT_ps, i + 1)
                v.tensor_copy(uT[:, 4 * (i % 2):4 * (i % 2) + 4, g, PAD:PAD + P],
                              ps[U_BANKS[i]][:, :].rearrange("p (c t) -> p c t", c=4)).then_inc(uT_ev, 1)
            dve.wait_ge(uT_ev, 4)
            done = 0
            for c0 in range(0, CC, 2):
                for k in range(TAPS):
                    for cc in (c0, c0 + 1):
                        src = uT[:, cc, :, k:k + P]
                        if k == 0:
                            last = v.tensor_scalar(convacc[:, cc], src, tapT[:, cc, 0:1], tapT[:, cc, TAPS:TAPS + 1],
                                                   ALU.mult, ALU.add)
                        else:
                            dve.wait_ge(conv_c, done - 1)
                            last = v.scalar_tensor_tensor(convacc[:, cc], src, tapT[:, cc, k:k + 1], convacc[:, cc],
                                                          ALU.mult, ALU.add)
                        last.then_inc(conv_c, 1)
                        done += 1

            def gla(gi, g):
                for d in range(2):
                    dve.wait_ge(a_exp, 6 * gi + 3 * d + 1)
                    cols = (63, 127) if d == 0 else (0, 64)
                    for ch in range(2):
                        link(v.tensor_copy(decay[:, d, ch, :], qTt[:, d, :, cols[ch]]))
                    dve.wait_ge(a_ps, 6 * gi + 5)
                    v.scalar_tensor_tensor(qTt[:, d], ps[6][:, :].rearrange("p (h t) -> p h t", h=HEADS), QSCALE,
                                           qTt[:, d], ALU.mult, ALU.mult).then_inc(a_rdy, 1)
                    dve.wait_ge(a_exp, 6 * gi + 3 * d + 2)
                    dve.wait_ge(a_ps, 6 * gi + 6)
                    v.tensor_tensor(kTt[:, d], ps[7][:, :].rearrange("p (h t) -> p h t", h=HEADS), kTt[:, d],
                                    ALU.mult).then_inc(a_rdy, 1)
                    dve.wait_ge(a_exp, 6 * gi + 3 * d + 3)
                    v.tensor_tensor(kdec[:, d, :], qk[:, g, 512:1024], kdec[:, d, :], ALU.mult).then_inc(a_rdy, 2)
                for d in range(2):
                    dve.wait_ge(at_ps, 2 * gi + d + 1)
                    v.copy_predicated(attnT[:, d], incl[d].bitcast(U32).unsqueeze(1).broadcast_to([P, HEADS, P]),
                                      ps[2 + d][:, :].rearrange("p (h t) -> p h t", h=HEADS)).then_inc(at_ev, 1)
                if g == 1:
                    dve.wait_ge(s_s0, 16)
                    for i in range(8):
                        d, h = divmod(i, HEADS)
                        dve.wait_ge(kv_ps, i // 2 + 1)
                        v.scalar_tensor_tensor(smid[:, d, h, :], s0[:, d, h, :], decay[:, d, d, h:h + 1],
                                               ps[4 + i // 2][:, (i % 2) * DV:(i % 2 + 1) * DV],
                                               ALU.mult, ALU.add).then_inc(kv_ev, 1)
                else:
                    dve.wait_ge(kv_ev, 12)
                    for i in range(8):
                        d, h = divmod(i, HEADS)
                        dve.wait_ge(kv2_ps, i // 2 + 1)
                        v.scalar_tensor_tensor(s0[:, d, h, :], smid[:, d, h, :], decay[:, d, 1 - d, h:h + 1],
                                               ps[4 + i // 2][:, (i % 2) * DV:(i % 2 + 1) * DV],
                                               ALU.mult, ALU.add).then_inc(fin_rdy, 1)
                dve.wait_ge(o_sq, gi + 1)
                link(v.reciprocal(small[:, 20 + 4 * g:24 + 4 * g], small[:, 16 + 4 * g:20 + 4 * g]))
                for h in range(HEADS):
                    v.scalar_tensor_tensor(vv[:, g, h * DV:(h + 1) * DV], ps[2 + h // 2][:, (h % 2) * DV:(h % 2 + 1) * DV],
                                           small[:, 20 + 4 * g + h:21 + 4 * g + h], rs[:, g, h * DV:(h + 1) * DV],
                                           ALU.mult, ALU.mult).then_inc(o_rdy, 1)

            def segment_in(s, bank, units):
                dve.wait_ge(used, units)
                v.tensor_tensor(modrow[:, s - 2, :], ps[bank][:, :], modrow[:, s - 2, :], ALU.add).then_inc(seg_dve, 1)

            dve.wait_ge(ev[4], 4)
            gla(0, 1)
            dve.wait_ge(s_bmod, 32)
            segment_in(4, 0, pass_end(4) + 1 + SEG_UNITS)
            gla(1, 0)
            for i in range(4):
                g, b = divmod(i, 2)
                dve.wait_ge(back_ps, i + 1)
                link(v.bn_stats(stats[:, g, b, :], ps[4 + i][:, :]))
            for g in range(G):
                link(v.bn_aggr(small[:, 50 + 2 * g:52 + 2 * g], stats[:, g, 0:2, :]))
            v.tensor_copy(small[:, 28:30], small[:, 51:54:2]).then_inc(back_var, 1)
            dve.wait_ge(o_sq, 3)
            link(v.reciprocal(small[:, 34:36], small[:, 32:34]))
            for g in range(G):
                for b in range(2):
                    last = v.tensor_scalar(uu[:, g, b * BANK:(b + 1) * BANK], ps[4 + 2 * g + b][:, :],
                                           small[:, 50 + 2 * g:51 + 2 * g], small[:, 34 + g:35 + g],
                                           ALU.subtract, ALU.mult)
                last.then_inc(back_ev, 1)
            for i in range(4):
                g, b = divmod(i, 2)
                dve.wait_ge(yT_ps, i + 1)
                v.tensor_tensor(hT[:, 4 * b:4 * b + 4, g * P:(g + 1) * P],
                                ps[2 + i][:, :].rearrange("p (k t) -> p k t", k=4),
                                gcol[:, 0, 4 * b:4 * b + 4].unsqueeze(2).broadcast_to([P, 4, P]), ALU.mult).then_inc(yT_ev, 1)
            dve.wait_ge(s_ln, 64)
            dve.wait_ge(seg_dve, 1)
            dve.wait_ge(seg_add, 2)
            link(v.scalar_tensor_tensor(lnrow[:, 1, :], modrow[:, 2, :], 1.0, lnrow[:, 1, :], ALU.add, ALU.mult))
            link(v.scalar_tensor_tensor(modrow[:, 2, :], modrow[:, 2, :], 1.0, lnrow[:, 0, :], ALU.add, ALU.mult))
            v.tensor_tensor(modrow[:, 1, :], modrow[:, 1, :], lnrow[:, 1, :], ALU.add).then_inc(row2, 1)

            dve.wait_ge(bc_ev, 8)
            for p in range(2):
                dve.wait_ge(used, PRE_UNITS - SEG_UNITS + (p - 1) * PASS_UNITS)
                for g in range(G):
                    for hf in range(2):
                        q = 2 * p + hf
                        cs = slice(q * BANK, (q + 1) * BANK)
                        ins = v.tensor_tensor(g1b[:, g, cs], ps[4 * p + 2 * g + hf][:, :], g1b[:, g, cs], ALU.mult)
                        ins.then_inc(m_ev, 1)
                        dve.wait_ge(m_ev, 4 * p + 2 * g + hf + 1)
                        link(v.scalar_tensor_tensor(xres[:, g, cs], xres[:, g, cs], ALPHA, g1b[:, g, cs], ALU.mult, ALU.add))
                        v.bn_stats(stats[:, g, q, :], xres[:, g, cs]).then_inc(dch, 1)
                        n += 1
            dve.wait_ge(dch, n)
            for g in range(G):
                v.bn_aggr(small[:, 36 + 2 * g:38 + 2 * g], stats[:, g, :, :]).then_inc(ln_v, 1)
            for g in range(G):
                dve.wait_ge(ln_s, g + 1)
                link(v.reciprocal(small[:, 42 + g:43 + g], small[:, 40 + g:41 + g]))
                if g == 0:
                    dve.wait_ge(bc_ev, 24)
                link(v.scalar_tensor_tensor(h2[:, g, :], xres[:, g, :], small[:, 36 + 2 * g:37 + 2 * g],
                                            G2b[:, g, :], ALU.subtract, ALU.mult))
                v.scalar_tensor_tensor(h2[:, g, :], h2[:, g, :], small[:, 42 + g:43 + g], B2b[:, g, :],
                                       ALU.mult, ALU.add).then_inc(h2_rdy, 1)
                for b in range(2):
                    dve.wait_ge(h2T_ps, 4 * g + 2 * b + 1)
                    v.tensor_copy(hT[:, 8 * b:8 * b + 4, g * P:(g + 1) * P],
                                  ps[H2T_BANKS[2 * b]][:, :].rearrange("p (k t) -> p k t", k=4)).then_inc(h2T_v, 1)
            for g in range(G):
                v.tensor_scalar(xres[:, g, :], xres[:, g, :], small[:, 36 + 2 * g:37 + 2 * g],
                                small[:, 42 + g:43 + g], ALU.subtract, ALU.mult).then_inc(xn_rdy, 1)
            v.memset(acc, 0.0).then_inc(st_add, 8)
            v.memset(wselT, 0.0).then_inc(st_wT, 1)
            dve.wait_ge(h2_rdy, 2)
            v.memset(ye, 0.0).then_inc(bk_y, 1)
            segment_in(5, 3, PRE_UNITS)

            N8 = G * NGRP
            f = lambda i: rt[:, i, 0:32]
            f3 = lambda i: rt[:, i, 0:32].rearrange("p (a b) -> p a b", b=PER)
            f8 = lambda i: rt[:, 13, 8 * i:8 * i + 8]
            b4 = lambda a: a.unsqueeze(2).broadcast_to([P, a.shape[1], PER])
            bN = lambda a: a.unsqueeze(2).broadcast_to([P, G, NE])
            g16 = lambda i: rt[:, i, 0:32].rearrange("p (g e) -> p g e", g=G)
            dve.wait_ge(s_wr, 32)
            dve.wait_ge(lg_ps, 2)
            link(v.tensor_tensor(g16(0), ps[4][:, 0:32].rearrange("p (g e) -> p g e", g=G),
                                 br[:, :].unsqueeze(1).broadcast_to([P, G, NE]), ALU.add))
            link(v.tensor_reduce(small[:, 24:26], g16(0), AX.X, ALU.max))
            v.tensor_scalar(small[:, 44:46], small[:, 24:26], -1.0, None, ALU.mult).then_inc(lmax, 1)
            dve.wait_ge(lexp, 2)
            link(v.reciprocal(small[:, 54:56], small[:, 48:50]))
            link(v.tensor_tensor(g16(2), g16(1), bN(small[:, 54:56]), ALU.mult))

            def best(src, mx, key, hot):
                link(v.tensor_reduce(mx, src, AX.X, ALU.max))
                link(v.tensor_tensor(key, src, b4(mx), ALU.is_equal))
                link(v.tensor_tensor(key, key, key4[:, 0:4 * mx.shape[1]].rearrange("p (a b) -> p a b", b=PER), ALU.mult))
                link(v.tensor_reduce(f8(3)[:, 0:mx.shape[1]], key, AX.X, ALU.max))
                link(v.tensor_tensor(hot, key, b4(f8(3)[:, 0:mx.shape[1]]), ALU.is_equal))

            best(f3(2), f8(0), f3(3), f3(4))
            link(v.scalar_tensor_tensor(f(5), f(4), -4.0, f(2), ALU.mult, ALU.add))
            best(f3(5), f8(1), f3(3), f3(6))
            link(v.tensor_tensor(f8(0), f8(0), f8(1), ALU.add))
            grp = rt[:, 7, 0:8]
            best(f8(0).rearrange("p (a b) -> p a b", b=NGRP), small[:, 24:26],
                 rt[:, 3, 0:8].rearrange("p (a b) -> p a b", b=NGRP), grp.rearrange("p (a b) -> p a b", b=NGRP))
            link(v.tensor_tensor(f(4), f(4), f(6), ALU.add))
            v.tensor_tensor(f3(8), f3(4), b4(grp), ALU.mult).then_inc(sel_rdy, 1)
            dve.wait_ge(sel_rdy, 1)
            link(v.tensor_tensor(f(5), f(8), f(2), ALU.mult))
            link(v.tensor_reduce(small[:, 24:26], g16(5), AX.X, ALU.add))
            link(v.reciprocal(small[:, 26:28], small[:, 24:26]))
            link(v.tensor_tensor(g16(5), g16(5), bN(small[:, 26:28]), ALU.mult))
            dve.wait_ge(rk_ps, 1)
            link(v.scalar_tensor_tensor(f(7), ps[5][:, 0:32], 1.0, f(8), ALU.add, ALU.mult))
            link(v.tensor_scalar(f(7), f(7), -1.0, None, ALU.add))
            r20 = lambda i: extra[:, i, 0:NSTEP + 1]
            ex = lambda i: extra[:, i, :].rearrange("p (j e) -> p j e", j=MAX_EXTRA)
            exs = lambda i: extra[:, i, 0:MAX_EXTRA]
            jn = lambda a: a.unsqueeze(1).broadcast_to([P, MAX_EXTRA, NE])
            jrow = const[:, C_J:C_J + NE * MAX_EXTRA].rearrange("p (j e) -> p j e", j=MAX_EXTRA)
            cnt, ov = rt[:, 9, 0:NE], rt[:, 9, NE:2 * NE]
            link(v.tensor_copy(cnt, ps[5][:, 32:48]))

            def block_count(dst, src, base):
                link(v.tensor_scalar(dst, src, base + BLK + 0.5, 1.0, ALU.is_gt, ALU.add))
                for k in range(2, NBLK):
                    link(v.scalar_tensor_tensor(dst, src, base + k * BLK + 0.5, dst, ALU.is_gt, ALU.add))

            def prefix(a, b, width):
                sh = 1
                while sh < width:
                    link(v.tensor_copy(rt[:, b, 0:sh], rt[:, a, 0:sh]))
                    link(v.tensor_tensor(rt[:, b, sh:width], rt[:, a, sh:width], rt[:, a, 0:width - sh], ALU.add))
                    a, b, sh = b, a, 2 * sh
                return a

            link(v.memset(rt[:, 10, :], 0.0))
            block_count(rt[:, 10, 0:NE], cnt, 0.0)
            link(v.tensor_scalar(ov, cnt, CAP + 0.5, None, ALU.is_gt))
            link(v.tensor_copy(rt[:, 11, 0:NE], ov))
            cum = rt[:, prefix(11, 12, NE), 0:NE]
            link(v.tensor_tensor(ex(0), jn(cum), jrow, ALU.is_le))
            link(v.tensor_reduce(exs(1), ex(0), AX.X, ALU.add))
            link(v.tensor_tensor(ex(2), jn(iota[:, 0:NE]), exs(1).unsqueeze(2).broadcast_to([P, MAX_EXTRA, NE]),
                                 ALU.is_equal))
            link(v.tensor_tensor(ex(2), ex(2), jn(cnt), ALU.mult))
            link(v.tensor_reduce(exs(3), ex(2), AX.X, ALU.add))
            block_count(rt[:, 10, NE:NSTEP], exs(3), float(CAP))
            link(v.tensor_copy(steps[:, 1, :], rt[:, 10, 0:NSTEP + 1]))
            link(v.tensor_copy(exs(7), rt[:, 10, NE:NSTEP]))
            blocks_to = rt[:, prefix(10, 11, NSTEP), 0:NSTEP]
            link(v.memset(steps[:, 2, 0:1], 0))
            link(v.tensor_copy(steps[:, 2, 1:NSTEP + 1], blocks_to))
            link(v.tensor_copy(steps[:, 0, :], const[:, C_EXP:C_EXP + NSTEP + 1]))
            link(v.tensor_scalar(steps[:, 0, NE:NSTEP], exs(1), NE - 1.0, None, ALU.min))
            link(v.tensor_scalar(exs(5), exs(1), NE - 0.5, None, ALU.is_lt))
            link(v.tensor_reduce(extra[:, 6, 0:1], exs(5), AX.X, ALU.add))
            link(v.tensor_scalar(steps[:, 4, 0:1], extra[:, 6, 0:1], float(NE), None, ALU.add))
            link(v.tensor_tensor(exs(5), exs(5), exs(7), ALU.mult))
            link(v.tensor_reduce(extra[:, 6, 1:2], exs(5), AX.X, ALU.add))
            link(v.tensor_tensor(steps[:, 4, 1:2], extra[:, 6, 1:2], blocks_to[:, NE - 1:NE], ALU.add))
            link(v.memset(steps[:, 3, :], 1))
            v.tensor_scalar(steps[:, 3, NE:NSTEP], exs(1), NE - 0.5, None, ALU.is_lt).then_inc(tab_rdy, 1)
            dve.wait_ge(tab_rdy, 1)

            def select(t, e):
                for g in range(G):
                    v.tensor_scalar(sel[:, g, :], iota, const[:, bass.ds(t + C_OFF, 1)],
                                    rt[:, 7, bass.ds(e + g * NE, 1)], ALU.add, ALU.is_equal).then_inc(st_onehot, 1)
                dve.wait_ge(st_onehot, t * 2 + 2)
                for g in range(G):
                    last = v.tensor_scalar(wsel[:, g, :], sel[:, g, :], rt[:, 5, bass.ds(e + g * NE, 1)], None, ALU.mult)
                last.then_inc(st_sel, 1)

            def expert(t, b0):
                for i in (0, 2):
                    dve.wait_ge(st_gath, t * 4 + (i + 1))
                    v.tensor_copy(XT[:, 4 * i:4 * i + 4, :],
                                  ps[i][:, :].rearrange("p (k s) -> p k s", k=4)).then_inc(st_xv, 1)
                dve.wait_ge(st_wTp, t + 1)
                nxt = dve.value_load(steps[0:1, 0, bass.ds(t + 1, 1)], min_val=0, max_val=NE - 1)
                select(t + 1, nxt)

            def blocks(t, b0, nb):
                for b in range(nb):
                    dve.wait_ge(bk_hs, b0 + (b + 1))
                    if b >= 2:
                        dve.wait_ge(bk_hTp, b0 + (b - 1))
                    v.tensor_tensor(hh[:, b % 2, :], hs[:, b % 2, :], ps[b][:, 256:512], ALU.mult).then_inc(bk_h, 1)
                    if b >= 1:
                        hT_out(b0, b - 1)
                hT_out(b0, nb - 1)
                add(t)

            def add(t):
                for j in range(8):
                    g, q = divmod(j, 4)
                    cs = slice(q * BANK, (q + 1) * BANK)
                    dve.wait_ge(st_cmb, t * 8 + (j + 1))
                    v.tensor_tensor(acc[:, g, cs], ps[q][:, :], acc[:, g, cs], ALU.add).then_inc(st_add, 1)

            def hT_out(b0, b):
                dve.wait_ge(bk_hTp, b0 + (b + 1))
                v.tensor_copy(hTm[:, b], ps[4 + b][:, 0:256].rearrange("p (j t) -> p j t", j=2)).then_inc(bk_hT, 1)

            select(0, 0)
            v.memset(yf, 0.0).then_inc(bk_yf, 64)
            for_steps(dve, expert, blocks)
            add(dve.value_load(steps[0:1, 4, 0:1], min_val=NE, max_val=NSTEP))

            dve.wait_ge(x1_rdy, 2)
            for g in range(G):
                for q in range(NQ):
                    cs = slice(q * BANK, (q + 1) * BANK)
                    dve.wait_ge(t_bc, 4 * g + q + 1)
                    v.tensor_tensor(acc[:, g, cs], ps[4 + q][:, :], acc[:, g, cs], ALU.mult).then_inc(t_mul, 1)
                    dve.wait_ge(t_mul, 4 * g + q + 1)
                    link(v.scalar_tensor_tensor(acc[:, g, cs], xres[:, g, cs], ALPHA, acc[:, g, cs], ALU.mult, ALU.add))
                    link(v.bn_stats(stats[:, g, q, :], acc[:, g, cs]))
                v.bn_aggr(small[:, 36 + 2 * g:38 + 2 * g], stats[:, g, :, :]).then_inc(t_var, 1)
                dve.wait_ge(t_sd, g + 1)
                link(v.reciprocal(small[:, 42 + g:43 + g], small[:, 40 + g:41 + g]))
                v.tensor_scalar(acc[:, g, :], acc[:, g, :], small[:, 36 + 2 * g:37 + 2 * g],
                                small[:, 42 + g:43 + g], ALU.subtract, ALU.mult).then_inc(t_nrm, 1)
            for g in range(G):
                dve.wait_ge(t_gain, g + 1)
                v.tensor_tensor(acc[:, g, :], acc[:, g, :], lnb, ALU.add).then_inc(t_out, 1)


_INS = ['x_prompt', 'x_sample', 'state_gla', 'c', 'c_ctx', 'w_mod', 'b_mod', 'w_in', 'w_gate_up', 'b_gate',
        'gla_norm_g', 'w_dw', 'b_dw', 'conv_ln_g', 'conv_ln_b', 'w_out', 'ln1_g', 'ln1_b', 'ln2_g', 'ln2_b',
        'w_router', 'b_router', 'w_e_gate', 'w_e_up', 'w_e_down']
_OUTS = [((1, 128, 2048), 'float32'), ((1, 128, 2048), 'float32'), ((1, 1, 2, 4, 128, 256), 'float32')]


def _constants():
    import numpy as np
    t = np.zeros((P, C_END), np.float32)
    s, m = np.arange(P)[:, None], np.arange(P)[None, :]
    same = s // HALF == m // HALF
    t[:, C_ID:C_ID + P] = s == m
    t[:, C_INCF:C_INCF + P] = np.where(same & (s <= m), -1 / TAU, 0.0)
    t[:, C_RESTF:C_RESTF + P] = np.where(same & (s > m), -1 / TAU, 0.0)
    t[:, C_INCB:C_INCB + P] = np.where(same & (s >= m), -1 / TAU, 0.0)
    t[:, C_RESTB:C_RESTB + P] = np.where(same & (s < m), -1 / TAU, 0.0)
    t[:, C_BEFORE:C_BEFORE + P] = s < m
    t[:, C_ONES:C_ONES + P] = 1.0
    t[:, C_IOTA:C_IOTA + P] = m
    for q in range(NQ):
        for g in range(G):
            t[32 * q + g, C_SEL + (2 * q + g) * P:C_SEL + (2 * q + g + 1) * P] = 1.0
            t[32 * q + g, C_SUM + g] = 1.0
    t[:, C_KEY:C_KEY + 32] = np.tile([4, 3, 2, 1], 8)
    t[:, C_J:C_J + NE * MAX_EXTRA] = np.repeat(np.arange(MAX_EXTRA), NE)
    t[:, C_EXP:C_OFF] = np.minimum(np.arange(NSTEP + 1), NE - 1)
    t[:, C_OFF:C_END] = CAP * (np.arange(NSTEP + 1) >= NE)
    nf = D // 4
    omega = np.float32(1.0) / np.power(np.float32(10000.0), np.arange(nf, dtype=np.float32) / np.float32(nf))
    tok = np.arange(P)
    pr = (tok // 64).astype(np.float32)[:, None] * omega
    pc = (tok % 64).astype(np.float32)[:, None] * omega
    pos = np.concatenate([np.sin(pr), np.cos(pr), np.sin(pc), np.cos(pc)], axis=-1).astype(np.float32)
    return t, pos


def kernel(**inputs):
    import numpy as _np
    import concourse.bacc as _bacc
    from concourse import mybir as _mybir
    from concourse.bass_utils import run_bass_kernel_spmd as _run

    nc = _bacc.Bacc("TRN2", target_bir_lowering=False, num_devices=1)
    arrays, args = {}, []
    table, pos = _constants()
    for name, a in [(n, inputs[n]) for n in _INS] + [("table", table), ("pos", pos)]:
        a = _np.ascontiguousarray(a)
        arrays[f"in_{name}_dram"] = a
        args.append(nc.dram_tensor(f"in_{name}_dram", a.shape, _mybir.dt.from_np(a.dtype), kind="ExternalInput").ap())
    for i, (shape, dtype) in enumerate(_OUTS):
        dt = _mybir.dt.from_np(_np.dtype(dtype))
        args.append(nc.dram_tensor(f"out_{i}_dram", shape, dt, kind="ExternalOutput").ap())
    hybrid_step(nc, *args)
    r = _run(nc, [arrays], core_ids=[0])
    return tuple(r.results[0][f"out_{i}_dram"] for i in range(len(_OUTS)))
```

```python
from contextlib import ExitStack

import concourse.bass as bass
from concourse import mybir

ALU = mybir.AluOpType
ACT = mybir.ActivationFunctionType
F32 = mybir.dt.float32
I32 = mybir.dt.int32
U32 = mybir.dt.uint32
AX = mybir.AxisListType

P = 128
G = 2
D = 2048
KT = D // P
BANK = 512
NQ = D // BANK
HEADS, DK, DV = 4, 128, 256
HALF = 64
CAP = 128
BLK = 32
NBLK = CAP // BLK
CONV_W = 1024
CC = CONV_W // P
TAPS, PAD = 31, 15
RANK = 16
NE, NGRP, PER = 16, 4, 4
FF = 1024
FT = FF // P
EPS = 1e-5
ALPHA = 2.0 ** 0.25
TAU = 16.0
QSCALE = DK ** -0.5

SLOTS = 8
UNIT = 2048
SEG_UNITS = KT
PASS_UNITS = 8
PASSES_IN = 5
PASS_COL = (4128, 3104, 0, 1024, 2048)
Z_COL = 3072
GATE_BANKS = {1: (1, 2), 0: (2, 3)}
U_BANKS = (5, 6, 0, 5)
BACK_BANKS = ((6, 0), (1, 6))
H2T_BANKS = (0, 1, 2, 7)
STEP_UNITS = 24
PRE_UNITS = 6 * SEG_UNITS + (PASSES_IN + 2) * PASS_UNITS
MAX_EXTRA = G * P * 2 // (CAP + 1)
NSTEP = NE + MAX_EXTRA

C_ID, C_INCF, C_RESTF, C_INCB, C_RESTB, C_BEFORE, C_ONES, C_IOTA, C_SEL = [P * i for i in range(9)]
C_SUM = C_SEL + 8 * P
C_KEY = C_SUM + 2
C_J = C_KEY + 32
C_EXP = C_J + 16 * MAX_EXTRA
C_OFF = C_EXP + NSTEP + 1
C_END = C_OFF + NSTEP + 1


def hybrid_step(nc, x_prompt, x_sample, state_gla, c, c_ctx, w_mod, b_mod, w_in, w_gate_up, b_gate,
                gla_norm_g, w_dw, b_dw, conv_ln_g, conv_ln_b, w_out, ln1_g, ln1_b, ln2_g, ln2_b,
                w_router, b_router, w_e_gate, w_e_up, w_e_down, table, pos,
                y_prompt, y_sample, new_state):
    with ExitStack() as ctx:
        def sb(name, shape, dt=F32):
            return ctx.enter_context(nc.sbuf_tensor(name, shape, dt))

        def sem(name):
            return ctx.enter_context(nc.semaphore(name))

        ps = [ctx.enter_context(nc.psum_tensor(f"bank{i}", [P, BANK], F32)) for i in range(8)]

        ring = sb("ring", [P, SLOTS, UNIT])
        xres = sb("xres", [P, G, D])
        hT = sb("hT", [P, KT, G * P])
        arena = sb("arena", [P, 5 * 2048])
        work = sb("work", [P, 10720])
        const = sb("const", [P, C_END])
        modrow = sb("modrow", [P, 4, BANK])
        lnrow = sb("lnrow", [P, 2, BANK])
        condT = sb("condT", [P, KT, 32])
        gcol = sb("gcol", [P, 3, CC])
        tapT = sb("tapT", [P, CC, 32])
        wr = sb("wr", [P, KT, NE])
        br = sb("br", [P, NE])
        bcol = sb("bcol", [P, 2, NQ, NQ])
        modcol = sb("modcol", [P, 2, NQ, NQ, 2])
        decay = sb("decay", [P, 2, 2, HEADS])
        small = sb("small", [P, 64])
        stats = sb("stats", [P, G, NQ, 6])
        rt = sb("rt", [P, 14, 32])
        extra = sb("extra", [P, 10, NE * MAX_EXTRA])
        steps = sb("steps", [P, 5, NSTEP + 1], I32)

        def part(t, at, *dims):
            n = 1
            for d in dims:
                n *= d
            v = t[:, at:at + n]
            if len(dims) == 2:
                return v.rearrange("p (a b) -> p a b", a=dims[0])
            if len(dims) == 3:
                return v.rearrange("p (a b c) -> p a b c", a=dims[0], b=dims[1])
            return v

        qk = part(arena, 0, G, 1024)
        vv = part(arena, 2048, G, 1024)
        rs = part(arena, 4096, G, 1024)
        uu = part(arena, 6144, G, 1024)
        convacc = part(arena, 6144, CC, G, P)
        cn = part(work, 4096, G, 1024)
        gg = part(arena, 8192, G, 2, BANK)
        wz = part(arena, 0, KT, 32)
        zT = part(arena, 2048, 256)
        wgu = part(arena, 5120, 2, BANK)
        taprow = part(arena, 4096, 1024)
        posb = part(arena, 6144, D)
        rows = arena[0:88, 8192:8192 + P]
        h2 = part(arena, 0, G, D)
        acc = part(arena, 4096, G, D)
        g2b = part(arena, 0, G, D)
        g1b = part(arena, 4096, G, D)
        wsel = part(arena, 8192, G, CAP)
        wselT = part(arena, 8448, G, P)
        hTm = part(arena, 8704, NBLK, 2, P)
        hTf = part(arena, 8704, FT, P)
        wselN = part(arena, 9728, G, P)
        kTt = part(work, 0, 2, HEADS, P)
        kdec = part(work, 1024, 2, BANK)
        attnT = part(work, 2048, 2, HEADS, P)
        qTt = part(work, 3072, 2, HEADS, P)
        smid = part(work, 4096, 2, HEADS, DV)
        sig = part(work, 4096, G, 1024)
        s0 = part(work, 6144, 2, HEADS, DV)
        UW = P + 2 * PAD
        uT = part(work, 8192, CC, G, UW)
        modpart = part(work, 0, 2, BANK)
        grelu = part(work, 0, 2, BANK)
        segrow = part(work, 3072, BANK)
        G2b = part(work, 0, G, D)
        B2b = part(work, 4096, G, D)
        XT = part(work, 0, KT, CAP)
        ye = part(work, 2048, NBLK, BANK)
        hs = part(work, 8704, 2, 256)
        hh = part(work, 9216, 2, 256)
        hs1, hh1 = part(work, 8704, BANK), part(work, 9216, BANK)
        sel = part(work, 9728, G, CAP)
        yf = part(hT[:, :, :].rearrange("p k t -> p (k t)"), 0, D)
        lng = part(work, 4096, D)
        lnb = part(work, 6144, D)
        junk = part(work, 8192, BANK)

        ident = const[:, C_ID:C_ID + P]
        incl = [const[:, C_INCF:C_INCF + P], const[:, C_INCB:C_INCB + P]]
        rest = [const[:, C_RESTF:C_RESTF + P], const[:, C_RESTB:C_RESTB + P]]
        before = const[:, C_BEFORE:C_BEFORE + P]
        ones = const[:, C_ONES:C_ONES + P]
        iota = const[:, C_IOTA:C_IOTA + P]
        pick = lambda g, q: const[:, C_SEL + (2 * q + g) * P:C_SEL + (2 * q + g + 1) * P]
        key4 = const[:, C_KEY:C_KEY + 32]

        slot = [sem(f"slot{i}") for i in range(SLOTS)]
        used = sem("weights_used")
        s_zero = sem("zeroed")
        s_const, s_rows, s_tap, s_wz, s_wgu, s_s0, s_wr, s_bmod, s_ln, s_lnb, s_ln2 = [
            sem(n) for n in ("const_in", "rows_in", "taps_in", "wz_in", "wgu_in", "s0_in", "router_in",
                             "bmod_in", "ln1_in", "ln1_bcast_in", "ln2_bcast_in")]
        s_x = [sem("x_prompt_in"), sem("x_sample_in")]
        silu_c = sem("cond_silu")
        rows_ps, tap_ps, cond_rdy, tap_rdy, xpos = [sem(n) for n in (
            "rows_ps", "tap_ps", "cond_ready", "tap_ready", "pos_added")]
        xT_ps, xT_ev, part_ev, col_ps, bcol_rdy, col_rdy, h_dve, h_act = [sem(n) for n in (
            "xT_ps", "xT_evacuated", "modpart_evacuated", "modcol_ps", "bcol_ready", "modcol_ready",
            "h1_prompt", "h1_sample")]
        seg_out, seg_add, seg_dve = [sem(n) for n in ("seg_out", "seg_added", "seg_evacuated")]
        z_ps, z_ev, gate_ps, gate_out, gate_rdy = [sem(n) for n in (
            "z_ps", "z_evacuated", "gate_ps", "gate_out", "gate_ready")]
        ev = [sem(f"pass{i}_evacuated") for i in range(PASSES_IN)]
        uT_ps, uT_ev, conv_c, back_ps, back_var, back_sd, back_ev = [sem(n) for n in (
            "uT_ps", "uT_evacuated", "conv_chain", "conv_back_ps", "conv_var", "conv_sd", "conv_normed")]
        a_ps, a_exp, a_rdy, at_ps, at_ev, kv_ps, kv_ev, kv2_ps, o_ps, o_sq, o_rdy = [sem(n) for n in (
            "decays_ps", "decays_exp", "qk_decayed", "attn_ps", "attn_masked", "kv_ps", "state_mid", "kv2_ps",
            "o_ps", "o_rms", "o_ready")]
        fin_rdy, state_out = sem("final_state_ready"), sem("state_out")
        yT_ps, yT_ev, cT_ps, cT_ev = [sem(n) for n in ("yT_ps", "yT_evacuated", "cT_ps", "cT_evacuated")]
        g1_in, mod2_in, row2 = [sem(n) for n in ("g1_broadcast", "ln1_mod_broadcast", "ln1_mod_rows")]
        m_ev, ln_v, ln_s, xn_rdy, h2_rdy, h2T_ps, h2T_v, h2T_s, lg_ps = [sem(n) for n in (
            "m_evacuated", "ln1_var", "ln1_sd", "x_normed", "h2_ready", "h2T_ps", "h2T_dve", "h2T_act", "logits_ps")]
        lmax, lexp, sel_rdy, rk_ps, tab_rdy = [sem(n) for n in (
            "logit_max", "logit_exp", "selected", "rank_ps", "steps_ready")]
        dch, ach = sem("dve_chain"), sem("act_chain")
        st_onehot, st_sel, st_gath, st_wTp, st_wN, st_wT, st_xv = [sem(n) for n in (
            "step_onehot", "step_weights", "step_gather_ps", "step_wT_ps", "step_wN", "step_wT", "step_x")]
        st_cmb, st_add = sem("step_combine_ps"), sem("step_added")
        bk_hs, bk_h, bk_hTp, bk_hT, bk_y, bk_yf = [sem(n) for n in (
            "block_silu", "block_h", "block_hT_ps", "block_hT", "block_y", "block_y_by_slot")]
        x1_rdy, added, g2_ps, g2_ev, t_g2f, t_base, t_mul, t_var, t_sd, t_nrm, t_gain, out_s = [sem(n) for n in (
            "x1_ready", "all_but_last_step_added", "g2_ps", "g2_evacuated", "tail_g2_f", "tail_base",
            "tail_last_g2_f", "tail_var", "tail_sd", "tail_normed", "tail_gained", "out_done")]
        t_out = [sem("y_prompt_ready"), sem("y_sample_ready")]
        pch = sem("pool_chain")

        wmod2, win2, wout2 = w_mod[0], w_in[0], w_out[0]

        def pass_bank(p, i):
            return (4 * p + i) % 7

        def pass_end(p):
            return 2 * SEG_UNITS + PASS_UNITS + 2 * PASS_UNITS * p - (1 if p else 0)

        def seg_slice(q):
            return slice(32 * q, 32 * q + 32)

        def for_steps(eng, expert, blocks, full):
            def step(t):
                nb = eng.value_load(steps[0:1, 1, bass.ds(t, 1)], min_val=1, max_val=NBLK)
                b0 = eng.value_load(steps[0:1, 2, bass.ds(t, 1)], min_val=0, max_val=NBLK * NSTEP)
                expert(t, b0)
                for v in range(1, NBLK + 1):
                    with eng.If(nb == v):
                        if v < NBLK:
                            blocks(t, b0, v)
                        else:
                            full(t, b0)

            eng.wait_ge(tab_rdy, 1)
            with eng.Fori(0, NE) as e:
                step(e)
            eng.wait_ge(tab_rdy, 2)
            total = eng.value_load(steps[0:1, 4, 0:1], min_val=NE, max_val=NSTEP)
            with eng.If(total > NE):
                with eng.Fori(0, MAX_EXTRA) as j:
                    go = eng.value_load(steps[0:1, 3, bass.ds(j + NE, 1)], min_val=0, max_val=1)
                    with eng.If(go > 0):
                        step(j + NE)

        block = ctx.enter_context(nc.Block())

        @block.sync
        def _(sp):
            n = 0

            def unit(dst, src):
                nonlocal n
                if n >= SLOTS:
                    sp.wait_ge(used, n - SLOTS + 1)
                sp.dma_start(dst, src).then_inc(slot[n % SLOTS], 16)
                n += 1

            def segment(s, kts=range(KT)):
                for kt in kts:
                    unit(ring[:, n % SLOTS, :], wmod2[kt * P:(kt + 1) * P, s * D:(s + 1) * D])

            def first_mod(qb):
                for s in range(2):
                    for u in range(4):
                        unit(ring[:, n % SLOTS, :].rearrange("p (i n) -> p i n", i=4),
                             wmod2[u * 512:(u + 1) * 512, s * D + qb * BANK:s * D + (qb + 1) * BANK]
                             .rearrange("(i p) n -> p i n", i=4))

            def wide_pass(w, col, us=range(PASS_UNITS), seg=None, kt0=0):
                for i, u in enumerate(us):
                    unit(ring[:, n % SLOTS, :].rearrange("p (i n) -> p i n", i=2),
                         w[u * 256:(u + 1) * 256, col:col + 1024].rearrange("(i p) n -> p i n", i=2))
                    if seg is not None:
                        segment(seg, [kt0 + i])

            first_mod(0)
            for qb in range(1, NQ):
                first_mod(qb)
                wide_pass(win2, PASS_COL[0], (2 * qb - 2, 2 * qb - 1))
            wide_pass(win2, PASS_COL[0], (6, 7))
            for p in range(1, PASSES_IN):
                wide_pass(win2, PASS_COL[p], seg=2 + (p - 1) // 2, kt0=8 * ((p - 1) % 2))
            segment(4)
            wide_pass(wout2, 0)
            wide_pass(wout2, 1024)
            segment(5)

            def expert(t, e):
                for i in range(STEP_UNITS):
                    sl = i % SLOTS
                    r = i // 2
                    if i < 16:
                        w = w_e_gate if i % 2 == 0 else w_e_up
                        src = w[0, e, r * 256:(r + 1) * 256, :].rearrange("(i p) n -> p i n", i=2)
                        dst = ring[:, sl, :].rearrange("p (i n) -> p i n", i=2)
                    else:
                        src = w_e_down[0, e, (i - 16) * P:(i - 15) * P, :]
                        dst = ring[:, sl, :]
                    sp.wait_ge(used, t * STEP_UNITS + (PRE_UNITS + i - SLOTS + 1))
                    sp.dma_start(dst, src).then_inc(slot[sl], 16)

            with sp.Fori(0, PER) as a:
                with sp.Fori(0, NGRP) as b:
                    expert(a * NGRP + b, b * PER + a)
            sp.wait_ge(tab_rdy, 2)
            with sp.Fori(0, MAX_EXTRA) as j:
                go = sp.value_load(steps[0:1, 3, bass.ds(j + NE, 1)], min_val=0, max_val=1)
                eo = sp.value_load(steps[0:1, 0, bass.ds(j + NE, 1)], min_val=0, max_val=NE - 1)
                with sp.If(go > 0):
                    expert(j + NE, eo)

        @block.gpsimd
        def _(pool):
            for t in (condT[:, :, :], modrow[:, :, :], lnrow[:, :, :], wgu, attnT, uT):
                nc.gpsimd.memset(t, 0.0).then_inc(s_zero, 1)
            nc.gpsimd.memset(zT, 1.0).then_inc(s_zero, 1)
            def gates(g):
                for d in range(2):
                    pool.wait_ge(gate_out, 4 * (1 - g) + 2 * d + 2)
                    nc.gpsimd.tensor_tensor(gg[:, g, d, :], gg[:, g, d, :], grelu[:, d, :], ALU.add).then_inc(gate_rdy, 1)

            def add_segment(s):
                pool.wait_ge(seg_out, s - 1)
                nc.gpsimd.tensor_tensor(modrow[:, s - 2, :], modrow[:, s - 2, :], segrow, ALU.add).then_inc(seg_add, 1)

            gates(1)
            pool.wait_ge(s_bmod, 32)
            add_segment(2)
            gates(0)
            add_segment(3)
            pool.wait_ge(ln_v, 2)
            nc.gpsimd.memset(acc, 0.0).then_inc(st_add, 8)
            nc.gpsimd.memset(wselT, 0.0).then_inc(st_wT, 1)
            pool.wait_ge(h2_rdy, 2)
            nc.gpsimd.memset(ye, 0.0).then_inc(bk_y, 1)
            pool.wait_ge(lg_ps, 2)
            nc.gpsimd.memset(yf, 0.0).then_inc(bk_yf, 64)
            pool.wait_ge(xn_rdy, 2)
            pool.wait_ge(s_lnb, 32)
            for g in range(G):
                nc.gpsimd.tensor_tensor(xres[:, g, :], xres[:, g, :], lng, ALU.mult).then_inc(pch, 1)
            for g in range(G):
                pool.wait_ge(pch, g + 1)
                nc.gpsimd.tensor_tensor(xres[:, g, :], xres[:, g, :], lnb, ALU.add).then_inc(x1_rdy, 1)

            for g in range(G):
                pool.wait_ge(x1_rdy, g + 1)
                nc.gpsimd.tensor_scalar(xres[:, g, :], xres[:, g, :], ALPHA, None, ALU.mult).then_inc(pch, 1)
            pool.wait_ge(added, 1)
            for q in range(NQ):
                cs = slice(q * BANK, (q + 1) * BANK)
                pool.wait_ge(g2_ev, NQ + q + 1)
                nc.gpsimd.tensor_tensor(acc[:, 1, cs], acc[:, 1, cs], g2b[:, 1, cs], ALU.mult).then_inc(t_g2f, 1)
                pool.wait_ge(t_g2f, q + 1)
                pool.wait_ge(pch, 2 * G)
                nc.gpsimd.tensor_tensor(acc[:, 1, cs], acc[:, 1, cs], xres[:, 1, cs], ALU.add).then_inc(t_base, 1)
            pool.wait_ge(s_ln2, 32)
            pool.wait_ge(t_nrm, 1)
            nc.gpsimd.tensor_tensor(acc[:, 0, :], acc[:, 0, :], lng, ALU.mult).then_inc(t_gain, 1)
            pool.wait_ge(t_gain, 1)
            nc.gpsimd.tensor_tensor(acc[:, 0, :], acc[:, 0, :], lnb, ALU.add).then_inc(t_out[0], 1)

        @block.scalar
        def _(act):
            n = 0

            def link(ins):
                nonlocal n
                n += 1
                ins.then_inc(ach, 1)
                act.wait_ge(ach, n)

            act.dma_start(const[:, :], table).then_inc(s_const, 16)
            r128 = lambda a: a.rearrange("(k p) -> k p", p=P)
            act.dma_start(rows[0:16, :], r128(c_ctx)).then_inc(s_rows, 16)
            act.dma_start(rows[16:32, :], r128(c[0])).then_inc(s_rows, 16)
            act.dma_start(rows[32:40, :], r128(gla_norm_g[0])).then_inc(s_rows, 16)
            act.dma_start(rows[40:48, :], r128(conv_ln_g[0])).then_inc(s_rows, 16)
            act.dma_start(rows[48:56, :], r128(conv_ln_b[0])).then_inc(s_rows, 16)
            act.dma_start(rows[56:88, :], r128(b_mod[0, 0:2 * D])).then_inc(s_rows, 16)
            act.dma_start(taprow[0:TAPS, :], w_dw[0]).then_inc(s_tap, 16)
            act.dma_start(taprow[TAPS:TAPS + 1, :], b_dw).then_inc(s_tap, 16)
            act.dma_start(xres[:, 0, :], x_prompt[0]).then_inc(s_x[0], 16)
            act.dma_start(xres[:, 1, :], x_sample[0]).then_inc(s_x[1], 16)
            act.dma_start(posb, pos).then_inc(s_x[1], 16)
            act.wait_ge(s_zero, 7)
            mod_rows = b_mod[0].rearrange("(s q j) -> q s j", q=NQ, j=BANK)
            for g in range(G):
                act.dma_start(modrow[g:97 + g:32, :, :], mod_rows[:, 2:6, :]).then_inc(s_bmod, 16)
            for i, w in enumerate((ln1_g, ln1_b)):
                for g in range(G):
                    act.dma_start(lnrow[g:97 + g:32, i, :], w[0].rearrange("(q j) -> q j", q=NQ)).then_inc(s_ln, 16)
            act.dma_start(wz, win2[:, Z_COL:Z_COL + 32].rearrange("(k p) n -> p k n", p=P)).then_inc(s_wz, 16)
            for d in range(2):
                act.dma_start(wgu[RANK * d:RANK * d + RANK, d, :], w_gate_up[0, d]).then_inc(s_wgu, 16)
            act.dma_start(wgu[2 * RANK:2 * RANK + 1, :, :], b_gate).then_inc(s_wgu, 16)

            act.wait_ge(s_rows, 96)
            nc.scalar.activation(rows[0:32, :], rows[0:32, :], ACT.Silu).then_inc(silu_c, 1)

            act.wait_ge(xT_ev, 8)
            for kt in range(KT):
                q, j = divmod(kt, NQ)
                act.wait_ge(col_rdy, q + 1)
                nc.scalar.activation(hT[:, kt, P:2 * P], hT[:, kt, P:2 * P], ACT.Identity,
                                     bias=modcol[:, 0, q, j, 1:2], scale=modcol[:, 1, q, j, 1:2]).then_inc(h_act, 1)

            def evac(p, dst, func):
                act.wait_ge(used, pass_end(p))
                for g in range(G):
                    for hf in range(2):
                        nc.scalar.activation(dst[:, g, hf * BANK:(hf + 1) * BANK],
                                             ps[pass_bank(p, 2 * g + hf)][:, :], func).then_inc(ev[p], 1)

            evac(0, sig, ACT.Sigmoid)
            act.dma_start(s0, state_gla[0, 0].rearrange("d h k v -> k d h v")).then_inc(s_s0, 16)
            act.dma_start(wr[:, :, :], w_router.rearrange("(k p) e -> p k e", p=P)).then_inc(s_wr, 16)
            act.dma_start(br[:, :], b_router.partition_broadcast(P)).then_inc(s_wr, 16)
            act.wait_ge(z_ps, 1)
            nc.scalar.copy(zT[0:32, :], ps[6][0:32, 0:256]).then_inc(z_ev, 1)

            def gates(g, banks):
                if g == 0:
                    act.wait_ge(gate_rdy, 2)
                for d in range(2):
                    dst = gg[:, g, d, :]
                    act.wait_ge(gate_ps, 2 * (1 - g) + d + 1)
                    nc.scalar.activation(grelu[:, d, :], ps[banks[d]][:, :], ACT.Relu, scale=-1.0).then_inc(gate_out, 1)
                    link(nc.scalar.activation(dst, ps[banks[d]][:, :], ACT.Abs))
                    link(nc.scalar.activation(dst, dst, ACT.Exp, scale=-1.0))
                    nc.scalar.activation(dst, dst, ACT.Ln, bias=ones[:, 0:1]).then_inc(gate_out, 1)

            def segment_out(s):
                act.wait_ge(used, pass_end(2 * s - 2) + 1)
                if s == 3:
                    act.wait_ge(seg_add, 1)
                nc.scalar.copy(segrow, ps[7][:, :]).then_inc(seg_out, 1)

            gates(1, GATE_BANKS[1])
            evac(2, qk, ACT.Copy)
            segment_out(2)
            gates(0, GATE_BANKS[0])
            evac(3, vv, ACT.Copy)
            for g in range(G):
                act.wait_ge(back_var, g + 1)
                nc.scalar.activation(small[:, 32 + g:33 + g], small[:, 51 + 2 * g:52 + 2 * g], ACT.Sqrt,
                                     bias=small[:, 63:64]).then_inc(back_sd, 1)
            evac(4, rs, ACT.Silu)
            segment_out(3)

            for gi, g in enumerate((1, 0)):
                if gi:
                    act.wait_ge(o_ps, 2)
                else:
                    act.wait_ge(gate_rdy, 4)
                    act.wait_ge(seg_add, 2)
                for d in range(2):
                    act.wait_ge(a_ps, 6 * gi + 1 + d)
                    nc.scalar.activation(qTt[:, d], ps[2 + d][:, :].rearrange("p (h t) -> p h t", h=HEADS),
                                         ACT.Exp).then_inc(a_exp, 1)
                    nc.scalar.activation(kTt[:, d], ps[2 + d][:, :].rearrange("p (h t) -> p h t", h=HEADS),
                                         ACT.Exp, scale=-1.0).then_inc(a_exp, 1)
                    act.wait_ge(a_ps, 6 * gi + 3 + d)
                    nc.scalar.activation(kdec[:, d, :], ps[4 + d][:, :], ACT.Exp).then_inc(a_exp, 1)
                if g == 1:
                    for i in range(G * CC):
                        cg, cc = divmod(i, CC)
                        act.wait_ge(cT_ps, i // 4 + 1)
                        nc.scalar.activation(hT[:, CC + cc, cg * P:(cg + 1) * P], ps[1][:, (i % 4) * P:(i % 4 + 1) * P],
                                             ACT.Silu, bias=gcol[:, 2, cc:cc + 1], scale=gcol[:, 1, cc:cc + 1]).then_inc(cT_ev, 1)
                if g == 0:
                    for i in range(4):
                        act.wait_ge(kv_ps, 4 + i + 1)
                        nc.scalar.copy(smid[:, i // 2, 2 * (i % 2):2 * (i % 2) + 2, :],
                                       ps[4 + i][:, :].rearrange("p (h v) -> p h v", h=2)).then_inc(kv_ev, 1)
                for h in range(HEADS):
                    act.wait_ge(o_ps, 2 * gi + h // 2 + 1)
                    link(nc.scalar.activation(junk[:, 0:DV], ps[2 + h // 2][:, (h % 2) * DV:(h % 2 + 1) * DV],
                                              ACT.Square, accum_out=small[:, 4 * g + h:4 * g + h + 1]))
                nc.scalar.activation(small[:, 16 + 4 * g:20 + 4 * g], small[:, 4 * g:4 * g + 4], ACT.Sqrt,
                                     bias=small[:, 63:64], scale=1.0 / DV).then_inc(o_sq, 1)

            act.wait_ge(fin_rdy, 8)
            act.dma_start(new_state[0, 0].rearrange("d h k v -> k d h v"), s0).then_inc(state_out, 16)
            def broadcast(dst, place, signal):
                for g in range(G):
                    for q in range(NQ):
                        r = 32 * q + g
                        act.dma_start(dst[:, g, q * BANK:(q + 1) * BANK],
                                      modrow[r:r + 1, place, :].unsqueeze(1).broadcast_to([1, P, BANK])).then_inc(signal, 16)

            act.wait_ge(o_rdy, 8)
            act.wait_ge(cT_ps, 4)
            act.wait_ge(seg_add, 1)
            broadcast(g1b, 0, g1_in)
            act.wait_ge(row2, 1)
            act.wait_ge(state_out, 16)
            broadcast(G2b, 2, mod2_in)
            broadcast(B2b, 1, mod2_in)
            for g in range(G):
                act.wait_ge(ln_v, g + 1)
                nc.scalar.activation(small[:, 40 + g:41 + g], small[:, 37 + 2 * g:38 + 2 * g], ACT.Sqrt,
                                     bias=small[:, 63:64]).then_inc(ln_s, 1)
                for b in range(2):
                    act.wait_ge(h2T_ps, 4 * g + 2 * b + 2)
                    nc.scalar.copy(hT[:, 4 * (2 * b + 1):4 * (2 * b + 2), g * P:(g + 1) * P],
                                   ps[H2T_BANKS[2 * b + 1]][:, :].rearrange("p (k t) -> p k t", k=4)).then_inc(h2T_s, 1)
            act.wait_ge(h2_rdy, 2)
            act.dma_start(lng, ln1_g[0].partition_broadcast(P)).then_inc(s_lnb, 16)
            act.dma_start(lnb, ln1_b[0].partition_broadcast(P)).then_inc(s_lnb, 16)
            act.wait_ge(lmax, 1)
            for g in range(G):
                nc.scalar.activation(rt[:, 1, g * NE:(g + 1) * NE], rt[:, 0, g * NE:(g + 1) * NE], ACT.Exp,
                                     bias=small[:, 44 + g:45 + g], accum_out=small[:, 48 + g:49 + g]).then_inc(lexp, 1)

            def expert(t, b0):
                pass

            def blocks(t, b0, v):
                act.wait_ge(used, t * STEP_UNITS + (PRE_UNITS + 16))
                for b in range(v):
                    if b >= 2:
                        act.wait_ge(bk_h, b0 + (b - 1))
                    nc.scalar.activation(hs[:, b % 2, :], ps[b][:, 0:256], ACT.Silu).then_inc(bk_hs, 1)
                act.wait_ge(st_cmb, t * 8 + 8)
                act.wait_ge(st_wN, t + 1)
                nc.scalar.copy(wselT, wselN).then_inc(st_wT, 1)
                act.wait_ge(used, t * STEP_UNITS + (PRE_UNITS + 24))
                act.wait_ge(bk_yf, b0 * 64 + 64)
                for b in range(v):
                    nc.scalar.copy(ye[:, b, :], ps[4 + b][:, :]).then_inc(bk_y, 1)
                    act.wait_ge(bk_y, b0 + (b + 2))
                    for q in range(4):
                        act.dma_start(yf[seg_slice(b), q * BANK:(q + 1) * BANK],
                                      ye[seg_slice(q), b, :]).then_inc(bk_yf, 16)

            def full(t, b0):
                act.wait_ge(used, t * STEP_UNITS + (PRE_UNITS + 16))
                for hf in range(2):
                    if hf:
                        act.wait_ge(bk_h, b0 + 2)
                    nc.scalar.activation(hs1, ps[hf][:, :], ACT.Silu).then_inc(bk_hs, 2)
                act.wait_ge(st_cmb, t * 8 + 8)
                act.wait_ge(st_wN, t + 1)
                nc.scalar.copy(wselT, wselN).then_inc(st_wT, 1)
                act.wait_ge(used, t * STEP_UNITS + (PRE_UNITS + 24))
                for q in range(2):
                    nc.scalar.copy(yf[:, q * BANK:(q + 1) * BANK], ps[4 + q][:, :]).then_inc(bk_y, 2)

            for_steps(act, expert, blocks, full)

            for j in range(G * NQ):
                g, q = divmod(j, NQ)
                if j == NQ:
                    act.wait_ge(x1_rdy, 2)
                    act.dma_start(lng, ln2_g[0].partition_broadcast(P)).then_inc(s_ln2, 16)
                    act.dma_start(lnb, ln2_b[0].partition_broadcast(P)).then_inc(s_ln2, 16)
                act.wait_ge(g2_ps, j + 1)
                nc.scalar.copy(g2b[:, g, q * BANK:(q + 1) * BANK], ps[4 + j % 2][:, :]).then_inc(g2_ev, 1)
            for g in range(G):
                act.wait_ge(t_var, g + 1)
                nc.scalar.activation(small[:, 40 + g:41 + g], small[:, 37 + 2 * g:38 + 2 * g], ACT.Sqrt,
                                     bias=small[:, 63:64]).then_inc(t_sd, 1)
            act.wait_ge(t_out[0], 1)
            act.dma_start(y_prompt[0], acc[:, 0, :]).then_inc(out_s, 16)
            for i in range(2):
                cs = slice(i * D // 2, (i + 1) * D // 2)
                act.wait_ge(t_out[1], i + 1)
                act.dma_start(y_sample[0, :, cs], acc[:, 1, cs]).then_inc(out_s, 16)
            act.wait_ge(out_s, 48)

        @block.tensor
        def _(pe):
            n = 0
            mm = nc.tensor.matmul
            tr = nc.tensor.transpose

            def arrive():
                pe.wait_ge(slot[n % SLOTS], 16 * (n // SLOTS + 1))

            pe.wait_ge(s_const, 16)
            pe.wait_ge(s_rows, 96)
            pe.wait_ge(silu_c, 1)
            tr(ps[6][:, 0:88], rows[:, :], ident[0:88, 0:88]).then_inc(rows_ps, 1)
            pe.wait_ge(s_tap, 32)
            for cc in range(CC):
                last = tr(ps[7][:, cc * 32:cc * 32 + 32], taprow[0:32, cc * P:(cc + 1) * P], ident[0:32, 0:32])
            last.then_inc(tap_ps, 1)

            def seg_units(bank, kts):
                nonlocal n
                for kt in kts:
                    arrive()
                    for q in range(NQ):
                        last = mm(ps[bank][seg_slice(q), :], condT[:, kt, :],
                                  ring[:, n % SLOTS, q * BANK:(q + 1) * BANK], start=(kt == 0), stop=(kt == KT - 1))
                    last.then_inc(used, 1)
                    n += 1

            def first_mod(qb):
                nonlocal n
                for s in range(2):
                    if qb:
                        pe.wait_ge(part_ev, 2 * qb - 1 + s)
                    for u in range(4):
                        arrive()
                        for i in range(4):
                            last = mm(ps[4 + s][seg_slice(i), :], condT[:, 4 * u + i, :],
                                      ring[:, n % SLOTS, i * BANK:(i + 1) * BANK], start=(u == 0), stop=(u == 3))
                        last.then_inc(used, 1)
                        n += 1

            def mod_columns(qb):
                if qb:
                    pe.wait_ge(col_rdy, qb)
                for s in range(2):
                    pe.wait_ge(part_ev, 2 * qb + s + 1)
                    for j in range(NQ):
                        c0 = 8 * s + 2 * j
                        last = mm(ps[6][:, c0:c0 + 2], modpart[:, s, j * P:(j + 1) * P], const[:, C_SUM:C_SUM + 2],
                                  start=True, stop=True)
                last.then_inc(col_ps, 1)

            def wide_pass(bank, us=range(PASS_UNITS), before=None, after=None):
                nonlocal n
                for u in us:
                    arrive()
                    for i in range(2):
                        kt = 2 * u + i
                        for k in range(4):
                            if before and kt == 0:
                                before(k)
                            g, hf = divmod(k, 2)
                            last = mm(ps[bank[k]][:, :], hT[:, kt, g * P:(g + 1) * P],
                                      ring[:, n % SLOTS, i * 1024 + hf * BANK:i * 1024 + (hf + 1) * BANK],
                                      start=(kt == 0), stop=(kt == KT - 1))
                    last.then_inc(used, 1)
                    n += 1
                    if after:
                        after(u)

            pe.wait_ge(cond_rdy, 1)
            first_mod(0)
            pe.wait_ge(s_x[0], 16)
            for b in range(8):
                g = b // 4
                if b == 4:
                    pe.wait_ge(xpos, 1)
                if b >= 4:
                    pe.wait_ge(xT_ev, b - 3)
                for i in range(4):
                    kt = 4 * (b % 4) + i
                    last = tr(ps[b % 4][:, i * P:(i + 1) * P], xres[:, g, kt * P:(kt + 1) * P], ident)
                last.then_inc(xT_ps, 1)
            pe.wait_ge(bcol_rdy, 1)
            mod_columns(0)
            bank0 = [pass_bank(0, i) for i in range(4)]
            pe.wait_ge(xT_ev, 8)
            for qb in range(NQ):
                if qb < NQ - 1:
                    first_mod(qb + 1)
                pe.wait_ge(h_dve, 4 * qb + 4)
                pe.wait_ge(h_act, 4 * qb + 4)
                wide_pass(bank0, (2 * qb, 2 * qb + 1))
                if qb < NQ - 1:
                    mod_columns(qb + 1)
            pe.wait_ge(s_wz, 16)
            pe.wait_ge(col_rdy, NQ)
            for kt in range(KT):
                last = mm(ps[6][0:32, 0:256], wz[:, kt, :], hT[:, kt, :], start=(kt == 0), stop=(kt == KT - 1))
            last.then_inc(z_ps, 1)

            def gates(g, banks):
                for d in range(2):
                    mm(ps[banks[d]][:, :], zT[:, g * P:(g + 1) * P], wgu[:, d, :], start=True, stop=True).then_inc(gate_ps, 1)

            def u_transposed():
                pe.wait_ge(ev[1], 4)
                for i in range(G * CC):
                    g, cc = divmod(i, CC)
                    b = i // 4
                    if i == 12:
                        pe.wait_ge(uT_ev, 1)
                    last = tr(ps[U_BANKS[b]][:, (i % 4) * P:(i % 4 + 1) * P], uu[:, g, cc * P:(cc + 1) * P], ident)
                    if i % 4 == 3:
                        last.then_inc(uT_ps, 1)

            for p in range(1, PASSES_IN):
                def free_bank(k):
                    if p == 1 and k == 0:
                        pe.wait_ge(part_ev, 8)
                    if p == 1 and k == 2:
                        pe.wait_ge(z_ev, 1)
                    if p >= 2 and k == 0:
                        pe.wait_ge(ev[p - 2], 4)
                    if p == 2 and k == 0:
                        pe.wait_ge(gate_out, 4)
                    if p == 3 and k == 0:
                        pe.wait_ge(uT_ev, 4)
                    if p == 4 and k == 0:
                        pe.wait_ge(gate_out, 8)
                    if k == 3:
                        pe.wait_ge(ev[p - 1], 1)

                def after(u):
                    s = 2 + (p - 1) // 2
                    if u == 0 and p == 1:
                        pe.wait_ge(tap_rdy, 2)
                    if u == 0 and p == 3:
                        pe.wait_ge(seg_out, 1)
                    seg_units(7, [8 * ((p - 1) % 2) + u])
                    if p == 1 and u == 2:
                        pe.wait_ge(ev[0], 4)
                        pe.wait_ge(z_ev, 1)
                        pe.wait_ge(s_wgu, 48)
                        gates(1, GATE_BANKS[1])
                    if p == 2 and u == 1:
                        u_transposed()
                    if p == 4 and u in (1, 4):
                        g = (u - 1) // 3
                        if g == 0:
                            pe.wait_ge(ev[3], 4)
                            pe.wait_ge(conv_c, TAPS * CC)
                        else:
                            pe.wait_ge(back_ev, 1)
                        for cc in range(CC):
                            last = tr(ps[BACK_BANKS[g][cc // 4]][:, (cc % 4) * P:(cc % 4 + 1) * P], convacc[:, cc, g, :], ident)
                        last.then_inc(back_ps, 1)
                    if p == 3 and u == 1:
                        pe.wait_ge(ev[2], 4)
                        gates(0, GATE_BANKS[0])

                wide_pass([pass_bank(p, i) for i in range(4)], before=free_bank, after=after)

            def segment_part(k):
                seg_units(0, range((0, 3, 6, 9, 12)[k], (3, 6, 9, 12, 16)[k]))

            def decays(gi, g):
                if gi == 0:
                    pe.wait_ge(gate_rdy, 4)
                    pe.wait_ge(ev[4], 4)
                    pe.wait_ge(seg_out, 2)
                else:
                    pe.wait_ge(o_rdy, 4)
                    pe.wait_ge(kv_ev, 8)
                for d in range(2):
                    for h in range(HEADS):
                        last = mm(ps[2 + d][:, h * P:(h + 1) * P], gg[:, g, d, h * P:(h + 1) * P], incl[d],
                                  start=True, stop=True)
                    last.then_inc(a_ps, 1)
                for d in range(2):
                    mm(ps[4 + d][:, :], rest[d], gg[:, g, d, :], start=True, stop=True).then_inc(a_ps, 1)
                for i in range(2):
                    for h in range(HEADS):
                        last = tr(ps[6 + i][:, h * P:(h + 1) * P], qk[:, g, i * 512 + h * P:i * 512 + (h + 1) * P], ident)
                    last.then_inc(a_ps, 1)

            def kv(g, chunk, signal):
                for d in range(2):
                    r = slice(HALF * chunk[d], HALF * chunk[d] + HALF)
                    for h in range(HEADS):
                        last = mm(ps[4 + 2 * d + h // 2][:, (h % 2) * DV:(h % 2 + 1) * DV],
                                  kdec[r, d, h * P:(h + 1) * P], vv[r, g, h * DV:(h + 1) * DV], start=True, stop=True)
                        if h % 2:
                            last.then_inc(signal, 1)

            def scores(gi, g):
                pe.wait_ge(a_rdy, 8 * (gi + 1))
                for d in range(2):
                    for h in range(HEADS):
                        last = mm(ps[2 + d][:, h * P:(h + 1) * P], kTt[:, d, h, :], qTt[:, d, h, :],
                                  start=True, stop=True)
                    last.then_inc(at_ps, 1)
                kv(g, (0, 1), kv_ps)

            def outputs(gi, g):
                pe.wait_ge(at_ev, 2 * (gi + 1))
                pe.wait_ge(kv_ev, 8 if gi == 0 else 12)
                if g == 1:
                    pe.wait_ge(s_s0, 16)
                for h in range(HEADS):
                    o = ps[2 + h // 2][:, (h % 2) * DV:(h % 2 + 1) * DV]
                    v = vv[:, g, h * DV:(h + 1) * DV]
                    mm(o, attnT[:, 0, h, :], v, start=True, stop=False)
                    parts = [(0, 1, smid), (1, 0, smid)]
                    if g == 1:
                        parts += [(0, 0, s0), (1, 1, s0)]
                    mm(o, attnT[:, 1, h, :], v, start=False, stop=False)
                    for i, (d, ch, st) in enumerate(parts):
                        r = slice(HALF * ch, HALF * ch + HALF)
                        last = mm(o[r, :], qTt[:, d, h, r], st[:, d, h, :], start=False,
                                  stop=(i >= len(parts) - 2))
                    if h % 2:
                        last.then_inc(o_ps, 1)

            def conv_transposed(i):
                g = i // 2
                if i:
                    pe.wait_ge(cT_ev, 4 * i)
                for k in range(4):
                    cc = 4 * (i % 2) + k
                    last = tr(ps[1][:, k * P:(k + 1) * P], cn[:, g, cc * P:(cc + 1) * P], ident)
                last.then_inc(cT_ps, 1)

            pe.wait_ge(back_ev, 2)
            decays(0, 1)
            conv_transposed(0)
            segment_part(0)
            conv_transposed(1)
            segment_part(1)
            conv_transposed(2)
            scores(0, 1)
            conv_transposed(3)
            segment_part(2)
            outputs(0, 1)
            segment_part(3)
            decays(1, 0)
            segment_part(4)
            scores(1, 0)
            pe.wait_ge(kv_ev, 12)
            kv(0, (1, 0), kv2_ps)
            outputs(1, 0)
            pe.wait_ge(o_rdy, 8)
            pe.wait_ge(fin_rdy, 8)
            for i in range(G * 8):
                g, kt = divmod(i, 8)
                last = tr(ps[2 + i // 4][:, (i % 4) * P:(i % 4 + 1) * P], vv[:, g, kt * P:(kt + 1) * P], ident)
                if i % 4 == 3:
                    last.then_inc(yT_ps, 1)
            pe.wait_ge(yT_ev, 4)
            wide_pass([0, 1, 2, 3])
            wide_pass([4, 5, 6, 7])

            pe.wait_ge(m_ev, 4)
            seg_units(3, range(0, 8))
            for g in range(G):
                pe.wait_ge(h2_rdy, g + 1)
                for b in range(4):
                    if g:
                        pe.wait_ge((h2T_v, h2T_s)[b % 2], b // 2 + 1)
                    for i in range(4):
                        kt = 4 * b + i
                        last = tr(ps[H2T_BANKS[b]][:, i * P:(i + 1) * P], h2[:, g, kt * P:(kt + 1) * P], ident)
                    last.then_inc(h2T_ps, 1)
                seg_units(3, (range(8, 10), range(10, 11))[g])
                if g == 0:
                    pe.wait_ge(s_wr, 32)
                pe.wait_ge(h2T_v, 2 * (g + 1))
                pe.wait_ge(h2T_s, 2 * (g + 1))
                for kt in range(KT):
                    last = mm(ps[4][:, g * NE:(g + 1) * NE], hT[:, kt, g * P:(g + 1) * P], wr[:, kt, :],
                              start=(kt == 0), stop=(kt == KT - 1))
                last.then_inc(lg_ps, 1)
            seg_units(3, range(11, 16))
            pe.wait_ge(sel_rdy, 1)
            s_g = [rt[:, 8, 0:NE], rt[:, 8, NE:2 * NE]]
            mm(ps[5][:, 0:NE], before, s_g[0], start=True, stop=True)
            mm(ps[5][:, NE:2 * NE], before, s_g[1], start=True, stop=False)
            mm(ps[5][:, NE:2 * NE], ones, s_g[0], start=False, stop=True)
            mm(ps[5][:, 32:48], ones, s_g[0], start=True, stop=False)
            last = mm(ps[5][:, 32:48], ones, s_g[1], start=False, stop=True)
            last.then_inc(rk_ps, 1)

            def unit_in(t, i):
                pe.wait_ge(slot[i % SLOTS], t * 48 + 16 * (PRE_UNITS // SLOTS + i // SLOTS + 1))

            def expert(t, b0):
                pe.wait_ge(st_onehot, t * 2 + 2)
                pe.wait_ge(st_add, t * 8 + 8)
                for kt in range(KT):
                    for g in range(G):
                        last = mm(ps[kt // 4][:, (kt % 4) * P:(kt % 4 + 1) * P],
                                  h2[:, g, kt * P:(kt + 1) * P], sel[:, g, :], start=(g == 0), stop=(g == 1))
                    if kt % 4 == 3:
                        last.then_inc(st_gath, 1)
                pe.wait_ge(st_sel, t + 1)
                pe.wait_ge(bk_y, b0 + 1)
                for g in range(G):
                    last = tr(ps[4][:, g * P:(g + 1) * P], wsel[:, g, :], ident)
                last.then_inc(st_wTp, 1)
                pe.wait_ge(st_xv, t * 4 + 4)
                pe.wait_ge(st_wN, t + 1)

            def combine_one(j):
                g, q = divmod(j, NQ)
                mm(ps[q][:, :], wselT[:, g, :], yf[:, q * BANK:(q + 1) * BANK], start=True, stop=True).then_inc(st_cmb, 1)

            def combine(t, b0):
                pe.wait_ge(bk_yf, b0 * 64 + 64)
                pe.wait_ge(bk_y, b0 + 1)
                pe.wait_ge(st_wT, t + 1)
                for j in range(G * NQ):
                    if j >= NQ:
                        pe.wait_ge(st_add, t * 8 + (j + 5))
                    combine_one(j)

            def blocks(t, b0, v):
                for i in range(16):
                    unit_in(t, i)
                    for k in range(2):
                        kt = 2 * (i // 2) + k
                        for b in range(v):
                            for q in range(4):
                                last = mm(ps[b][seg_slice(q), (i % 2) * 256:(i % 2 + 1) * 256], XT[:, kt, b * BLK:(b + 1) * BLK],
                                          ring[:, i % SLOTS, k * 1024 + q * 256:k * 1024 + (q + 1) * 256],
                                          start=(i == 0 and k == 0), stop=(kt == KT - 1), skip_group_check=True)
                    last.then_inc(used, 1)
                for b in range(v):
                    pe.wait_ge(bk_h, b0 + (b + 1))
                    for j in range(2):
                        last = tr(ps[4 + b][:, j * P:(j + 1) * P], hh[:, b % 2, j * P:(j + 1) * P], ident)
                    last.then_inc(bk_hTp, 1)
                combine(t, b0)
                pe.wait_ge(bk_hT, b0 + v)
                for i in range(FT):
                    unit_in(t, 16 + i)
                    for b in range(v):
                        lhsT = hTm[:, b, i % 2, BLK * (i // 2):BLK * (i // 2 + 1)]
                        for q in range(4):
                            last = mm(ps[4 + b][seg_slice(q), :], lhsT, ring[:, i, q * BANK:(q + 1) * BANK],
                                      start=(i == 0), stop=(i == FT - 1))
                    last.then_inc(used, 1)
            def full(t, b0):
                for i in range(16):
                    unit_in(t, i)
                    for k in range(2):
                        kt = 2 * (i // 2) + k
                        for hf in range(2):
                            last = mm(ps[2 * (i % 2) + hf][:, :], XT[:, kt, :],
                                      ring[:, i % SLOTS, k * 1024 + hf * BANK:k * 1024 + (hf + 1) * BANK],
                                      start=(kt == 0), stop=(kt == KT - 1))
                    last.then_inc(used, 1)
                for hf in range(2):
                    pe.wait_ge(bk_h, b0 + (2 * hf + 2))
                    for j in range(4):
                        last = tr(ps[4 + hf][:, j * P:(j + 1) * P], hh1[:, j * P:(j + 1) * P], ident)
                    last.then_inc(bk_hTp, 2)
                combine(t, b0)
                pe.wait_ge(bk_hT, b0 + 4)
                for i in range(FT):
                    unit_in(t, 16 + i)
                    for q in range(NQ):
                        last = mm(ps[4 + q][:, :], hTf[:, i, :], ring[:, i, q * BANK:(q + 1) * BANK],
                                  start=(i == 0), stop=(i == FT - 1))
                    last.then_inc(used, 1)

            pe.wait_ge(seg_dve, 2)
            for_steps(pe, expert, blocks, full)
            tl = pe.value_load(steps[0:1, 4, 0:1], min_val=NE, max_val=NSTEP)
            bl = pe.value_load(steps[0:1, 4, 1:2], min_val=NE, max_val=NBLK * NSTEP)
            pe.wait_ge(bk_y, bl + 1)
            for g in range(G):
                for q in range(NQ):
                    j = NQ * g + q
                    if j >= 2:
                        pe.wait_ge(g2_ev, j - 1)
                    mm(ps[4 + j % 2][:, :], pick(g, q), modrow[:, 3, :], start=True, stop=True).then_inc(g2_ps, 1)
                if g == 0:
                    pe.wait_ge(st_add, tl * 8 + 8)
                    pe.wait_ge(bk_yf, bl * 64 + 64)
                    pe.wait_ge(st_wT, tl + 1)
                for q in range(NQ):
                    if g:
                        pe.wait_ge(t_mul, q + 1)
                    combine_one(NQ * g + q)

        @block.vector
        def _(dve):
            n = 0
            v = nc.vector

            def link(ins):
                nonlocal n
                n += 1
                ins.then_inc(dch, 1)
                dve.wait_ge(dch, n)

            link(v.memset(small[:, 63:64], EPS))
            dve.wait_ge(s_zero, 1)
            dve.wait_ge(rows_ps, 1)
            v.tensor_copy(condT[:, :, 0:2].rearrange("p k c -> p c k"),
                          ps[6][:, 0:32].rearrange("p (c k) -> p c k", c=2)).then_inc(cond_rdy, 1)
            v.tensor_copy(gcol[:, :, :], ps[6][:, 32:56].rearrange("p (a c) -> p a c", a=3)).then_inc(tap_rdy, 1)
            v.tensor_copy(bcol[:, 0], ps[6][:, 56:72].rearrange("p (a c) -> p a c", a=NQ))
            v.tensor_scalar(bcol[:, 1], ps[6][:, 72:88].rearrange("p (a c) -> p a c", a=NQ),
                            1.0, None, ALU.add).then_inc(bcol_rdy, 1)
            dve.wait_ge(bcol_rdy, 1)
            dve.wait_ge(tap_ps, 1)
            v.tensor_copy(tapT[:, :, :], ps[7][:, 0:256].rearrange("p (c k) -> p c k", c=CC)).then_inc(tap_rdy, 1)

            def parts_out(qb):
                if qb:
                    dve.wait_ge(col_ps, qb)
                for s in range(2):
                    dve.wait_ge(used, (10 * qb - 2 if qb else 0) + 4 * (s + 1))
                    v.tensor_copy(modpart[:, s, :], ps[4 + s][:, :]).then_inc(part_ev, 1)

            parts_out(0)
            for b in range(8):
                g = b // 4
                if b == 4:
                    dve.wait_ge(s_x[1], 32)
                    v.tensor_tensor(xres[:, 1, :], xres[:, 1, :], posb, ALU.add).then_inc(xpos, 1)
                dve.wait_ge(xT_ps, b + 1)
                v.tensor_copy(hT[:, 4 * (b % 4):4 * (b % 4) + 4, g * P:(g + 1) * P],
                              ps[b % 4][:, :].rearrange("p (k t) -> p k t", k=4)).then_inc(xT_ev, 1)
            dve.wait_ge(xT_ev, 8)
            for qb in range(NQ):
                if qb:
                    parts_out(qb)
                dve.wait_ge(col_ps, qb + 1)
                v.tensor_tensor(modcol[:, :, qb], ps[6][:, 0:16].rearrange("p (s j c) -> p s j c", s=2, j=NQ),
                                bcol[:, :, qb].unsqueeze(3).broadcast_to([P, 2, NQ, G]), ALU.add).then_inc(col_rdy, 1)
                dve.wait_ge(col_rdy, qb + 1)
                for j in range(NQ):
                    kt = NQ * qb + j
                    v.tensor_scalar(hT[:, kt, 0:P], hT[:, kt, 0:P], modcol[:, 1, qb, j, 0:1], modcol[:, 0, qb, j, 0:1],
                                    ALU.mult, ALU.add).then_inc(h_dve, 1)
            dve.wait_ge(used, pass_end(1))
            dve.wait_ge(xpos, 1)
            for i in range(4):
                g, hf = divmod(i, 2)
                dve.wait_ge(ev[0], i + 1)
                cs = slice(hf * BANK, (hf + 1) * BANK)
                v.tensor_tensor(uu[:, g, cs], ps[pass_bank(1, i)][:, :], sig[:, g, cs], ALU.mult).then_inc(ev[1], 1)
            for i in range(4):
                g = i // 2
                dve.wait_ge(uT_ps, i + 1)
                v.tensor_copy(uT[:, 4 * (i % 2):4 * (i % 2) + 4, g, PAD:PAD + P],
                              ps[U_BANKS[i]][:, :].rearrange("p (c t) -> p c t", c=4)).then_inc(uT_ev, 1)
            dve.wait_ge(uT_ev, 4)
            done = 0
            for c0 in range(0, CC, 2):
                for k in range(TAPS):
                    for cc in (c0, c0 + 1):
                        src = uT[:, cc, :, k:k + P]
                        if k == 0:
                            last = v.tensor_scalar(convacc[:, cc], src, tapT[:, cc, 0:1], tapT[:, cc, TAPS:TAPS + 1],
                                                   ALU.mult, ALU.add)
                        else:
                            dve.wait_ge(conv_c, done - 1)
                            last = v.scalar_tensor_tensor(convacc[:, cc], src, tapT[:, cc, k:k + 1], convacc[:, cc],
                                                          ALU.mult, ALU.add)
                        last.then_inc(conv_c, 1)
                        done += 1

            for g in range(G):
                dve.wait_ge(back_ps, g + 1)
                for b in range(2):
                    link(v.bn_stats(stats[:, g, b, :], ps[BACK_BANKS[g][b]][:, :]))
                v.bn_aggr(small[:, 50 + 2 * g:52 + 2 * g], stats[:, g, 0:2, :]).then_inc(back_var, 1)
                dve.wait_ge(back_sd, g + 1)
                link(v.reciprocal(small[:, 34 + g:35 + g], small[:, 32 + g:33 + g]))
                for b in range(2):
                    last = v.tensor_scalar(cn[:, g, b * BANK:(b + 1) * BANK], ps[BACK_BANKS[g][b]][:, :],
                                           small[:, 50 + 2 * g:51 + 2 * g], small[:, 34 + g:35 + g],
                                           ALU.subtract, ALU.mult)
                last.then_inc(back_ev, 1)

            def gla(gi, g):
                for d in range(2):
                    dve.wait_ge(a_exp, 6 * gi + 3 * d + 1)
                    cols = (63, 127) if d == 0 else (0, 64)
                    for ch in range(2):
                        link(v.tensor_copy(decay[:, d, ch, :], qTt[:, d, :, cols[ch]]))
                    dve.wait_ge(a_ps, 6 * gi + 5)
                    v.scalar_tensor_tensor(qTt[:, d], ps[6][:, :].rearrange("p (h t) -> p h t", h=HEADS), QSCALE,
                                           qTt[:, d], ALU.mult, ALU.mult).then_inc(a_rdy, 1)
                    dve.wait_ge(a_exp, 6 * gi + 3 * d + 2)
                    dve.wait_ge(a_ps, 6 * gi + 6)
                    v.tensor_tensor(kTt[:, d], ps[7][:, :].rearrange("p (h t) -> p h t", h=HEADS), kTt[:, d],
                                    ALU.mult).then_inc(a_rdy, 1)
                    dve.wait_ge(a_exp, 6 * gi + 3 * d + 3)
                    v.tensor_tensor(kdec[:, d, :], qk[:, g, 512:1024], kdec[:, d, :], ALU.mult).then_inc(a_rdy, 2)
                for d in range(2):
                    dve.wait_ge(at_ps, 2 * gi + d + 1)
                    v.copy_predicated(attnT[:, d], incl[d].bitcast(U32).unsqueeze(1).broadcast_to([P, HEADS, P]),
                                      ps[2 + d][:, :].rearrange("p (h t) -> p h t", h=HEADS)).then_inc(at_ev, 1)
                if g == 1:
                    dve.wait_ge(s_s0, 16)
                    dve.wait_ge(cT_ps, 4)
                    for i in range(8):
                        d, h = divmod(i, HEADS)
                        dve.wait_ge(kv_ps, i // 2 + 1)
                        v.scalar_tensor_tensor(smid[:, d, h, :], s0[:, d, h, :], decay[:, d, d, h:h + 1],
                                               ps[4 + i // 2][:, (i % 2) * DV:(i % 2 + 1) * DV],
                                               ALU.mult, ALU.add).then_inc(kv_ev, 1)
                else:
                    dve.wait_ge(kv_ev, 12)
                    for i in range(8):
                        d, h = divmod(i, HEADS)
                        dve.wait_ge(kv2_ps, i // 2 + 1)
                        v.scalar_tensor_tensor(s0[:, d, h, :], smid[:, d, h, :], decay[:, d, 1 - d, h:h + 1],
                                               ps[4 + i // 2][:, (i % 2) * DV:(i % 2 + 1) * DV],
                                               ALU.mult, ALU.add).then_inc(fin_rdy, 1)
                dve.wait_ge(o_sq, gi + 1)
                link(v.reciprocal(small[:, 20 + 4 * g:24 + 4 * g], small[:, 16 + 4 * g:20 + 4 * g]))
                for h in range(HEADS):
                    v.scalar_tensor_tensor(vv[:, g, h * DV:(h + 1) * DV], ps[2 + h // 2][:, (h % 2) * DV:(h % 2 + 1) * DV],
                                           small[:, 20 + 4 * g + h:21 + 4 * g + h], rs[:, g, h * DV:(h + 1) * DV],
                                           ALU.mult, ALU.mult).then_inc(o_rdy, 1)

            def segment_in(s, bank, units):
                dve.wait_ge(used, units)
                v.tensor_tensor(modrow[:, s - 2, :], ps[bank][:, :], modrow[:, s - 2, :], ALU.add).then_inc(seg_dve, 1)

            dve.wait_ge(ev[4], 4)
            gla(0, 1)
            dve.wait_ge(s_bmod, 32)
            segment_in(4, 0, pass_end(4) + 1 + SEG_UNITS)
            gla(1, 0)
            for i in range(4):
                g, b = divmod(i, 2)
                dve.wait_ge(yT_ps, i + 1)
                v.tensor_tensor(hT[:, 4 * b:4 * b + 4, g * P:(g + 1) * P],
                                ps[2 + i][:, :].rearrange("p (k t) -> p k t", k=4),
                                gcol[:, 0, 4 * b:4 * b + 4].unsqueeze(2).broadcast_to([P, 4, P]), ALU.mult).then_inc(yT_ev, 1)
            dve.wait_ge(s_ln, 64)
            dve.wait_ge(seg_dve, 1)
            dve.wait_ge(seg_add, 2)
            link(v.scalar_tensor_tensor(lnrow[:, 1, :], modrow[:, 2, :], 1.0, lnrow[:, 1, :], ALU.add, ALU.mult))
            link(v.scalar_tensor_tensor(modrow[:, 2, :], modrow[:, 2, :], 1.0, lnrow[:, 0, :], ALU.add, ALU.mult))
            v.tensor_tensor(modrow[:, 1, :], modrow[:, 1, :], lnrow[:, 1, :], ALU.add).then_inc(row2, 1)

            dve.wait_ge(g1_in, 128)
            for p in range(2):
                dve.wait_ge(used, PRE_UNITS - SEG_UNITS + (p - 1) * PASS_UNITS)
                for g in range(G):
                    for hf in range(2):
                        q = 2 * p + hf
                        cs = slice(q * BANK, (q + 1) * BANK)
                        ins = v.tensor_tensor(g1b[:, g, cs], ps[4 * p + 2 * g + hf][:, :], g1b[:, g, cs], ALU.mult)
                        ins.then_inc(m_ev, 1)
                        dve.wait_ge(m_ev, 4 * p + 2 * g + hf + 1)
                        link(v.scalar_tensor_tensor(xres[:, g, cs], xres[:, g, cs], ALPHA, g1b[:, g, cs], ALU.mult, ALU.add))
                        v.bn_stats(stats[:, g, q, :], xres[:, g, cs]).then_inc(dch, 1)
                        n += 1
            dve.wait_ge(dch, n)
            for g in range(G):
                v.bn_aggr(small[:, 36 + 2 * g:38 + 2 * g], stats[:, g, :, :]).then_inc(ln_v, 1)
            for g in range(G):
                dve.wait_ge(ln_s, g + 1)
                link(v.reciprocal(small[:, 42 + g:43 + g], small[:, 40 + g:41 + g]))
                if g == 0:
                    dve.wait_ge(mod2_in, 256)
                link(v.scalar_tensor_tensor(h2[:, g, :], xres[:, g, :], small[:, 36 + 2 * g:37 + 2 * g],
                                            G2b[:, g, :], ALU.subtract, ALU.mult))
                v.scalar_tensor_tensor(h2[:, g, :], h2[:, g, :], small[:, 42 + g:43 + g], B2b[:, g, :],
                                       ALU.mult, ALU.add).then_inc(h2_rdy, 1)
                for b in range(2):
                    dve.wait_ge(h2T_ps, 4 * g + 2 * b + 1)
                    v.tensor_copy(hT[:, 8 * b:8 * b + 4, g * P:(g + 1) * P],
                                  ps[H2T_BANKS[2 * b]][:, :].rearrange("p (k t) -> p k t", k=4)).then_inc(h2T_v, 1)
            for g in range(G):
                v.tensor_scalar(xres[:, g, :], xres[:, g, :], small[:, 36 + 2 * g:37 + 2 * g],
                                small[:, 42 + g:43 + g], ALU.subtract, ALU.mult).then_inc(xn_rdy, 1)

            link(v.memset(steps[:, 2, 0:1], 0))
            link(v.memset(steps[:, 3, 0:NE], 1))
            link(v.tensor_copy(steps[:, 0, :], const[:, C_EXP:C_EXP + NSTEP + 1]))

            f = lambda i: rt[:, i, 0:32]
            f3 = lambda i: rt[:, i, 0:32].rearrange("p (a b) -> p a b", b=PER)
            f8 = lambda i: rt[:, 13, 8 * i:8 * i + 8]
            b4 = lambda a: a.unsqueeze(2).broadcast_to([P, a.shape[1], PER])
            bN = lambda a: a.unsqueeze(2).broadcast_to([P, G, NE])
            g16 = lambda i: rt[:, i, 0:32].rearrange("p (g e) -> p g e", g=G)
            dve.wait_ge(s_wr, 32)
            dve.wait_ge(lg_ps, 2)
            link(v.tensor_tensor(g16(0), ps[4][:, 0:32].rearrange("p (g e) -> p g e", g=G),
                                 br[:, :].unsqueeze(1).broadcast_to([P, G, NE]), ALU.add))
            link(v.tensor_reduce(small[:, 24:26], g16(0), AX.X, ALU.max))
            v.tensor_scalar(small[:, 44:46], small[:, 24:26], -1.0, None, ALU.mult).then_inc(lmax, 1)
            dve.wait_ge(lexp, 2)
            link(v.reciprocal(small[:, 54:56], small[:, 48:50]))
            link(v.tensor_tensor(g16(2), g16(1), bN(small[:, 54:56]), ALU.mult))

            def best(src, mx, key, hot):
                link(v.tensor_reduce(mx, src, AX.X, ALU.max))
                link(v.tensor_tensor(key, src, b4(mx), ALU.is_equal))
                link(v.tensor_tensor(key, key, key4[:, 0:4 * mx.shape[1]].rearrange("p (a b) -> p a b", b=PER), ALU.mult))
                link(v.tensor_reduce(f8(3)[:, 0:mx.shape[1]], key, AX.X, ALU.max))
                link(v.tensor_tensor(hot, key, b4(f8(3)[:, 0:mx.shape[1]]), ALU.is_equal))

            best(f3(2), f8(0), f3(3), f3(4))
            link(v.scalar_tensor_tensor(f(5), f(4), -4.0, f(2), ALU.mult, ALU.add))
            best(f3(5), f8(1), f3(3), f3(6))
            link(v.tensor_tensor(f8(0), f8(0), f8(1), ALU.add))
            grp = rt[:, 7, 0:8]
            best(f8(0).rearrange("p (a b) -> p a b", b=NGRP), small[:, 24:26],
                 rt[:, 3, 0:8].rearrange("p (a b) -> p a b", b=NGRP), grp.rearrange("p (a b) -> p a b", b=NGRP))
            link(v.tensor_tensor(f(4), f(4), f(6), ALU.add))
            v.tensor_tensor(f3(8), f3(4), b4(grp), ALU.mult).then_inc(sel_rdy, 1)
            dve.wait_ge(sel_rdy, 1)
            link(v.tensor_tensor(f(5), f(8), f(2), ALU.mult))
            link(v.tensor_reduce(small[:, 24:26], g16(5), AX.X, ALU.add))
            link(v.reciprocal(small[:, 26:28], small[:, 24:26]))
            link(v.tensor_tensor(g16(5), g16(5), bN(small[:, 26:28]), ALU.mult))
            segment_in(5, 3, PRE_UNITS)
            dve.wait_ge(rk_ps, 1)
            link(v.scalar_tensor_tensor(f(7), ps[5][:, 0:32], 1.0, f(8), ALU.add, ALU.mult))
            link(v.tensor_scalar(f(7), f(7), -1.0, None, ALU.add))
            ex = lambda i: extra[:, i, :].rearrange("p (j e) -> p j e", j=MAX_EXTRA)
            exs = lambda i: extra[:, i, 0:MAX_EXTRA]
            jn = lambda a: a.unsqueeze(1).broadcast_to([P, MAX_EXTRA, NE])
            jrow = const[:, C_J:C_J + NE * MAX_EXTRA].rearrange("p (j e) -> p j e", j=MAX_EXTRA)
            cnt, ov = rt[:, 9, 0:NE], rt[:, 9, NE:2 * NE]
            link(v.tensor_copy(cnt, ps[5][:, 32:48]))

            def block_count(dst, src, base):
                link(v.tensor_scalar(dst, src, base + BLK + 0.5, 1.0, ALU.is_gt, ALU.add))
                for k in range(2, NBLK):
                    link(v.scalar_tensor_tensor(dst, src, base + k * BLK + 0.5, dst, ALU.is_gt, ALU.add))

            def prefix(a, b, width):
                sh = 1
                while sh < width:
                    link(v.tensor_copy(rt[:, b, 0:sh], rt[:, a, 0:sh]))
                    link(v.tensor_tensor(rt[:, b, sh:width], rt[:, a, sh:width], rt[:, a, 0:width - sh], ALU.add))
                    a, b, sh = b, a, 2 * sh
                return a

            by_step = lambda a: a.rearrange("p (g e) -> p e g", g=NGRP)
            block_count(rt[:, 10, 0:NE].rearrange("p (e g) -> p e g", g=NGRP), by_step(cnt), 0.0)
            link(v.tensor_copy(steps[:, 1, 0:NE], rt[:, 10, 0:NE]))
            v.tensor_copy(steps[:, 2, 1:NE + 1], rt[:, prefix(10, 11, NE), 0:NE]).then_inc(tab_rdy, 1)

            def extra_steps():
                link(v.tensor_scalar(ov, cnt, CAP + 0.5, None, ALU.is_gt))
                link(v.tensor_copy(rt[:, 11, 0:NE], ov))
                cum = rt[:, prefix(11, 12, NE), 0:NE]
                link(v.tensor_tensor(ex(0), jn(cum), jrow, ALU.is_le))
                link(v.tensor_reduce(exs(1), ex(0), AX.X, ALU.add))
                link(v.tensor_tensor(ex(2), jn(iota[:, 0:NE]), exs(1).unsqueeze(2).broadcast_to([P, MAX_EXTRA, NE]),
                                     ALU.is_equal))
                link(v.tensor_tensor(ex(2), ex(2), jn(cnt), ALU.mult))
                link(v.tensor_reduce(exs(3), ex(2), AX.X, ALU.add))
                link(v.memset(rt[:, 10, :], 0.0))
                link(v.tensor_copy(rt[:, 10, 0:NE], steps[:, 1, 0:NE]))
                block_count(rt[:, 10, NE:NSTEP], exs(3), float(CAP))
                link(v.tensor_copy(steps[:, 1, NE:NSTEP], rt[:, 10, NE:NSTEP]))
                link(v.tensor_copy(exs(7), rt[:, 10, NE:NSTEP]))
                blocks_to = rt[:, prefix(10, 11, NSTEP), 0:NSTEP]
                link(v.tensor_copy(steps[:, 2, NE + 1:NSTEP + 1], blocks_to[:, NE:NSTEP]))
                link(v.tensor_scalar(steps[:, 0, NE:NSTEP], exs(1), NE - 1.0, None, ALU.min))
                link(v.tensor_scalar(steps[:, 3, NE:NSTEP], exs(1), NE - 0.5, None, ALU.is_lt))
                link(v.tensor_scalar(exs(5), exs(1), NE - 0.5, None, ALU.is_lt))
                link(v.tensor_reduce(extra[:, 6, 0:1], exs(5), AX.X, ALU.add))
                link(v.tensor_scalar(steps[:, 4, 0:1], extra[:, 6, 0:1], float(NE), None, ALU.add))
                link(v.tensor_tensor(exs(5), exs(5), exs(7), ALU.mult))
                link(v.tensor_reduce(extra[:, 6, 1:2], exs(5), AX.X, ALU.add))
                v.tensor_tensor(steps[:, 4, 1:2], extra[:, 6, 1:2], blocks_to[:, NE - 1:NE], ALU.add).then_inc(tab_rdy, 1)
                dve.wait_ge(tab_rdy, 2)

            def select(t, e):
                for g in range(G):
                    v.tensor_scalar(sel[:, g, :], iota, const[:, bass.ds(t + C_OFF, 1)],
                                    rt[:, 7, bass.ds(e + g * NE, 1)], ALU.add, ALU.is_equal).then_inc(st_onehot, 1)
                dve.wait_ge(st_onehot, t * 2 + 2)
                for g in range(G):
                    last = v.tensor_scalar(wsel[:, g, :], sel[:, g, :], rt[:, 5, bass.ds(e + g * NE, 1)], None, ALU.mult)
                last.then_inc(st_sel, 1)

            def expert(t, b0):
                for i in range(4):
                    dve.wait_ge(st_gath, t * 4 + (i + 1))
                    v.tensor_copy(XT[:, 4 * i:4 * i + 4, :],
                                  ps[i][:, :].rearrange("p (k s) -> p k s", k=4)).then_inc(st_xv, 1)
                dve.wait_ge(st_wTp, t + 1)
                dve.wait_ge(st_wT, t + 1)
                v.tensor_copy(wselN, ps[4][:, 0:256].rearrange("p (g t) -> p g t", g=G)).then_inc(st_wN, 1)
                nxt = dve.value_load(steps[0:1, 0, bass.ds(t + 1, 1)], min_val=0, max_val=NE - 1)
                select(t + 1, nxt)

            def blocks(t, b0, nb):
                for b in range(nb):
                    dve.wait_ge(bk_hs, b0 + (b + 1))
                    if b >= 2:
                        dve.wait_ge(bk_hTp, b0 + (b - 1))
                    v.tensor_tensor(hh[:, b % 2, :], hs[:, b % 2, :], ps[b][:, 256:512], ALU.mult).then_inc(bk_h, 1)
                    if b >= 1:
                        hT_out(b0, b - 1)
                hT_out(b0, nb - 1)
                add(t)

            def full(t, b0):
                for hf in range(2):
                    dve.wait_ge(bk_hs, b0 + (2 * hf + 2))
                    if hf:
                        dve.wait_ge(bk_hTp, b0 + 2)
                    v.tensor_tensor(hh1, hs1, ps[2 + hf][:, :], ALU.mult).then_inc(bk_h, 2)
                    dve.wait_ge(bk_hTp, b0 + (2 * hf + 2))
                    v.tensor_copy(hTf[:, 4 * hf:4 * hf + 4, :],
                                  ps[4 + hf][:, :].rearrange("p (j t) -> p j t", j=4)).then_inc(bk_hT, 2)
                add(t)
                dve.wait_ge(used, t * STEP_UNITS + (PRE_UNITS + 24))
                for q in range(2, 4):
                    v.tensor_copy(yf[:, q * BANK:(q + 1) * BANK], ps[4 + q][:, :]).then_inc(bk_yf, 128)

            def add(t):
                for j in range(8):
                    g, q = divmod(j, 4)
                    cs = slice(q * BANK, (q + 1) * BANK)
                    dve.wait_ge(st_cmb, t * 8 + (j + 1))
                    v.tensor_tensor(acc[:, g, cs], ps[q][:, :], acc[:, g, cs], ALU.add).then_inc(st_add, 1)

            def hT_out(b0, b):
                dve.wait_ge(bk_hTp, b0 + (b + 1))
                v.tensor_copy(hTm[:, b], ps[4 + b][:, 0:256].rearrange("p (j t) -> p j t", j=2)).then_inc(bk_hT, 1)

            select(0, 0)
            extra_steps()
            for_steps(dve, expert, blocks, full)

            v.memset(small[:, 62:63], 0.0).then_inc(added, 1)
            for q in range(NQ):
                cs = slice(q * BANK, (q + 1) * BANK)
                dve.wait_ge(g2_ev, q + 1)
                link(v.tensor_tensor(acc[:, 0, cs], acc[:, 0, cs], g2b[:, 0, cs], ALU.mult))
                dve.wait_ge(pch, 2 * G)
                link(v.tensor_tensor(acc[:, 0, cs], acc[:, 0, cs], xres[:, 0, cs], ALU.add))
            tl = dve.value_load(steps[0:1, 4, 0:1], min_val=NE, max_val=NSTEP)
            for g in range(G):
                for q in range(NQ):
                    j = NQ * g + q
                    cs = slice(q * BANK, (q + 1) * BANK)
                    if g:
                        dve.wait_ge(t_base, q + 1)
                    dve.wait_ge(st_cmb, tl * 8 + (j + 1))
                    v.tensor_tensor(g2b[:, g, cs], ps[q][:, :], g2b[:, g, cs], ALU.mult).then_inc(t_mul, 1)
                    dve.wait_ge(t_mul, j + 1)
                    link(v.tensor_tensor(acc[:, g, cs], g2b[:, g, cs], acc[:, g, cs], ALU.add))
                    link(v.bn_stats(stats[:, g, q, :], acc[:, g, cs]))
                v.bn_aggr(small[:, 36 + 2 * g:38 + 2 * g], stats[:, g, :, :]).then_inc(t_var, 1)
                if g == 0:
                    dve.wait_ge(t_sd, 1)
                    link(v.reciprocal(small[:, 42:43], small[:, 40:41]))
                    v.tensor_scalar(acc[:, 0, :], acc[:, 0, :], small[:, 36:37], small[:, 42:43],
                                    ALU.subtract, ALU.mult).then_inc(t_nrm, 1)
            dve.wait_ge(s_ln2, 32)
            dve.wait_ge(t_sd, 2)
            link(v.reciprocal(small[:, 43:44], small[:, 41:42]))
            for i in range(2):
                cs = slice(i * D // 2, (i + 1) * D // 2)
                link(v.scalar_tensor_tensor(acc[:, 1, cs], acc[:, 1, cs], small[:, 38:39], lng[:, cs], ALU.subtract, ALU.mult))
                v.scalar_tensor_tensor(acc[:, 1, cs], acc[:, 1, cs], small[:, 43:44], lnb[:, cs],
                                       ALU.mult, ALU.add).then_inc(t_out[1], 1)


_INS = ['x_prompt', 'x_sample', 'state_gla', 'c', 'c_ctx', 'w_mod', 'b_mod', 'w_in', 'w_gate_up', 'b_gate',
        'gla_norm_g', 'w_dw', 'b_dw', 'conv_ln_g', 'conv_ln_b', 'w_out', 'ln1_g', 'ln1_b', 'ln2_g', 'ln2_b',
        'w_router', 'b_router', 'w_e_gate', 'w_e_up', 'w_e_down']
_OUTS = [((1, 128, 2048), 'float32'), ((1, 128, 2048), 'float32'), ((1, 1, 2, 4, 128, 256), 'float32')]


def _constants():
    import numpy as np
    t = np.zeros((P, C_END), np.float32)
    s, m = np.arange(P)[:, None], np.arange(P)[None, :]
    same = s // HALF == m // HALF
    t[:, C_ID:C_ID + P] = s == m
    t[:, C_INCF:C_INCF + P] = np.where(same & (s <= m), -1 / TAU, 0.0)
    t[:, C_RESTF:C_RESTF + P] = np.where(same & (s > m), -1 / TAU, 0.0)
    t[:, C_INCB:C_INCB + P] = np.where(same & (s >= m), -1 / TAU, 0.0)
    t[:, C_RESTB:C_RESTB + P] = np.where(same & (s < m), -1 / TAU, 0.0)
    t[:, C_BEFORE:C_BEFORE + P] = s < m
    t[:, C_ONES:C_ONES + P] = 1.0
    t[:, C_IOTA:C_IOTA + P] = m
    for q in range(NQ):
        for g in range(G):
            t[32 * q + g, C_SEL + (2 * q + g) * P:C_SEL + (2 * q + g + 1) * P] = 1.0
            t[32 * q + g, C_SUM + g] = 1.0
    t[:, C_KEY:C_KEY + 32] = np.tile([4, 3, 2, 1], 8)
    t[:, C_J:C_J + NE * MAX_EXTRA] = np.repeat(np.arange(MAX_EXTRA), NE)
    t[:, C_EXP:C_OFF] = NE - 1
    t[:, C_EXP:C_EXP + NE] = np.arange(NE).reshape(NGRP, PER).T.reshape(-1)
    t[:, C_OFF:C_END] = CAP * (np.arange(NSTEP + 1) >= NE)
    nf = D // 4
    omega = np.float32(1.0) / np.power(np.float32(10000.0), np.arange(nf, dtype=np.float32) / np.float32(nf))
    tok = np.arange(P)
    pr = (tok // 64).astype(np.float32)[:, None] * omega
    pc = (tok % 64).astype(np.float32)[:, None] * omega
    pos = np.concatenate([np.sin(pr), np.cos(pr), np.sin(pc), np.cos(pc)], axis=-1).astype(np.float32)
    return t, pos


def kernel(**inputs):
    import numpy as _np
    import concourse.bacc as _bacc
    from concourse import mybir as _mybir
    from concourse.bass_utils import run_bass_kernel_spmd as _run

    nc = _bacc.Bacc("TRN2", target_bir_lowering=False, num_devices=1)
    arrays, args = {}, []
    table, pos = _constants()
    for name, a in [(n, inputs[n]) for n in _INS] + [("table", table), ("pos", pos)]:
        a = _np.ascontiguousarray(a)
        arrays[f"in_{name}_dram"] = a
        args.append(nc.dram_tensor(f"in_{name}_dram", a.shape, _mybir.dt.from_np(a.dtype), kind="ExternalInput").ap())
    for i, (shape, dtype) in enumerate(_OUTS):
        dt = _mybir.dt.from_np(_np.dtype(dtype))
        args.append(nc.dram_tensor(f"out_{i}_dram", shape, dt, kind="ExternalOutput").ap())
    hybrid_step(nc, *args)
    r = _run(nc, [arrays], core_ids=[0])
    return tuple(r.results[0][f"out_{i}_dram"] for i in range(len(_OUTS)))
```
